# Optimizing a Trainium2 kernel written in Bass

```python
import jax, jax.numpy as jnp
from jax import lax
import numpy as np

D_MODEL = 1024
BATCH = 1
SEQ = 256
DEPTH = 2

GRID_W = 64
CTX_LEN = 256
N_BRANCH = 3
GLA_HEADS = 4
GLA_DK = 64
GLA_DV = 128
GLA_GATE_RANK = 16
GLA_GATE_NORM = 16.0
GLA_CHUNK = 64
MLA_HEADS = 8
MLA_Q_LORA = 256
MLA_KV_LORA = 128
MLA_NOPE = 64
MLA_ROPE = 32
MLA_DV = 64
ROPE_THETA = 10000.0
ROPE_FREQS = MLA_ROPE // 4
Q_BLOCK = 128
SC_W = 512
D_FF = 2816
NORM_EPS = 1e-6
IN_SIZES = (GLA_HEADS * GLA_DK, GLA_HEADS * GLA_DK, GLA_HEADS * GLA_DV, GLA_HEADS * GLA_DV,
            2 * GLA_GATE_RANK, MLA_Q_LORA, MLA_KV_LORA, MLA_ROPE, SC_W, SC_W, SC_W,
            N_BRANCH * D_MODEL)
IN_W = sum(IN_SIZES)

kernel_name = 'hybrid_gla_mla_shortconv_dit'

def rms_norm(x, g):
    xf = x.astype(jnp.float32)
    y = xf * lax.rsqrt(jnp.mean(xf * xf, axis=-1, keepdims=True) + NORM_EPS)
    return (y * g).astype(x.dtype)

def modulate(h, shift, scale):
    return h * (1.0 + scale) + shift

def flip(t):
    return jnp.flip(t, axis=1)

def split_proj(p):
    idx = np.cumsum(IN_SIZES)[:-1].tolist()
    return jnp.split(p, idx, axis=-1)

def dwconv3(u, w):
    L = u.shape[1]
    up = jnp.pad(u, ((0, 0), (1, 1), (0, 0)))
    return up[:, 0:L] * w[0] + up[:, 1:L + 1] * w[1] + up[:, 2:L + 2] * w[2]

def axial_rope(rows):
    row = jnp.repeat(jnp.arange(rows, dtype=jnp.float32), GRID_W)
    col = jnp.tile(jnp.arange(GRID_W, dtype=jnp.float32), rows)
    inv = ROPE_THETA ** (-jnp.arange(ROPE_FREQS, dtype=jnp.float32) / ROPE_FREQS)
    ang = jnp.stack([row[:, None] * inv, col[:, None] * inv], axis=1)
    return jnp.cos(ang), jnp.sin(ang)

def apply_rope(x, cos, sin):
    xr = x.reshape(x.shape[:-1] + (2, 2, ROPE_FREQS)).astype(jnp.float32)
    x0, x1 = xr[..., 0, :], xr[..., 1, :]
    out = jnp.stack([x0 * cos - x1 * sin, x1 * cos + x0 * sin], axis=-2)
    return out.reshape(x.shape).astype(x.dtype)

def gla_heads(t, dh):
    return t.reshape(t.shape[0], t.shape[1], GLA_HEADS, dh)

def gla_log_decay(lr, w2, b2):
    z = (lr @ w2 + b2).astype(jnp.float32)
    return gla_heads(jax.nn.log_sigmoid(z) / GLA_GATE_NORM, GLA_DK)

def gla_chunked(q, k, v, log_a, s0):
    B, L, H, DK = q.shape
    DV = v.shape[-1]
    nc = L // GLA_CHUNK
    to_chunks = lambda t: t.reshape(B, nc, GLA_CHUNK, H, t.shape[-1])
    qc, kc, vc = to_chunks(q), to_chunks(k), to_chunks(v)
    b = jnp.cumsum(to_chunks(log_a).astype(jnp.float32), axis=2)
    b_last = b[:, :, -1:]
    q_in = qc * jnp.exp(b)
    k_in = kc * jnp.exp(-b)
    k_st = kc * jnp.exp(b_last - b)
    lower = jnp.tril(jnp.ones((GLA_CHUNK, GLA_CHUNK), dtype=bool))
    a_intra = jnp.where(lower, jnp.einsum('bnihd,bnjhd->bnhij', q_in, k_in), 0.0)
    o_intra = jnp.einsum('bnhij,bnjhv->bnihv', a_intra, vc)
    u = jnp.einsum('bnjhd,bnjhv->bnhdv', k_st, vc)
    decay = jnp.exp(b_last[:, :, 0])

    def step(s, xs):
        q_n, d_n, u_n = xs
        o_n = jnp.einsum('bihd,bhdv->bihv', q_n, s)
        return d_n[..., None] * s + u_n, o_n

    s_fin, o_inter = lax.scan(step, s0.astype(jnp.float32),
                              (q_in.swapaxes(0, 1), decay.swapaxes(0, 1), u.swapaxes(0, 1)))
    o = o_intra + o_inter.swapaxes(0, 1)
    return o.reshape(B, L, H, DV).astype(v.dtype), s_fin

def gla_final_state(k, v, log_a):
    b = jnp.cumsum(log_a.astype(jnp.float32), axis=1)
    return jnp.einsum('blhd,blhv->bhdv', k * jnp.exp(b[:, -1:] - b), v)

def gla_branch(q_a, k_a, v_a, r_a, alr, lp, s_f0, s_b0):
    B, L = q_a.shape[:2]
    q = gla_heads(q_a, GLA_DK) * GLA_DK ** -0.5
    k = gla_heads(k_a, GLA_DK)
    v = gla_heads(v_a, GLA_DV)
    lr_f, lr_b = jnp.split(alr, 2, axis=-1)
    la_f = gla_log_decay(lr_f, lp['w_gk2'][0], lp['b_gk2'][0])
    la_b = gla_log_decay(lr_b, lp['w_gk2'][1], lp['b_gk2'][1])
    o_f, _ = gla_chunked(q, k, v, la_f, s_f0)
    o_b, _ = gla_chunked(flip(q), flip(k), flip(v), flip(la_b), s_b0)
    o = rms_norm(o_f + flip(o_b), lp['gla_norm_g'].reshape(GLA_HEADS, GLA_DV))
    return (o.reshape(B, L, GLA_HEADS * GLA_DV) * jax.nn.silu(r_a)) @ lp['w_br_a']

def mla_q(cq, lp, rope):
    B, L = cq.shape[:2]
    q = (rms_norm(cq, lp['mla_q_norm_g']) @ lp['w_uq']).reshape(B, L, MLA_HEADS, MLA_NOPE + MLA_ROPE)
    if rope is not None:
        q_rope = apply_rope(q[..., MLA_NOPE:], rope[0][:, None], rope[1][:, None])
        q = jnp.concatenate([q[..., :MLA_NOPE], q_rope], axis=-1)
    return q * (MLA_NOPE + MLA_ROPE) ** -0.5

def mla_kv(ckv, kr, lp, rope):
    B, L = ckv.shape[:2]
    kv = (rms_norm(ckv, lp['mla_kv_norm_g']) @ lp['w_ukv']).reshape(B, L, MLA_HEADS, MLA_NOPE + MLA_DV)
    k_nope, v = kv[..., :MLA_NOPE], kv[..., MLA_NOPE:]
    if rope is not None:
        kr = apply_rope(kr, rope[0], rope[1])
    k_rope = jnp.broadcast_to(kr[:, :, None, :], (B, L, MLA_HEADS, MLA_ROPE))
    return jnp.concatenate([k_nope, k_rope], axis=-1), v

def softmax_attend(q, k, v):
    s = jnp.einsum('bqhd,bkhd->bhqk', q, k).astype(jnp.float32)
    p = jax.nn.softmax(s, axis=-1).astype(v.dtype)
    return jnp.einsum('bhqk,bkhv->bqhv', p, v)

def blocked_attend(q, k, v):
    B, L, H, Dq = q.shape
    qb = q.reshape(B, L // Q_BLOCK, Q_BLOCK, H, Dq).swapaxes(0, 1)
    o = lax.map(lambda qq: softmax_attend(qq, k, v), qb)
    return o.swapaxes(0, 1).reshape(B, L, H, v.shape[-1])

def short_conv_branch(sb, sc, sx, lp):
    return (sb * dwconv3(sc * sx, lp['sc_w'])) @ lp['w_br_c']

def merge_branches(y_a, y_b, y_c, gates, lp):
    g_a, g_b, g_c = jnp.split(jax.nn.sigmoid(gates), N_BRANCH, axis=-1)
    return (g_a * y_a + g_b * y_b + g_c * y_c) @ lp['w_o']

def context_memory(proj_c, lp):
    _, k_a, v_a, _, alr, _, ckv, kr, _, _, _, _ = split_proj(proj_c)
    k = gla_heads(k_a, GLA_DK)
    v = gla_heads(v_a, GLA_DV)
    lr_f, lr_b = jnp.split(alr, 2, axis=-1)
    s_f = gla_final_state(k, v, gla_log_decay(lr_f, lp['w_gk2'][0], lp['b_gk2'][0]))
    s_b = gla_final_state(flip(k), flip(v), flip(gla_log_decay(lr_b, lp['w_gk2'][1], lp['b_gk2'][1])))
    k_m, v_m = mla_kv(ckv, kr, lp, None)
    return (k_m, v_m, s_f, s_b)

def latent_mixers(proj, lp, rope, mem):
    k_ctx, v_ctx, s_f, s_b = mem
    q_a, k_a, v_a, r_a, alr, cq, ckv, kr, sb, sc, sx, gates = split_proj(proj)
    y_a = gla_branch(q_a, k_a, v_a, r_a, alr, lp, s_f, s_b)
    q = mla_q(cq, lp, rope)
    k, v = mla_kv(ckv, kr, lp, rope)
    o = blocked_attend(q, jnp.concatenate([k, k_ctx], axis=1), jnp.concatenate([v, v_ctx], axis=1))
    y_b = o.reshape(o.shape[0], o.shape[1], MLA_HEADS * MLA_DV) @ lp['w_br_b']
    y_c = short_conv_branch(sb, sc, sx, lp)
    return merge_branches(y_a, y_b, y_c, gates, lp)

def context_mixers(proj_c, lp, mem):
    k_ctx, v_ctx, _, _ = mem
    q_a, k_a, v_a, r_a, alr, cq, _, _, sb, sc, sx, gates = split_proj(proj_c)
    zero = jnp.zeros((proj_c.shape[0], GLA_HEADS, GLA_DK, GLA_DV), jnp.float32)
    y_a = gla_branch(q_a, k_a, v_a, r_a, alr, lp, zero, zero)
    o = softmax_attend(mla_q(cq, lp, None), k_ctx, v_ctx)
    y_b = o.reshape(o.shape[0], o.shape[1], MLA_HEADS * MLA_DV) @ lp['w_br_b']
    y_c = short_conv_branch(sb, sc, sx, lp)
    return merge_branches(y_a, y_b, y_c, gates, lp)

def conv_ffn(h, lp):
    g = dwconv3(h @ lp['w_ffn_gate'], lp['ffn_conv_w']) + lp['ffn_conv_b']
    return (jax.nn.silu(g) * (h @ lp['w_ffn_up'])) @ lp['w_ffn_down']

def setup_inputs(seed: int = 0) -> dict:
    key = jax.random.key(seed)
    ks = iter(jax.random.split(key, 32))

    def nrm(shape, scale):
        return jax.random.normal(next(ks), shape, jnp.float32) * scale

    def gain(shape):
        return 1.0 + nrm(shape, 0.05)

    L = DEPTH
    D = D_MODEL
    return {
        'x': nrm((BATCH, SEQ, D), 1.0),
        'c': nrm((BATCH, D), 1.0),
        'ctx': nrm((BATCH, CTX_LEN, D), 1.0),
        'c_ctx': nrm((D,), 1.0),
        'w_ada': nrm((L, D, 6 * D), 0.5 * D ** -0.5),
        'b_ada': nrm((L, 6 * D), 0.02),
        'norm1_g': gain((L, D)),
        'w_in': nrm((L, D, IN_W), D ** -0.5),
        'w_gk2': nrm((L, 2, GLA_GATE_RANK, GLA_HEADS * GLA_DK), GLA_GATE_RANK ** -0.5),
        'b_gk2': nrm((L, 2, GLA_HEADS * GLA_DK), 0.1),
        'gla_norm_g': gain((L, GLA_HEADS * GLA_DV)),
        'mla_q_norm_g': gain((L, MLA_Q_LORA)),
        'w_uq': nrm((L, MLA_Q_LORA, MLA_HEADS * (MLA_NOPE + MLA_ROPE)), MLA_Q_LORA ** -0.5),
        'mla_kv_norm_g': gain((L, MLA_KV_LORA)),
        'w_ukv': nrm((L, MLA_KV_LORA, MLA_HEADS * (MLA_NOPE + MLA_DV)), MLA_KV_LORA ** -0.5),
        'sc_w': nrm((L, 3, SC_W), 3 ** -0.5),
        'w_br_a': nrm((L, GLA_HEADS * GLA_DV, D), (GLA_HEADS * GLA_DV) ** -0.5),
        'w_br_b': nrm((L, MLA_HEADS * MLA_DV, D), (MLA_HEADS * MLA_DV) ** -0.5),
        'w_br_c': nrm((L, SC_W, D), SC_W ** -0.5),
        'w_o': nrm((L, D, D), D ** -0.5),
        'norm2_g': gain((L, D)),
        'w_ffn_gate': nrm((L, D, D_FF), D ** -0.5),
        'w_ffn_up': nrm((L, D, D_FF), D ** -0.5),
        'ffn_conv_w': nrm((L, 3, D_FF), 3 ** -0.5),
        'ffn_conv_b': nrm((L, D_FF), 0.02),
        'w_ffn_down': nrm((L, D_FF, D), D_FF ** -0.5),
        'final_norm_g': gain((D,)),
    }

def reference(x, c, ctx, c_ctx, w_ada, b_ada, norm1_g, w_in, w_gk2, b_gk2, gla_norm_g,
              mla_q_norm_g, w_uq, mla_kv_norm_g, w_ukv, sc_w, w_br_a, w_br_b, w_br_c, w_o,
              norm2_g, w_ffn_gate, w_ffn_up, ffn_conv_w, ffn_conv_b, w_ffn_down, final_norm_g):
    rows = x.shape[1] // GRID_W
    rope = axial_rope(rows)
    xc = ctx
    for l in range(DEPTH):
        last = l == DEPTH - 1
        lp = {
            'w_gk2': w_gk2[l], 'b_gk2': b_gk2[l], 'gla_norm_g': gla_norm_g[l],
            'mla_q_norm_g': mla_q_norm_g[l], 'w_uq': w_uq[l],
            'mla_kv_norm_g': mla_kv_norm_g[l], 'w_ukv': w_ukv[l], 'sc_w': sc_w[l],
            'w_br_a': w_br_a[l], 'w_br_b': w_br_b[l], 'w_br_c': w_br_c[l], 'w_o': w_o[l],
            'w_ffn_gate': w_ffn_gate[l], 'w_ffn_up': w_ffn_up[l], 'ffn_conv_w': ffn_conv_w[l],
            'ffn_conv_b': ffn_conv_b[l], 'w_ffn_down': w_ffn_down[l],
        }
        mod = jax.nn.silu(c) @ w_ada[l] + b_ada[l]
        mod_c = jax.nn.silu(c_ctx) @ w_ada[l] + b_ada[l]
        sh1, sc1, g1, sh2, sc2, g2 = jnp.split(mod[:, None, :], 6, axis=-1)
        sh1c, sc1c, g1c, sh2c, sc2c, g2c = jnp.split(mod_c, 6, axis=-1)
        proj_c = modulate(rms_norm(xc, norm1_g[l]), sh1c, sc1c) @ w_in[l]
        mem = context_memory(proj_c, lp)
        proj = modulate(rms_norm(x, norm1_g[l]), sh1, sc1) @ w_in[l]
        x = x + g1 * latent_mixers(proj, lp, rope, mem)
        if not last:
            xc = xc + g1c * context_mixers(proj_c, lp, mem)
        x = x + g2 * conv_ffn(modulate(rms_norm(x, norm2_g[l]), sh2, sc2), lp)
        if not last:
            xc = xc + g2c * conv_ffn(modulate(rms_norm(xc, norm2_g[l]), sh2c, sc2c), lp)
    return rms_norm(x, final_norm_g)


_drawn_inputs = setup_inputs


def setup_inputs(seed=0):
    import zlib

    import numpy as np

    out = dict(_drawn_inputs(seed))
    spreads = {}
    factors = {'b_gk2': 8.0,
     'gla_norm_g': 7.49,
     'mla_q_norm_g': 8.0,
     'mla_kv_norm_g': 8.0,
     'ffn_conv_b': 8.0}
    for name, (base, spread) in spreads.items():
        noise = np.random.default_rng([zlib.crc32(name.encode()), seed]).standard_normal(out[name].shape)
        drawn = base * np.exp(spread * noise) if base else spread * noise
        out[name] = __import__('jax').numpy.asarray(drawn.astype(out[name].dtype))
    for name, factor in factors.items():
        out[name] = (out[name] * factor).astype(out[name].dtype)
    return out
```

```python
from contextlib import ExitStack

import numpy as np

import concourse.bass as bass
from concourse import mybir

F32 = mybir.dt.float32
F32R = mybir.dt.float32r
ALU = mybir.AluOpType
ACT = mybir.ActivationFunctionType
AX_X = mybir.AxisListType.X

P = 128
D = 1024
KD = D // P
C = 256
T = 2 * C
L = 2
GRID_W = 64
EPS = 1e-6
GH, DK, DV, RANK, CHUNK = 4, 64, 128, 16, 64
NCH = T // CHUNK
GATE_NORM = 16.0
MH, NOPE, ROPE, MDV = 8, 64, 32, 64
QK = NOPE + ROPE
QLORA, KVLORA = 256, 128
SCW = 512
FF = 2816
KF = FF // P
FF_PARTS = [8, 8, 6]
SLOTS = 4
AHEAD = 2
ADA_SLOTS = 4
ADA_CHUNK = 512
O_Q, O_K, O_V, O_R, O_LR = 0, 256, 512, 1024, 1536
O_CQ = O_LR + 2 * RANK
O_CKV = O_CQ + QLORA
O_KR = O_CKV + KVLORA
O_SB = O_KR + ROPE
O_SC, O_SX = O_SB + SCW, O_SB + 2 * SCW
O_G = O_SX + SCW
BR_A, BR_B, BR_C = 0, 1, 2
V_ADA, V_N1, V_N2, V_GN, V_QN, V_KN, V_SC, V_GK = 0, 48, 56, 64, 68, 70, 71, 83
VA = 87
V_FW, V_FB = 0, 3 * KF
VB = 4 * KF
VC_FIN, VC_CTX, VC_LAT = 0, 8, 16
VC = 24
SH1, SC1, G1, SH2, SC2, G2 = (8 * m for m in range(6))
K_ID, K_MF, K_MB, K_SCAN, K_ROPE = 0, 128, 192, 256, 768
K_ALL = 1024

PROJ = [(8, 1)] * 3 + [(8, 7)] + [(8, 1)] * 12
MLA_BODY = [(7, 7), (8, 1), (7, 7), (8, 1)]
HEAD_PANELS = [(8, 1), (8, 1), (8, 1), (4, 1), (8, 1), (4, 1)]
GLA = ([(8, 1)] * 2 + HEAD_PANELS * 2) * 2
GATE_BODY = [(8, 1), (4, 1)] * 2
WO = [(8, 1)] * 8
UP_BODY = [(8, 1)] * 4
VEC_DMAS = L * 11 + 3


def down_body(part):
    return [(FF_PARTS[part], 1)] * 4


class Panel:

    def __init__(self, slot, turn, loaded, nk, dmas):
        self.slot, self.turn, self.loaded, self.nk, self.dmas = slot, turn, loaded, nk, dmas


class Stream:

    def __init__(self):
        self.turns, self.loaded, self.at = [0] * SLOTS, [0] * SLOTS, 0

    def take(self, kinds):
        out = []
        for nk, dmas in kinds:
            s = self.at % SLOTS
            self.loaded[s] += 16 * dmas
            out.append(Panel(s, self.turns[s], self.loaded[s], nk, dmas))
            self.turns[s] += 1
            self.at += 1
        return out

    def peek(self, kinds):
        keep = list(self.turns), list(self.loaded), self.at
        out = self.take(kinds)
        self.turns, self.loaded, self.at = keep
        return out

    def body(self, i, kinds):
        assert self.at % SLOTS == 0 and len(kinds) == SLOTS
        return [Panel(s, i + self.turns[s], i * (16 * d) + (self.loaded[s] + 16 * d), nk, d)
                for s, (nk, d) in enumerate(kinds)]

    def skip(self, n, kinds):
        for _ in range(n):
            self.take(kinds)


class Steps:

    def __init__(self, eng, sem):
        self.eng, self.sem, self.base, self.n = eng, sem, 0, 0

    def link(self, ins):
        self.mark(ins)
        self.wait()

    def mark(self, ins):
        ins.then_inc(self.sem, 1)
        self.n += 1

    def wait(self, back=0):
        self.eng.wait_ge(self.sem, self.base + (self.n - back))

    def enter(self, i, per):
        self.kept, self.per, self.base = self.n, per, i * per

    def leave(self, turns):
        assert self.n - self.kept == self.per, self.n - self.kept
        self.base, self.n = 0, self.kept + self.per * turns


def build(nc, x, c, ctx, c_ctx, w_ada, b_ada, norm1_g, w_in, w_gk2, b_gk2, gla_norm_g, mla_q_norm_g,
          w_uq, mla_kv_norm_g, w_ukv, sc_w, w_br_a, w_br_b, w_br_c, w_o, norm2_g, w_ffn_gate,
          w_ffn_up, ffn_conv_w, ffn_conv_b, w_ffn_down, final_norm_g, consts, out):
    w_br = [w_br_a, w_br_b, w_br_c]

    with ExitStack() as stack:
        def sb(name, shape, dt=F32):
            return stack.enter_context(nc.sbuf_tensor(name, shape, dt))

        def sem(name):
            return stack.enter_context(nc.semaphore(name))

        def sems(name, n):
            return [sem(f"{name}{i}") for i in range(n)]

        bank = [stack.enter_context(nc.psum_tensor(f"bank{i}", [P, 512], F32)) for i in range(8)]

        raw = sb("raw", [P, SLOTS, 8, P])
        whi = sb("whi", [P, SLOTS, 8, P], F32R)
        wlo = sb("wlo", [P, SLOTS, 8, P], F32R)
        X = sb("X", [P, KD, T])
        hhi = sb("hhi", [P, KD, T], F32R)
        hlo = sb("hlo", [P, KD, T], F32R)
        M = sb("M", [P, KD, T])
        ahi = sb("ahi", [P, 8, T], F32R)
        alo = sb("alo", [P, 8, T], F32R)
        chi = sb("chi", [P, 3, T], F32R)
        clo = sb("clo", [P, 3, T], F32R)
        TA = sb("TA", [P, 2, T])
        TB = sb("TB", [P, 2, T])
        R = sb("R", [P, T])
        K = sb("K", [P, K_ALL])
        ones = sb("ones", [P, P])
        eps = sb("eps", [P, 1])
        va = sb("va", [P, L, VA])
        vb = sb("vb", [P, L, VB])
        vc = sb("vc", [P, VC])
        cs = sb("cs", [P, KD, 2])
        mod = sb("mod", [P, L, 48, 2])
        am = sb("am", [P, L, 2, KD, 2])
        Z = sb("Z", [P, 7680])
        W2 = sb("W2", [2 * RANK, GH, P])

        z_vec = [slice(n * P, (n + 1) * P) for n in range(5)]
        vec_rows = [VA, VA, VB, VB, VC]

        def zv(at, *shape):
            n = int(np.prod(shape))
            v = Z[:, at:at + n]
            if len(shape) == 2:
                v = v.rearrange("p (a b) -> p a b", a=shape[0])
            if len(shape) == 3:
                v = v.rearrange("p (a b c) -> p a b c", a=shape[0], b=shape[1])
            return v

        LR = Z[0:2 * RANK, 0:T]
        z0 = T
        adaw = zv(z0, ADA_SLOTS, ADA_CHUNK)
        adarow = Z[0:2, z0 + 2048:z0 + 2560]
        cf = zv(z0 + 2560, 3, T)
        R2 = zv(z0 + 4096, T)
        cu = zv(z0 + 4608, 2, T)
        cy = zv(z0 + 5632, 2, T)
        kr = zv(z0 + 6656, T)
        assert z0 + 7168 <= 7680
        fy, fs = cu, cy
        ff = zv(z0 + 2560, 2, T)
        Kb = zv(z0, 2, T)
        Qb = zv(z0 + 1024, 2, T)
        vT = zv(z0 + 2048, T)
        Vm = zv(z0 + 2560, 2, 4, MDV)
        Pc = zv(z0 + 3072, 2, C)
        Pl = zv(z0 + 3584, 2, T)
        Tc = zv(z0 + 4608, 2, C)
        Tl = zv(z0 + 5120, 4, C)
        OF = zv(z0 + 6144, T)
        mx = zv(z0 + 6656, 4, 4)
        gq = zv(z0, 2, T)
        gk = zv(z0 + 1024, 2, T)
        gV = zv(z0 + 2048, 4, DV)
        gvT = zv(z0 + 2560, T)
        gr = zv(z0 + 3072, T)
        gx = zv(z0 + 3584, T)
        gE = zv(z0 + 4096, T)
        gst = zv(z0 + 4608, T)
        gKT = zv(z0 + 5120, 4, P)
        gA = zv(z0 + 5632, 4, P)
        gS = zv(z0 + 6144, NCH, DV)
        assert z0 + 6144 + NCH * DV <= 7680

        scale = float(QK) ** -0.5

        raw_loaded = sems("raw_loaded", SLOTS)
        hi_ready = sems("hi_ready", SLOTS)
        lo_ready = sems("lo_ready", SLOTS)
        panel_done = sems("panel_done", SLOTS)
        bank_free = sems("bank_free", SLOTS)
        ada_loaded = sems("ada_loaded", ADA_SLOTS)
        ada_used = sem("ada_used")
        ada_row = sem("ada_row")
        ada_cols = sem("ada_cols")
        ada_mod = sem("ada_mod")
        consts_in = sem("consts_in")
        vecs_in = sem("vecs_in")
        tokens_in = sem("tokens_in")
        w2_zero = sem("w2_zero")
        w2_in = sem("w2_in")
        start_t = sem("start_t")
        start_c = sem("start_c")
        fin_t = sem("fin_t")
        fin_a = sem("fin_a")
        fin_v = sem("fin_v")
        stored = sem("stored")
        act_step = sem("act_step")
        dve_step = sem("dve_step")
        x_ready = sem("x_ready")
        sq_ready = sem("sq_ready")
        sum_ready = sem("sum_ready")
        stat_ready = sem("stat_ready")
        std_ready = sem("std_ready")
        t_ready = sem("t_ready")
        hf_hi = sem("hf_hi")
        h_ready = sem("h_ready")
        coef = sem("coef")
        m_ready = sem("m_ready")
        m_hi = sem("m_hi")
        m_lo = sem("m_lo")

        per_layer = {}

        def event(name, context_layer, last_layer=None):
            per_layer[name] = context_layer
            return sem(name)

        cf_ready = event("cf_ready", 3)
        cf_sq = event("cf_sq", 3)
        c_stat = event("c_stat", 2)
        c_std = event("c_std", 2)
        c_norm = event("c_norm", 3)
        c_hi = event("c_hi", 3)
        c_lo = event("c_lo", 3)
        kr_act = event("kr_act", 1)
        kr_dve = event("kr_dve", 1)
        conv_mid = event("conv_mid", 4)
        cat_hi = event("cat_hi", 12)
        cat_lo = event("cat_lo", 12)
        a_q = event("a_q", MH)
        a_kv = event("a_kv", MH)
        q_act = event("q_act", MH)
        q_dve = event("q_dve", MH)
        k_act = event("k_act", MH)
        v_turned = event("v_turned", MH)
        v_act = event("v_act", MH)
        scored = event("scored", 4 * MH)
        max_ready = event("max_ready", MH)
        exped = event("exped", 4 * MH)
        p_ready = event("p_ready", 4 * MH)
        p_turned = event("p_turned", 3 * MH)
        pt_act = event("pt_act", 2 * MH)
        pt_dve = event("pt_dve", MH)
        o_done = event("o_done", MH)
        o_act = event("o_act", MH)
        z_done = event("z_done", GH)
        z_ln = event("z_ln", GH)
        z_read = event("z_read", GH)
        b_ready = event("b_ready", GH)
        e_ready = event("e_ready", GH)
        qk_decayed = event("qk_decayed", GH)
        kst_ready = event("kst_ready", GH)
        g_turned = event("g_turned", 2 * GH)
        g_turned_act = event("g_turned_act", 2 * GH)
        ga_done = event("ga_done", GH)
        ga_masked = event("ga_masked", GH)
        gu_done = event("gu_done", 2 * GH)
        gs_ready = event("gs_ready", GH)
        go_done = event("go_done", GH)
        go_sq = event("go_sq", GH)
        g_stat = event("g_stat", GH)
        g_std = event("g_std", GH)
        r_tanh = event("r_tanh", GH)
        go_norm = event("go_norm", GH)
        f_mid = event("f_mid", KF)
        f_silu = event("f_silu", KF)
        f_hi = event("f_hi", KF)
        f_lo = event("f_lo", KF)

        def at(name, l, value):
            return value + per_layer[name] * l

        block = stack.enter_context(nc.Block())

        def q0(l):
            return 0 if l < L - 1 else C

        def streams(l):
            return [0, 1] if l < L - 1 else [1]

        def cols(st):
            return slice(C * st, C * st + C)

        def seg(ap, l):
            return ap.rearrange("p (s n) -> p s n", n=C)[:, q0(l) // C:, :]

        def flat(ap):
            return ap.rearrange("p a n -> p (a n)")

        def scan_order(back):
            if not back:
                return list(range(NCH))
            h = NCH // 2
            return list(range(h - 1, -1, -1)) + list(range(NCH - 1, h - 1, -1))

        def parts(l):
            return [(sum(FF_PARTS[:n]), FF_PARTS[n]) for n in range(len(FF_PARTS))]

        @block.sync
        def _(sp):
            st = Stream()

            def slot_of(p):
                if not (isinstance(p.turn, int) and p.turn == 0):
                    sp.wait_ge(lo_ready[p.slot], p.turn)
                return raw[:, p.slot]

            def load(p, src):
                sp.dma_start(slot_of(p)[:, 0:p.nk, :], src.rearrange("(k p) n -> p k n", p=P)) \
                    .then_inc(raw_loaded[p.slot], 16)

            def load_ada(l, chunk, k, unit_turn, first):
                slot = k % ADA_SLOTS
                if not first:
                    sp.wait_ge(ada_used, unit_turn + k - ADA_SLOTS + 1)
                sp.dma_start(adaw[:, slot, :],
                             w_ada[l, k * P:(k + 1) * P, bass.ds(chunk * ADA_CHUNK, ADA_CHUNK)]) \
                    .then_inc(ada_loaded[slot], 16)

            def swapped(dst, src, sem_):
                for half in range(2):
                    for axis in range(2):
                        to, fro = axis * 16 + half * 8, axis * 16 + (1 - half) * 8
                        sp.dma_start(dst[:, :, to:to + 8], src[:, :, fro:fro + 8]).then_inc(sem_, 16)

            sp.dma_start(K[:, :], consts).then_inc(consts_in, 16)
            tok = flat(M[:, :, :]).rearrange("p (t d) -> p t d", t=4)
            sp.dma_start(tok[:, 0:2, :], ctx[0].rearrange("(t p) d -> p t d", p=P)).then_inc(tokens_in, 16)
            sp.dma_start(tok[:, 2:4, :], x[0].rearrange("(t p) d -> p t d", p=P)).then_inc(tokens_in, 16)
            n = 0
            for l in range(L):
                va_rows, vb_rows = Z[:, z_vec[l]], Z[:, z_vec[2 + l]]
                for rows, src in ((V_ADA, b_ada[l]), (V_N1, norm1_g[l]), (V_N2, norm2_g[l]),
                                  (V_GN, gla_norm_g[l]), (V_QN, mla_q_norm_g[l]),
                                  (V_KN, mla_kv_norm_g[l]), (V_SC, sc_w[l].rearrange("a b -> (a b)"))):
                    src = src.rearrange("(a b) -> a b", b=P)
                    sp.dma_start(va_rows[rows:rows + src.shape[0], :], src).then_inc(vecs_in, 16)
                    n += 1
                for way in range(2):
                    sp.dma_start(va_rows[V_GK:V_GK + GH, way * DK:(way + 1) * DK],
                                 b_gk2[l, way].rearrange("(h k) -> h k", h=GH)).then_inc(vecs_in, 16)
                    n += 1
                for rows, src in ((V_FW, ffn_conv_w[l].rearrange("a b -> (a b)")), (V_FB, ffn_conv_b[l])):
                    src = src.rearrange("(a b) -> a b", b=P)
                    sp.dma_start(vb_rows[rows:rows + src.shape[0], :], src).then_inc(vecs_in, 16)
                    n += 1
            for rows, src in ((VC_FIN, final_norm_g), (VC_CTX, c_ctx), (VC_LAT, c[0])):
                sp.dma_start(Z[rows:rows + KD, z_vec[4]], src.rearrange("(a b) -> a b", b=P)) \
                    .then_inc(vecs_in, 16)
                n += 1
            assert n == VEC_DMAS

            def load_w2(l):
                if l == 0:
                    sp.wait_ge(w2_zero, 1)
                else:
                    sp.wait_ge(z_done, at("z_done", l, 0))
                for way in range(2):
                    sp.dma_start(W2[way * RANK:(way + 1) * RANK, :, way * DK:(way + 1) * DK],
                                 w_gk2[l, way].rearrange("r (h k) -> r h k", h=GH)).then_inc(w2_in, 16)

            load_w2(0)
            sp.wait_ge(start_t, KD + 1)
            for chunk in range(4):
                for k in range(KD):
                    load_ada(0, chunk, k, chunk * KD, chunk == 0 and k < ADA_SLOTS)

            for l in range(L):
                starts = [O_CQ, O_CQ + P, O_CKV, None]
                for j in range(4):
                    starts += [O_SC + j * P, O_SX + j * P, O_SB + j * P]
                for n, p in enumerate(st.take(PROJ)):
                    if starts[n] is not None:
                        load(p, w_in[l][:, starts[n]:starts[n] + P])
                    else:
                        dst = slot_of(p)
                        w = w_in[l].rearrange("(k p) n -> p k n", p=P)
                        sp.dma_start(dst[:, :, 0:ROPE], w[:, :, O_LR:O_LR + 2 * RANK]) \
                            .then_inc(raw_loaded[p.slot], 16)
                        sp.dma_start(dst[:, :, ROPE:2 * ROPE], w[:, :, O_KR:O_KR + ROPE]) \
                            .then_inc(raw_loaded[p.slot], 16)
                        sp.dma_start(dst[:, :, 2 * ROPE:3 * ROPE], w[:, :, O_KR:O_KR + ROPE]) \
                            .then_inc(raw_loaded[p.slot], 16)
                        swapped(dst[:, :, 3 * ROPE:], w[:, :, O_KR:O_KR + ROPE], raw_loaded[p.slot])
                    if l == 0:
                        chunk = 4 + n // 2
                        for k in range(4 * (n % 2), 4 * (n % 2) + 4):
                            load_ada(0, chunk, k, chunk * KD, False)
                with sp.Fori(0, MH // 2) as i:
                    for p in st.body(i, MLA_BODY):
                        h = i * 2 + p.slot // 2
                        if p.slot % 2 == 0:
                            wc = w_br_c[l][:, bass.ds(h * P, P)].rearrange("(k p) n -> p k n", p=P)
                            wq = w_uq[l].rearrange("(k p) n -> p k n", p=P)
                            wr = wq[:, :, bass.ds(h * QK + NOPE, ROPE)]
                            wq = wq[:, :, bass.ds(h * QK, QK)]
                            wkv = w_ukv[l][:, bass.ds(h * P, P)]
                            dst = slot_of(p)
                            for part, src in ((dst[:, 0:4, :], wc), (dst[:, 4:6, 0:QK], wq), (dst[:, 6, :], wkv)):
                                sp.dma_start(part, src).then_inc(raw_loaded[p.slot], 16)
                            swapped(dst[:, 4:6, QK:P], wr, raw_loaded[p.slot])
                        else:
                            load(p, w_in[l][:, bass.ds(h * P + (O_G + BR_C * D), P)])
                st.skip(MH // 2, MLA_BODY)
                if l > 0:
                    load_w2(l)
                ps = iter(st.take(GLA))
                for h in range(GH):
                    if h % 2 == 0:
                        load(next(ps), w_in[l][:, O_Q + h * DK:O_Q + h * DK + P])
                        load(next(ps), w_in[l][:, O_K + h * DK:O_K + h * DK + P])
                    load(next(ps), w_in[l][:, O_V + h * DV:O_V + h * DV + P])
                    load(next(ps), w_in[l][:, O_R + h * DV:O_R + h * DV + P])
                    for j in (2 * h, 2 * h + 1):
                        load(next(ps), w_in[l][:, O_G + BR_B * D + j * P:O_G + BR_B * D + (j + 1) * P])
                        load(next(ps), w_br_b[l][:, j * P:(j + 1) * P])
                with sp.Fori(0, KD // 2) as i:
                    for p in st.body(i, GATE_BODY):
                        j = i * 2 + p.slot // 2
                        if p.slot % 2 == 0:
                            load(p, w_in[l][:, bass.ds(i * (2 * P) + (p.slot // 2 * P + O_G + BR_A * D), P)])
                        else:
                            load(p, w_br_a[l][:, bass.ds(j * P, P)])
                st.skip(KD // 2, GATE_BODY)
                with sp.Fori(0, KD // SLOTS) as i:
                    for p in st.body(i, UP_BODY):
                        load(p, w_o[l][:, bass.ds(i * (SLOTS * P) + p.slot * P, P)])
                st.skip(KD // SLOTS, UP_BODY)
                for n, (off, tiles) in enumerate(parts(l)):
                    with sp.Fori(0, tiles // 2) as i:
                        for p in st.body(i, UP_BODY):
                            w = w_ffn_gate if p.slot % 2 == 0 else w_ffn_up
                            load(p, w[l][:, bass.ds(i * (2 * P) + (off + p.slot // 2) * P, P)])
                            if l == 0 and p.slot < 2:
                                for k in range(4 * p.slot, 4 * p.slot + 4):
                                    load_ada(1, i + off // 2, k, (i + (12 + off // 2)) * KD, False)
                    st.skip(tiles // 2, UP_BODY)
                    with sp.Fori(0, KD // SLOTS) as i:
                        for p in st.body(i, down_body(n)):
                            load(p, w_ffn_down[l][off * P:(off + tiles) * P,
                                                  bass.ds(i * (SLOTS * P) + p.slot * P, P)])
                    st.skip(KD // SLOTS, down_body(n))
                if l == 0:
                    for k in range(KD):
                        load_ada(1, 11, k, 23 * KD, False)
            for t in range(2):
                sp.wait_ge(fin_a if t else fin_v, 2)
                sp.dma_start(out[0, t * P:(t + 1) * P, :], Z[:, t * D:(t + 1) * D]).then_inc(stored, 16)
            sp.wait_ge(stored, 32)

        @block.tensor
        def _(pe):
            st = Stream()
            ident = K[:, K_ID:K_ID + P]

            def weights(p):
                pe.wait_ge(lo_ready[p.slot], p.turn + 1)

            def bank_of(p):
                if not (isinstance(p.turn, int) and p.turn == 0):
                    pe.wait_ge(bank_free[p.slot], p.turn)
                return bank[p.slot]

            def mm3(dst, p, ks, rhi, rlo, before=None):
                for n, k in enumerate(ks):
                    if before is not None:
                        before(n)
                    hi, lo = whi[:, p.slot, k, :], wlo[:, p.slot, k, :]
                    pe.matmul(dst, hi, rlo(n), start=(n == 0), stop=False)
                    pe.matmul(dst, hi, rhi(n), start=False, stop=False)
                    last = pe.matmul(dst, lo, rhi(n), start=False, stop=(n == len(ks) - 1))
                return last

            def project(p, first, before=None):
                weights(p)
                mm3(bank_of(p)[:, first:T], p, range(KD), lambda k: hhi[:, k, first:T],
                    lambda k: hlo[:, k, first:T], before).then_inc(panel_done[p.slot], 1)

            def branch(p, tile0, first):
                weights(p)
                mm3(bank_of(p)[:, first:T], p, range(4), lambda k: ahi[:, tile0 + k, first:T],
                    lambda k: alo[:, tile0 + k, first:T]).then_inc(panel_done[p.slot], 1)

            def ada_unit(k, turn):
                if k == 0:
                    if not (isinstance(turn, int) and turn == 0):
                        pe.wait_ge(ada_row, turn)
                pe.wait_ge(ada_loaded[k % ADA_SLOTS], turn * 32 + 16 * (k // ADA_SLOTS + 1))
                pe.matmul(bank[7][0:2, :], cs[:, k, :], adaw[:, k % ADA_SLOTS, :], start=(k == 0),
                          stop=(k == KD - 1)).then_inc(ada_used, 1)

            def ada_wait(turn):
                pe.wait_ge(ada_row, turn + 1)
                if not (isinstance(turn, int) and turn == 0):
                    pe.wait_ge(ada_mod, turn)

            def ada_turn(turn):
                for m in range(4):
                    last = pe.transpose(bank[6][:, 2 * m:2 * m + 2], adarow[:, m * P:(m + 1) * P],
                                        ident[0:2, 0:2])
                last.then_inc(ada_cols, 1)

            def norm_stat(m, first):
                pe.wait_ge(sum_ready, m + 1)
                pe.matmul(bank[4][:, first:T], ones[:, :], M[:, 0, first:T], start=True, stop=False)
                pe.matmul(bank[4][:, first:T], ones[:, :], M[:, 1, first:T], start=False, stop=True) \
                    .then_inc(stat_ready, 1)

            pe.wait_ge(consts_in, 16)
            pe.wait_ge(vecs_in, 16 * VEC_DMAS)
            for n, rows in enumerate(vec_rows):
                last = pe.transpose(bank[5][:, n * 96:n * 96 + rows], Z[0:rows, z_vec[n]],
                                    ident[0:rows, 0:rows])
            last.then_inc(start_t, 1)
            pe.wait_ge(tokens_in, 32)
            tok = flat(M[:, :, :]).rearrange("p (t d) -> p t d", t=4)
            for k in range(KD):
                if k >= 4:
                    pe.wait_ge(x_ready, k - 3)
                for t in range(4):
                    last = pe.transpose(bank[k % 4][:, t * P:(t + 1) * P], tok[:, t, k * P:(k + 1) * P],
                                        ident)
                last.then_inc(start_t, 1)
            pe.wait_ge(start_c, 1)
            for turn in range(4):
                for k in range(KD):
                    ada_unit(k, turn)
                ada_wait(turn)
                ada_turn(turn)

            for l in range(L):
                first = q0(l)
                norm_stat(2 * l, 0)
                for n, p in enumerate(st.take(PROJ)):
                    if n == 0:
                        project(p, first, lambda k: pe.wait_ge(h_ready, 8 * 2 * l + k + 1))
                    else:
                        project(p, 0 if n in (2, 3) else first)
                    if n == 4:
                        pe.wait_ge(cf_sq, at("cf_sq", l, 3))
                        pe.matmul(bank[4][:, first:T], ones[:, :], cy[:, 0, first:T], start=True, stop=False)
                        pe.matmul(bank[4][:, first:T], ones[:, :], cy[:, 1, first:T], start=False, stop=True) \
                            .then_inc(c_stat, 1)
                        pe.matmul(bank[5][:, :], ones[:, :], cu[:, 0, :], start=True, stop=True) \
                            .then_inc(c_stat, 1)
                    if l == 0:
                        turn = 4 + n // 2
                        if n % 2 == 0 and n > 0:
                            ada_wait(turn - 1)
                            ada_turn(turn - 1)
                        for k in range(4 * (n % 2), 4 * (n % 2) + 4):
                            ada_unit(k, turn)
                if l == 0:
                    ada_wait(11)
                    ada_turn(11)
                pe.wait_ge(c_lo, at("c_lo", l, 3))
                pe.wait_ge(kr_dve, at("kr_dve", l, 1))
                pe.wait_ge(cat_lo, at("cat_lo", l, 4))
                nt = 4 if l == 0 else 2
                nb = 3 if l == 0 else 2
                with pe.Fori(0, MH // 2) as i:
                    ps = st.body(i, MLA_BODY)

                    def heads(e):
                        return i * 2 + (e + 1)

                    def project_head(e):
                        p = ps[2 * e]
                        weights(p)
                        if e == 1:
                            pe.wait_ge(exped, i * (2 * nt) + (at("exped", l, 0) + nt))
                        mm3(bank[4][:, first:T], p, (4, 5), lambda k: chi[:, k, first:T],
                            lambda k: clo[:, k, first:T]).then_inc(a_q, 1)
                        mm3(bank[5][:, :], p, (6,), lambda k: chi[:, 2, :], lambda k: clo[:, 2, :]) \
                            .then_inc(a_kv, 1)

                    def score(e):
                        pe.wait_ge(k_act, heads(e) + at("k_act", l, 0))
                        pe.wait_ge(q_act, heads(e) + at("q_act", l, 0))
                        pe.wait_ge(q_dve, heads(e) + at("q_dve", l, 0))
                        if e == 0:
                            pe.wait_ge(cat_hi, i + at("cat_hi", l, 4))
                        else:
                            pe.wait_ge(o_act, i * 2 + at("o_act", l, 1))
                        for t in range(2):
                            pe.matmul(bank[4 + t][:, :], Qb[0:QK, e, C + t * P:C + (t + 1) * P], Kb[0:QK, e, :],
                                      start=True, stop=True).then_inc(scored, 1)
                        if l == 0:
                            for t in range(2):
                                pe.matmul(bank[7][:, t * C:(t + 1) * C], Qb[0:QK, e, t * P:(t + 1) * P],
                                          Kb[0:QK, e, 0:C], start=True, stop=True).then_inc(scored, 1)
                        for t in range(4):
                            last = pe.transpose(bank[6][:, t * MDV:(t + 1) * MDV], vT[MDV:2 * MDV, t * P:(t + 1) * P],
                                                ident[MDV:2 * MDV, MDV:2 * MDV])
                        last.then_inc(v_turned, 1)

                    def values(e):
                        pe.wait_ge(p_ready, heads(e) * nt + at("p_ready", l, 0))
                        if e == 0:
                            pe.wait_ge(k_act, i * 2 + (at("k_act", l, 0) + 2))
                            pe.wait_ge(q_act, i * 2 + (at("q_act", l, 0) + 2))
                            pe.wait_ge(q_dve, i * 2 + (at("q_dve", l, 0) + 2))
                        for k in range(4):
                            for t in range(2):
                                at_ = (k % 2) * C + t * P
                                last = pe.transpose(bank[4 + k // 2][:, at_:at_ + P],
                                                    Pl[:, t, k * P:(k + 1) * P], ident)
                            if k % 2:
                                last.then_inc(p_turned, 1)
                        if l == 0:
                            for k in range(2):
                                for t in range(2):
                                    last = pe.transpose(bank[7][:, k * C + t * P:k * C + (t + 1) * P],
                                                        Pc[:, t, k * P:(k + 1) * P], ident)
                            last.then_inc(p_turned, 1)
                        pe.wait_ge(v_act, heads(e) + at("v_act", l, 0))
                        pe.wait_ge(pt_act, i * (2 * (nb - 1)) + (at("pt_act", l, 0) + e * (nb - 1) + 1))
                        for k in range(4):
                            if k == 2:
                                pe.wait_ge(pt_dve, heads(e) + at("pt_dve", l, 0))
                            last = pe.matmul(bank[6][0:MDV, C:T], Vm[:, e, k, :], Tl[:, k, :],
                                             start=(k == 0), stop=(k == 3))
                        if l == 0:
                            pe.wait_ge(pt_act, heads(e) * 2 + at("pt_act", l, 0))
                            for k in range(2):
                                last = pe.matmul(bank[6][0:MDV, 0:C], Vm[:, e, k, :], Tc[:, k, :],
                                                 start=(k == 0), stop=(k == 1))
                        last.then_inc(o_done, 1)

                    project_head(0)
                    project(ps[1], first)
                    score(0)
                    branch(ps[0], 0, first)
                    project_head(1)
                    values(0)
                    score(1)
                    project(ps[3], first)
                    branch(ps[2], 0, first)
                    values(1)
                st.skip(MH // 2, MLA_BODY)
                pe.wait_ge(w2_in, 32 * (l + 1))
                ps = iter(st.take(GLA))
                chunks = range(first // CHUNK, NCH)
                for h in range(GH):
                    e = h % 2
                    if e == 0:
                        project(next(ps), first)
                        project(next(ps), 0)
                    pv = next(ps)
                    project(pv, 0)
                    if h > 0:
                        pe.wait_ge(gs_ready, at("gs_ready", l, h))
                    else:
                        pe.wait_ge(pt_act, at("pt_act", l, (nb - 1) * MH))
                    pe.matmul(bank[4][:, :], W2[:, h, :], LR, start=True, stop=True).then_inc(z_done, 1)
                    project(next(ps), first)
                    project(next(ps), first)
                    if h == 0:
                        pe.wait_ge(cat_lo, at("cat_lo", l, 8))
                    branch(next(ps), 4, first)
                    pe.wait_ge(bank_free[pv.slot], pv.turn + 1)
                    for t in range(4):
                        last = pe.transpose(bank[5][:, t * P:(t + 1) * P], gvT[:, t * P:(t + 1) * P], ident)
                    last.then_inc(g_turned, 1)
                    pe.wait_ge(kst_ready, at("kst_ready", l, h + 1))
                    if h > 0:
                        pe.wait_ge(go_norm, at("go_norm", l, h))
                    for t in range(4):
                        last = pe.transpose(bank[6][:, t * P:(t + 1) * P], gst[:, t * P:(t + 1) * P], ident)
                    last.then_inc(g_turned, 1)
                    for n in chunks:
                        for way in range(2):
                            r = slice(way * DK, (way + 1) * DK)
                            o = slice((n % 2) * CHUNK, (n % 2 + 1) * CHUNK)
                            at_ = (n // 2) * CHUNK
                            tk = slice(n * CHUNK, (n + 1) * CHUNK)
                            last = pe.matmul(bank[7 if way else 4][o, at_:at_ + CHUNK], gk[r, e, tk], gq[r, e, tk],
                                             start=True, stop=True)
                    last.then_inc(ga_done, 1)
                    project(next(ps), first)
                    pe.wait_ge(g_turned_act, at("g_turned_act", l, 2 * h + 2))
                    pe.wait_ge(ga_masked, at("ga_masked", l, h + 1))
                    for n in range(NCH):
                        o = slice((n % 2) * CHUNK, (n % 2 + 1) * CHUNK)
                        last = pe.matmul(bank[4 + n % 2][:, (n // 2) * DV:(n // 2 + 1) * DV],
                                         gKT[o, n // 2, :], gV[o, n // 2, :], start=True, stop=True)
                        if n >= NCH - 2:
                            last.then_inc(gu_done, 1)
                    branch(next(ps), 4, first)
                    for n in range(first // P, T // P):
                        pe.matmul(bank[6][:, n * P:(n + 1) * P], gV[:, n, :], gA[:, n, :],
                                  start=(n == first // P), stop=False, skip_group_check=True)
                    pe.wait_ge(gs_ready, at("gs_ready", l, h + 1))
                    for n in chunks:
                        tk = slice(n * CHUNK, (n + 1) * CHUNK)
                        last = pe.matmul(bank[6][:, tk], gS[:, n, :], gq[:, e, tk], start=False,
                                         stop=(n == NCH - 1), skip_group_check=True)
                    last.then_inc(go_done, 1)
                    pe.wait_ge(go_sq, at("go_sq", l, h + 1))
                    pe.matmul(bank[7][:, first:T], ones[:, :], gvT[:, first:T], start=True, stop=True) \
                        .then_inc(g_stat, 1)
                pe.wait_ge(cat_lo, at("cat_lo", l, 12))
                with pe.Fori(0, KD // 2) as i:
                    for n, p in enumerate(st.body(i, GATE_BODY)):
                        if n % 2 == 0:
                            project(p, first)
                        else:
                            branch(p, 0, first)
                st.skip(KD // 2, GATE_BODY)
                with pe.Fori(0, KD // SLOTS) as i:
                    for n, p in enumerate(st.body(i, UP_BODY)):
                        project(p, first, (lambda k: pe.wait_ge(m_lo, 8 * l + k + 1)) if n == 0 else None)
                st.skip(KD // SLOTS, UP_BODY)
                norm_stat(2 * l + 1, first)
                for n, (off, tiles) in enumerate(parts(l)):
                    with pe.Fori(0, tiles // 2) as i:
                        for m, p in enumerate(st.body(i, UP_BODY)):
                            if l == 0 and m == 3:
                                ada_wait(i + (12 + off // 2))
                            project(p, first, (lambda k: pe.wait_ge(h_ready, 8 * (2 * l + 1) + k + 1))
                                    if m == 0 and n == 0 else None)
                            if l == 0 and m < 2:
                                for k in range(4 * m, 4 * m + 4):
                                    ada_unit(k, i + (12 + off // 2))
                            if l == 0 and m == 3:
                                ada_turn(i + (12 + off // 2))
                    st.skip(tiles // 2, UP_BODY)
                    pe.wait_ge(f_lo, at("f_lo", l, off + tiles))
                    with pe.Fori(0, KD // SLOTS) as i:
                        for p in st.body(i, down_body(n)):
                            weights(p)
                            mm3(bank_of(p)[:, first:T], p, range(tiles), lambda k: ahi[:, k, first:T],
                                lambda k: alo[:, k, first:T]).then_inc(panel_done[p.slot], 1)
                    st.skip(KD // SLOTS, down_body(n))
                if l == 0:
                    for k in range(KD):
                        ada_unit(k, 23)
                    ada_wait(23)
                    ada_turn(23)
            norm_stat(2 * L, C)
            for k in range(KD):
                pe.wait_ge(h_ready, 8 * 2 * L + k + 1)
                for t in range(2):
                    last = pe.transpose(bank[2 * t + k // 4][:, (k % 4) * P:(k % 4 + 1) * P],
                                        M[:, k, C + t * P:C + (t + 1) * P], ident)
                    if k % 4 == 3:
                        last.then_inc(fin_t, 1)

        @block.scalar
        def _(act):
            st = Stream()
            steps = Steps(act, act_step)

            def split(p):
                act.wait_ge(raw_loaded[p.slot], p.loaded)
                if not (isinstance(p.turn, int) and p.turn == 0):
                    act.wait_ge(panel_done[p.slot], p.turn)
                act.activation(whi[:, p.slot, 0:p.nk, :], raw[:, p.slot, 0:p.nk, :], ACT.Copy) \
                    .then_inc(hi_ready[p.slot], 1)

            def full(p):
                act.wait_ge(panel_done[p.slot], p.turn + 1)
                return bank[p.slot]

            def emptied(p):
                act.wait_ge(bank_free[p.slot], p.turn + 1)

            def gate(p, e, first):
                act.activation(TB[:, e, first:T], full(p)[:, first:T], ACT.Tanh, scale=0.5) \
                    .then_inc(bank_free[p.slot], 1)

            def ada_out(turn):
                act.wait_ge(ada_used, (turn + 1) * KD)
                if not (isinstance(turn, int) and turn == 0):
                    act.wait_ge(ada_cols, turn)
                act.activation(adarow, bank[7][0:2, :], ACT.Copy).then_inc(ada_row, 1)

            def norm(m, l, w, first, done):
                for k in range(KD):
                    if done is None:
                        act.wait_ge(x_ready, k + 1)
                    else:
                        emptied(done[k])
                    act.activation(M[:, k, first:T], X[:, k, first:T], ACT.Square).then_inc(sq_ready, 1)
                act.wait_ge(stat_ready, m + 1)
                act.activation(R[:, first:T], bank[4][:, first:T], ACT.Sqrt, scale=1.0 / D, bias=eps[:, :]) \
                    .then_inc(std_ready, 1)
                if w is None:
                    return
                act.wait_ge(coef, 2 * l + w + 1)
                for k in range(KD):
                    act.wait_ge(t_ready, 8 * m + k + 1)
                    for s_ in range(first // C, 2):
                        last = act.activation(M[:, k, cols(s_)], TA[:, k % 2, cols(s_)], ACT.Identity,
                                              scale=am[:, l, w, k, s_:s_ + 1],
                                              bias=mod[:, l, (SH2 if w else SH1) + k, s_:s_ + 1])
                    steps.link(last)
                    act.activation(hhi[:, k, first:T], M[:, k, first:T], ACT.Copy).then_inc(hf_hi, 1)

            act.wait_ge(start_t, 1)
            for s_, row in ((0, VC_CTX), (1, VC_LAT)):
                last = act.activation(cs[:, :, s_], bank[5][:, 4 * 96 + row:4 * 96 + row + KD], ACT.Silu)
            last.then_inc(start_c, 1)
            for turn in range(4):
                ada_out(turn)
            for p in st.peek(PROJ)[0:AHEAD]:
                split(p)

            done = None
            for l in range(L):
                first = q0(l)
                norm(2 * l, l, 0, 0, done)
                ps = st.take(PROJ)
                ahead = ps + st.peek(MLA_BODY)[0:AHEAD]
                for n, p in enumerate(ps):
                    split(ahead[n + AHEAD])
                    if n < 3:
                        f = 0 if n == 2 else first
                        src = full(p)[:, f:T]
                        act.activation(cf[:, n, f:T], src, ACT.Copy).then_inc(cf_ready, 1)
                        act.activation(cy[:, n, f:T] if n < 2 else cu[:, 0, :], src, ACT.Square) \
                            .then_inc(cf_sq, 1)
                        act.wait_ge(cf_sq, at("cf_sq", l, n + 1))
                        act.sem_inc(bank_free[p.slot], 1)
                    elif n == 3:
                        full(p)
                        act.activation(LR, bank[p.slot][0:2 * RANK, :], ACT.Copy)
                        act.activation(kr[NOPE:QK, 0:C], bank[p.slot][NOPE:QK, 0:C], ACT.Copy).then_inc(kr_act, 1)
                    else:
                        j, what = (n - 4) // 3, (n - 4) % 3
                        if what == 0:
                            if j >= 2:
                                emptied(ps[n - 5])
                            act.activation(TB[:, j % 2, first:T], full(p)[:, first:T], ACT.Copy) \
                                .then_inc(bank_free[p.slot], 1)
                        elif what == 1:
                            emptied(p)
                            if j >= 2:
                                act.wait_ge(cat_lo, at("cat_lo", l, j - 1))
                            act.activation(cy[:, j % 2, first:T], cu[:, j % 2, first:T], ACT.Copy,
                                           scale=va[:, l, V_SC + 4 + j:V_SC + 5 + j]).then_inc(conv_mid, 1)
                        else:
                            emptied(p)
                            act.activation(ahi[:, j, first:T], cy[:, j % 2, first:T], ACT.Copy) \
                                .then_inc(cat_hi, 1)
                    if n == 4:
                        act.wait_ge(c_stat, at("c_stat", l, 2))
                        act.activation(R[:, first:T], bank[4][:, first:T], ACT.Sqrt, scale=1.0 / QLORA,
                                       bias=eps[:, :]).then_inc(c_std, 1)
                        act.activation(R2, bank[5][:, :], ACT.Sqrt, scale=1.0 / KVLORA, bias=eps[:, :]) \
                            .then_inc(c_std, 1)
                    if 5 <= n <= 7:
                        f = 0 if n == 7 else first
                        act.wait_ge(c_norm, at("c_norm", l, n - 4))
                        act.activation(chi[:, n - 5, f:T], cf[:, n - 5, f:T], ACT.Copy).then_inc(c_hi, 1)
                    if l == 0 and n % 2:
                        ada_out(4 + n // 2)
                nt = 4 if l == 0 else 2

                def body(i, ps, after):
                    def heads(e):
                        return i * 2 + (e + 1)

                    def project_out(e):
                        act.wait_ge(a_q, heads(e) + at("a_q", l, 0))
                        if l == 0:
                            act.activation(Qb[0:QK, e, 0:C], bank[4][0:QK, 0:C], ACT.Copy)
                        act.activation(Qb[0:NOPE, e, C:T], bank[4][0:NOPE, C:T], ACT.Copy).then_inc(q_act, 1)
                        act.wait_ge(a_kv, heads(e) + at("a_kv", l, 0))
                        act.activation(Kb[0:NOPE, e, :], bank[5][0:NOPE, :], ACT.Copy)
                        act.activation(vT[NOPE:P, :], bank[5][NOPE:P, :], ACT.Copy).then_inc(k_act, 1)

                    def softmax(e):
                        act.wait_ge(v_turned, heads(e) + at("v_turned", l, 0))
                        act.activation(Vm[:, e, :, :], bank[6][:, 0:4 * MDV].rearrange("p (t n) -> p t n", t=4),
                                       ACT.Copy).then_inc(v_act, 1)
                        act.wait_ge(max_ready, heads(e) + at("max_ready", l, 0))
                        for t in range(nt):
                            src = bank[4 + t][:, :] if t < 2 else bank[7][:, (t - 2) * C:(t - 1) * C]
                            dst = Pl[:, t, :] if t < 2 else Pc[:, t - 2, :]
                            act.activation(dst, src, ACT.Exp, bias=mx[:, 1, t:t + 1], scale=scale,
                                           accum_out=mx[:, 2, t:t + 1]).then_inc(exped, 1)

                    def values_out(e):
                        nb = 3 if l == 0 else 2
                        act.wait_ge(p_turned, i * (2 * nb) + (at("p_turned", l, 0) + e * nb + 1))
                        act.activation(Tl[:, 0:2, :], bank[4][:, :].rearrange("p (k n) -> p k n", k=2), ACT.Copy) \
                            .then_inc(pt_act, 1)
                        if l == 0:
                            act.wait_ge(p_turned, i * (2 * nb) + (at("p_turned", l, 0) + e * nb + 3))
                            act.activation(Tc[:, :, :], bank[7][:, :].rearrange("p (k n) -> p k n", k=2), ACT.Copy) \
                                .then_inc(pt_act, 1)
                        act.wait_ge(o_done, heads(e) + at("o_done", l, 0))
                        act.activation(OF[e * MDV:(e + 1) * MDV, first:T], bank[6][0:MDV, first:T], ACT.Copy) \
                            .then_inc(o_act, 1)

                    project_out(0)
                    split(ps[2])
                    act.wait_ge(bank_free[0], ps[0].turn)
                    gate(ps[1], 0, first)
                    softmax(0)
                    split(ps[3])
                    project_out(1)
                    values_out(0)
                    softmax(1)
                    split(after[0])
                    act.wait_ge(bank_free[2], ps[2].turn)
                    gate(ps[3], 1, first)
                    split(after[1])
                    values_out(1)
                    act.wait_ge(o_act, i * 2 + (at("o_act", l, 2)))
                    act.activation(flat(ahi[:, bass.ds(i + 4, 1), first:T]), OF[:, first:T], ACT.Copy) \
                        .then_inc(cat_hi, 1)

                turns = MH // 2
                with act.Fori(0, turns - 1) as i:
                    body(i, st.body(i, MLA_BODY), st.body(i + 1, MLA_BODY))
                last_body = st.body(turns - 1, MLA_BODY)
                st.skip(turns, MLA_BODY)
                body(turns - 1, last_body, st.peek(GLA))

                ps = st.take(GLA)
                ahead = ps + st.peek(GATE_BODY)[0:AHEAD]
                of_branch = [p for p in ps if p.nk == 4]
                n = 0
                for h in range(GH):
                    e = h % 2
                    if e == 0:
                        for dst, f, mul in ((gq, first, DK ** -0.5), (gk, 0, 1.0)):
                            split(ahead[n + AHEAD])
                            src = full(ps[n])
                            for eh in range(2):
                                for way in range(2):
                                    last = act.activation(dst[way * DK:(way + 1) * DK, eh, f:T],
                                                          src[eh * DK:(eh + 1) * DK, f:T], ACT.Copy, scale=mul)
                            last.then_inc(bank_free[ps[n].slot], 1)
                            n += 1
                    split(ahead[n + AHEAD])
                    act.activation(gvT[:, :], full(ps[n])[:, :], ACT.Copy).then_inc(bank_free[ps[n].slot], 1)
                    n += 1
                    act.wait_ge(z_done, at("z_done", l, h + 1))
                    if h > 0:
                        act.wait_ge(cat_lo, at("cat_lo", l, 8 + h))
                    bias = va[:, l, V_GK + h:V_GK + h + 1]
                    steps.link(act.activation(gE[:, :], bank[4][:, :], ACT.Abs, bias=bias))
                    steps.link(act.activation(gE[:, :], gE[:, :], ACT.Exp, scale=-1.0))
                    act.activation(gE[:, :], gE[:, :], ACT.Ln, bias=1.0).then_inc(z_ln, 1)
                    split(ahead[n + AHEAD])
                    act.activation(gr[:, first:T], full(ps[n])[:, first:T], ACT.Tanh, scale=0.5) \
                        .then_inc(r_tanh, 1)
                    n += 1
                    act.wait_ge(b_ready, at("b_ready", l, h + 1))
                    act.activation(gE[:, :], gst[:, :], ACT.Exp, scale=1.0 / GATE_NORM)
                    act.activation(gx[:, :], gst[:, :], ACT.Exp, scale=-1.0 / GATE_NORM).then_inc(e_ready, 1)
                    split(ahead[n + AHEAD])
                    if h > 0:
                        emptied(of_branch[2 * h - 2])
                    gate(ps[n], 0, first)
                    n += 1
                    split(ahead[n + AHEAD])
                    n += 1
                    act.wait_ge(g_turned, at("g_turned", l, 2 * h + 1))
                    act.activation(gV[:, :, :], bank[5][:, :].rearrange("p (t n) -> p t n", t=4), ACT.Copy) \
                        .then_inc(g_turned_act, 1)
                    act.wait_ge(g_turned, at("g_turned", l, 2 * h + 2))
                    act.activation(gKT[:, :, :], bank[6][:, :].rearrange("p (t n) -> p t n", t=4), ACT.Copy) \
                        .then_inc(g_turned_act, 1)
                    split(ahead[n + AHEAD])
                    if h > 0:
                        emptied(of_branch[2 * h - 1])
                    gate(ps[n], 1, first)
                    n += 1
                    split(ahead[n + AHEAD])
                    n += 1
                    act.wait_ge(go_done, at("go_done", l, h + 1))
                    act.activation(gvT[:, first:T], bank[6][:, first:T], ACT.Square).then_inc(go_sq, 1)
                    act.wait_ge(g_stat, at("g_stat", l, h + 1))
                    act.activation(R[:, first:T], bank[7][:, first:T], ACT.Sqrt, scale=1.0 / DV,
                                   bias=eps[:, :]).then_inc(g_std, 1)
                    act.wait_ge(go_norm, at("go_norm", l, h + 1))
                    act.activation(ahi[:, h, first:T], gE[:, first:T], ACT.Copy, scale=0.5).then_inc(cat_hi, 1)

                def gates(i, ps, after):
                    for e in range(2):
                        split((ps + after)[2 * e + 2])
                        if e == 0:
                            act.wait_ge(bank_free[1], ps[1].turn)
                        else:
                            act.wait_ge(bank_free[3], ps[3].turn)
                        gate(ps[2 * e], e, first)
                        split((ps + after)[2 * e + 3])

                turns = KD // 2
                with act.Fori(0, turns - 1) as i:
                    gates(i, st.body(i, GATE_BODY), st.body(i + 1, GATE_BODY)[0:AHEAD])
                last_body = st.body(turns - 1, GATE_BODY)
                st.skip(turns, GATE_BODY)
                gates(turns - 1, last_body, st.peek(UP_BODY)[0:AHEAD])
                act.wait_ge(panel_done[2], last_body[2].turn + 1)
                for k in range(KD):
                    act.wait_ge(m_ready, 8 * l + k + 1)
                    act.activation(hhi[:, k, first:T], M[:, k, first:T], ACT.Copy, scale=0.5).then_inc(m_hi, 1)

                def only_split(turns, kinds, after):
                    with act.Fori(0, turns - 1) as i:
                        for p in st.body(i, kinds)[AHEAD:] + st.body(i + 1, kinds)[0:AHEAD]:
                            split(p)
                    last_ = st.body(turns - 1, kinds)
                    st.skip(turns, kinds)
                    for p in last_[AHEAD:] + st.peek(after)[0:AHEAD]:
                        split(p)
                    return last_

                prev = st.body(0, UP_BODY)
                prev += only_split(KD // SLOTS, UP_BODY, UP_BODY)
                norm(2 * l + 1, l, 1, first, prev)
                for n, (off, tiles) in enumerate(parts(l)):
                    def hidden(i, ps, after):
                        for e in range(2):
                            pg, pu = ps[2 * e], ps[2 * e + 1]
                            split((ps + after)[2 * e + 2])
                            t = i * 2 + (off + e)
                            act.activation(fy[:, e, first:T], full(pg)[:, first:T], ACT.Identity,
                                           scale=vb[:, l, bass.ds(t + (V_FW + KF), 1)],
                                           bias=vb[:, l, bass.ds(t + V_FB, 1)]).then_inc(f_mid, 1)
                            split((ps + after)[2 * e + 3])
                            emptied(pg)
                            act.activation(fs[:, e, first:T], fy[:, e, first:T], ACT.Silu).then_inc(f_silu, 1)
                            emptied(pu)
                            act.activation(flat(ahi[:, bass.ds(i * 2 + e, 1), first:T]), ff[:, e, first:T],
                                           ACT.Copy).then_inc(f_hi, 1)
                            if l == 0 and e == 0:
                                ada_out(i + (12 + off // 2))

                    turns = tiles // 2
                    with act.Fori(0, turns - 1) as i:
                        hidden(i, st.body(i, UP_BODY), st.body(i + 1, UP_BODY)[0:AHEAD])
                    last_body = st.body(turns - 1, UP_BODY)
                    st.skip(turns, UP_BODY)
                    hidden(turns - 1, last_body, st.peek(down_body(n))[0:AHEAD])
                    after = UP_BODY if n + 1 < len(FF_PARTS) else PROJ
                    done = st.body(0, down_body(n))
                    if l == L - 1 and n + 1 == len(FF_PARTS):
                        with act.Fori(0, 1) as i:
                            for p in st.body(i, down_body(n))[AHEAD:] + st.body(i + 1, down_body(n))[0:AHEAD]:
                                split(p)
                        done += st.body(1, down_body(n))
                        st.skip(2, down_body(n))
                        for p in done[4 + AHEAD:]:
                            split(p)
                    else:
                        done += only_split(KD // SLOTS, down_body(n), after)
                if l == 0:
                    ada_out(23)
            norm(2 * L, None, None, C, done)
            for q in range(2):
                act.wait_ge(fin_t, 2 * q + 2)
                act.activation(Z[:, D + q * 512:D + (q + 1) * 512], bank[2 + q][:, :], ACT.Copy) \
                    .then_inc(fin_a, 1)

        @block.vector
        def _(dve):
            st = Stream()
            steps = Steps(dve, dve_step)

            def split(p):
                dve.wait_ge(hi_ready[p.slot], p.turn + 1)
                dve.tensor_tensor(wlo[:, p.slot, 0:p.nk, :], raw[:, p.slot, 0:p.nk, :],
                                  whi[:, p.slot, 0:p.nk, :].bitcast(F32), ALU.subtract) \
                    .then_inc(lo_ready[p.slot], 1)

            def full(p):
                dve.wait_ge(panel_done[p.slot], p.turn + 1)
                return bank[p.slot]

            def norm(m, l, w, first):
                dve.wait_ge(sq_ready, 8 * (m + 1))
                steps.link(dve.tensor_tensor(M[:, 0:4, first:T], M[:, 0:4, first:T], M[:, 4:8, first:T], ALU.add))
                dve.tensor_tensor(M[:, 0:2, first:T], M[:, 0:2, first:T], M[:, 2:4, first:T], ALU.add) \
                    .then_inc(sum_ready, 1)
                dve.wait_ge(std_ready, m + 1)
                steps.link(dve.reciprocal(R[:, first:T], R[:, first:T]))
                if w is None:
                    for k in range(KD):
                        dve.scalar_tensor_tensor(out=M[:, k, first:T], in0=X[:, k, first:T],
                                                 scalar=vc[:, VC_FIN + k:VC_FIN + k + 1], in1=R[:, first:T],
                                                 op0=ALU.mult, op1=ALU.mult).then_inc(h_ready, 1)
                    return
                for k in range(KD + 1):
                    if k < KD:
                        if k >= 2:
                            dve.wait_ge(hf_hi, 8 * m + k - 1)
                        dve.tensor_tensor(TA[:, k % 2, first:T], X[:, k, first:T], R[:, first:T], ALU.mult) \
                            .then_inc(t_ready, 1)
                    if k > 0:
                        dve.wait_ge(hf_hi, 8 * m + k)
                        dve.tensor_tensor(hlo[:, k - 1, first:T], M[:, k - 1, first:T],
                                          hhi[:, k - 1, first:T].bitcast(F32), ALU.subtract) \
                            .then_inc(h_ready, 1)

            def ada_in(l, chunk, turn):
                dve.wait_ge(ada_cols, turn + 1)
                b = va[:, l, bass.ds(chunk * 4 + V_ADA, 4)] if not isinstance(chunk, int) else \
                    va[:, l, V_ADA + 4 * chunk:V_ADA + 4 * chunk + 4]
                dst = mod[:, l, bass.ds(chunk * 4, 4), :] if not isinstance(chunk, int) else \
                    mod[:, l, 4 * chunk:4 * chunk + 4, :]
                dve.tensor_tensor(dst, bank[6][:, 0:8].rearrange("p (m s) -> p m s", s=2),
                                  b.unsqueeze(2).to_broadcast([P, 4, 2]), ALU.add).then_inc(ada_mod, 1)

            def coefficients(l, w, turns):
                dve.wait_ge(ada_mod, turns)
                sc, g = (SC2, V_N2) if w else (SC1, V_N1)
                dve.scalar_tensor_tensor(out=am[:, l, w, :, :], in0=mod[:, l, sc:sc + KD, :], scalar=1.0,
                                         in1=va[:, l, g:g + KD].unsqueeze(2).to_broadcast([P, KD, 2]),
                                         op0=ALU.add, op1=ALU.mult).then_inc(coef, 1)

            def merge(p, e, j, first, begin):
                src = full(p)[:, first:T]
                dst = flat(M[:, bass.ds(j, 1), first:T]) if not isinstance(j, int) else M[:, j, first:T]
                if begin:
                    dve.scalar_tensor_tensor(out=dst, in0=TB[:, e, first:T], scalar=1.0, in1=src,
                                             op0=ALU.add, op1=ALU.mult).then_inc(bank_free[p.slot], 1)
                    return
                dve.scalar_tensor_tensor(out=TA[:, e, first:T], in0=TB[:, e, first:T], scalar=1.0, in1=src,
                                         op0=ALU.add, op1=ALU.mult).then_inc(bank_free[p.slot], 1)
                dve.wait_ge(bank_free[p.slot], p.turn + 1)
                steps.link(dve.tensor_tensor(dst, dst, TA[:, e, first:T], ALU.add))

            def residual(p, l, j, g):
                first_s = 0 if l < L - 1 else 1
                for s_ in range(first_s, 2):
                    dst = flat(X[:, bass.ds(j, 1), cols(s_)])
                    last = dve.scalar_tensor_tensor(
                        out=dst, in0=full(p)[:, cols(s_)], scalar=mod[:, l, bass.ds(j + g, 1), s_:s_ + 1]
                        .rearrange("p a b -> p (a b)"), in1=dst, op0=ALU.mult, op1=ALU.add)
                last.then_inc(bank_free[p.slot], 1)

            dve.memset(ones[:, :], 1.0)
            dve.memset(eps[:, :], EPS)
            dve.memset(W2[:, :, :], 0.0).then_inc(w2_zero, 1)
            dve.wait_ge(start_t, 1)
            dve.wait_ge(start_c, 1)
            for l in range(L):
                dve.tensor_copy(va[:, l, :], bank[5][:, l * 96:l * 96 + VA])
                dve.tensor_copy(vb[:, l, :], bank[5][:, (2 + l) * 96:(2 + l) * 96 + VB])
            dve.tensor_copy(vc[:, :], bank[5][:, 4 * 96:4 * 96 + VC])
            for k in range(KD):
                dve.wait_ge(start_t, k + 2)
                dve.tensor_copy(X[:, k, :], bank[k % 4][:, :]).then_inc(x_ready, 1)
            for turn in range(4):
                ada_in(0, turn, turn)
            coefficients(0, 0, 4)
            for p in st.peek(PROJ)[0:AHEAD]:
                split(p)

            for l in range(L):
                first = q0(l)
                norm(2 * l, l, 0, 0)
                ps = st.take(PROJ)
                ahead = ps + st.peek(MLA_BODY)[0:AHEAD]
                for n, p in enumerate(ps):
                    split(ahead[n + AHEAD])
                    if n == 3:
                        src = full(p)
                        dve.wait_ge(kr_act, at("kr_act", l, 1))
                        dve.tensor_tensor(TA[NOPE:QK, 0, C:T], src[QK:P, C:T], K[QK:P, K_ROPE:K_ROPE + C],
                                          ALU.mult)
                        steps.link(dve.tensor_tensor(kr[NOPE:QK, C:T], src[NOPE:QK, C:T],
                                                     K[NOPE:QK, K_ROPE:K_ROPE + C], ALU.mult))
                        dve.tensor_tensor(kr[NOPE:QK, C:T], kr[NOPE:QK, C:T], TA[NOPE:QK, 0, C:T], ALU.add) \
                            .then_inc(bank_free[p.slot], 1)
                    elif n > 3:
                        j, what = (n - 4) // 3, (n - 4) % 3
                        if what == 0:
                            pass
                        elif what == 1:
                            dve.wait_ge(bank_free[ps[n - 1].slot], ps[n - 1].turn + 1)
                            dve.tensor_tensor(cu[:, j % 2, first:T], TB[:, j % 2, first:T], full(p)[:, first:T],
                                              ALU.mult).then_inc(bank_free[p.slot], 1)
                            dve.wait_ge(conv_mid, at("conv_mid", l, j + 1))
                            u, y = seg(cu[:, j % 2, :], l), seg(cy[:, j % 2, :], l)
                            steps.link(dve.scalar_tensor_tensor(
                                out=y[:, :, 1:C], in0=u[:, :, 0:C - 1], scalar=va[:, l, V_SC + j:V_SC + j + 1],
                                in1=y[:, :, 1:C], op0=ALU.mult, op1=ALU.add))
                            steps.link(dve.scalar_tensor_tensor(
                                out=y[:, :, 0:C - 1], in0=u[:, :, 1:C],
                                scalar=va[:, l, V_SC + 8 + j:V_SC + 9 + j], in1=y[:, :, 0:C - 1],
                                op0=ALU.mult, op1=ALU.add))
                        else:
                            dve.tensor_tensor(cy[:, j % 2, first:T], cy[:, j % 2, first:T], full(p)[:, first:T],
                                              ALU.mult).then_inc(bank_free[p.slot], 1)
                            dve.wait_ge(cat_hi, at("cat_hi", l, j + 1))
                            dve.tensor_tensor(alo[:, j, first:T], cy[:, j % 2, first:T],
                                              ahi[:, j, first:T].bitcast(F32), ALU.subtract).then_inc(cat_lo, 1)
                    if n == 4:
                        dve.wait_ge(c_std, at("c_std", l, 1))
                        steps.link(dve.reciprocal(R[:, first:T], R[:, first:T]))
                        dve.wait_ge(c_std, at("c_std", l, 2))
                        steps.link(dve.reciprocal(R2, R2))
                        for m in range(3):
                            f, r = (0, R2) if m == 2 else (first, R)
                            g = va[:, l, (V_KN if m == 2 else V_QN + m):(V_KN if m == 2 else V_QN + m) + 1]
                            dve.scalar_tensor_tensor(out=cf[:, m, f:T], in0=cf[:, m, f:T], scalar=g,
                                                     in1=r[:, f:T], op0=ALU.mult, op1=ALU.mult) \
                                .then_inc(c_norm, 1)
                    if 6 <= n <= 8:
                        f = 0 if n == 8 else first
                        dve.wait_ge(c_hi, at("c_hi", l, n - 5))
                        dve.tensor_tensor(clo[:, n - 6, f:T], cf[:, n - 6, f:T],
                                          chi[:, n - 6, f:T].bitcast(F32), ALU.subtract).then_inc(c_lo, 1)
                    if l == 0 and n % 2 == 0 and n > 0:
                        ada_in(0, 3 + n // 2, 3 + n // 2)
                if l == 0:
                    ada_in(0, 11, 11)
                    coefficients(0, 1, 12)
                dve.wait_ge(bank_free[3], ps[3].turn + 1)
                for e in range(2):
                    last = dve.tensor_copy(Kb[NOPE:QK, e, :], kr[NOPE:QK, :])
                last.then_inc(kr_dve, 1)
                nt = 4 if l == 0 else 2
                nb = 3 if l == 0 else 2

                def body(i, ps, after):
                    def heads(e):
                        return i * 2 + (e + 1)

                    def rotate(e):
                        dve.wait_ge(a_q, heads(e) + at("a_q", l, 0))
                        dve.wait_ge(q_act, heads(e) + at("q_act", l, 0))
                        dve.tensor_tensor(TA[NOPE:QK, 0, C:T], bank[4][QK:P, C:T], K[QK:P, K_ROPE:K_ROPE + C],
                                          ALU.mult)
                        steps.link(dve.tensor_tensor(Qb[NOPE:QK, e, C:T], bank[4][NOPE:QK, C:T],
                                                     K[NOPE:QK, K_ROPE:K_ROPE + C], ALU.mult))
                        dve.tensor_tensor(Qb[NOPE:QK, e, C:T], Qb[NOPE:QK, e, C:T], TA[NOPE:QK, 0, C:T],
                                          ALU.add).then_inc(q_dve, 1)

                    def softmax(e):
                        for t in range(nt):
                            if t < 3:
                                tiles = t + 1 if t < 2 else nt
                                dve.wait_ge(scored, i * (2 * nt) + (at("scored", l, 0) + e * nt + tiles))
                            src = bank[4 + t][:, :] if t < 2 else bank[7][:, (t - 2) * C:(t - 1) * C]
                            last = dve.reduce_max(mx[:, 0, t:t + 1], src, AX_X)
                        steps.link(last)
                        dve.tensor_scalar(mx[:, 1, 0:nt], mx[:, 0, 0:nt], -scale, None, ALU.mult) \
                            .then_inc(max_ready, 1)
                        dve.wait_ge(exped, i * (2 * nt) + (at("exped", l, 0) + (e + 1) * nt))
                        steps.link(dve.reciprocal(mx[:, 3, 0:nt], mx[:, 2, 0:nt]))
                        for t in range(nt):
                            pr = Pl[:, t, :] if t < 2 else Pc[:, t - 2, :]
                            dve.tensor_scalar(pr, pr, mx[:, 3, t:t + 1], None, ALU.mult).then_inc(p_ready, 1)

                    def values_out(e):
                        dve.wait_ge(p_turned, i * (2 * nb) + (at("p_turned", l, 0) + e * nb + 2))
                        if e == 1:
                            dve.wait_ge(o_done, i * 2 + at("o_done", l, 1))
                        dve.tensor_copy(Tl[:, 2:4, :], bank[5][:, :].rearrange("p (k n) -> p k n", k=2)) \
                            .then_inc(pt_dve, 1)

                    rotate(0)
                    split(ps[2])
                    softmax(0)
                    dve.wait_ge(bank_free[1], ps[1].turn + 1)
                    merge(ps[0], 0, i * 2, first, True)
                    split(ps[3])
                    rotate(1)
                    values_out(0)
                    softmax(1)
                    split(after[0])
                    dve.wait_ge(bank_free[3], ps[3].turn + 1)
                    merge(ps[2], 1, i * 2 + 1, first, True)
                    split(after[1])
                    values_out(1)
                    dve.wait_ge(cat_hi, i + (at("cat_hi", l, 4) + 1))
                    dve.tensor_tensor(flat(alo[:, bass.ds(i + 4, 1), first:T]), OF[:, first:T],
                                      flat(ahi[:, bass.ds(i + 4, 1), first:T]).bitcast(F32),
                                      ALU.subtract).then_inc(cat_lo, 1)

                turns, links = MH // 2, 6
                with dve.Fori(0, turns - 1) as i:
                    steps.enter(i, links)
                    body(i, st.body(i, MLA_BODY), st.body(i + 1, MLA_BODY))
                steps.leave(turns - 1)
                last_body = st.body(turns - 1, MLA_BODY)
                st.skip(turns, MLA_BODY)
                body(turns - 1, last_body, st.peek(GLA))

                ps = st.take(GLA)
                ahead = ps + st.peek(GATE_BODY)[0:AHEAD]
                n = 0
                dve.wait_ge(cat_lo, at("cat_lo", l, 8))
                for half in range(2):
                    r, o = slice(half * CHUNK, (half + 1) * CHUNK), slice((1 - half) * CHUNK, (2 - half) * CHUNK)
                    dve.memset(gA[r, :, o], 0.0)
                dve.memset(gS[0:DK, 0, :], 0.0)
                steps.link(dve.memset(gS[DK:P, NCH // 2 - 1, :], 0.0))
                chunk_pairs = slice(first // P, T // P)
                pairs = (T - first) // P
                for h in range(GH):
                    e = h % 2
                    if e == 0:
                        split(ahead[n + AHEAD])
                        split(ahead[n + 1 + AHEAD])
                        n += 2
                    split(ahead[n + AHEAD])
                    n += 1
                    dve.wait_ge(z_done, at("z_done", l, h + 1))
                    dve.wait_ge(z_ln, at("z_ln", l, h + 1))
                    if h > 0:
                        dve.wait_ge(g_turned, at("g_turned", l, 2 * h))
                    steps.link(dve.tensor_scalar(gx[:, :], bank[4][:, :], va[:, l, V_GK + h:V_GK + h + 1], 0.0,
                                                 ALU.add, ALU.min))
                    steps.link(dve.tensor_tensor(gx[:, :], gx[:, :], gE[:, :], ALU.subtract))
                    dve.tensor_tensor_scan(gst[0:DK, :], K[0:DK, K_SCAN:K_SCAN + T], gx[0:DK, :], 0.0,
                                           ALU.mult, ALU.add)
                    dve.tensor_tensor_scan(gst[DK:P, ::-1], K[DK:P, K_SCAN:K_SCAN + T][:, ::-1],
                                           gx[DK:P, ::-1], 0.0, ALU.mult, ALU.add).then_inc(b_ready, 1)
                    split(ahead[n + AHEAD])
                    dve.wait_ge(r_tanh, at("r_tanh", l, h + 1))
                    dve.scalar_tensor_tensor(out=gr[:, first:T], in0=gr[:, first:T], scalar=1.0,
                                             in1=full(ps[n])[:, first:T], op0=ALU.add, op1=ALU.mult) \
                        .then_inc(bank_free[ps[n].slot], 1)
                    n += 1
                    dve.wait_ge(e_ready, at("e_ready", l, h + 1))
                    if e == 0:
                        for m in (n - 4, n - 3):
                            dve.wait_ge(bank_free[ps[m].slot], ps[m].turn + 1)
                    steps.mark(dve.tensor_tensor(gq[:, e, first:T], gq[:, e, first:T], gE[:, first:T], ALU.mult))
                    dve.tensor_tensor(gk[:, e, :], gk[:, e, :], gx[:, :], ALU.mult).then_inc(qk_decayed, 1)
                    dve.wait_ge(qk_decayed, at("qk_decayed", l, h + 1))
                    for way in range(2):
                        r = slice(way * DK, (way + 1) * DK)
                        end = 0 if way else CHUNK - 1
                        ends = gE[r, :].rearrange("p (n i) -> p n i", i=CHUNK)[:, :, end:end + 1]
                        last = dve.tensor_tensor(gst[r, :].rearrange("p (n i) -> p n i", i=CHUNK),
                                                 gk[r, e, :].rearrange("p (n i) -> p n i", i=CHUNK),
                                                 ends.to_broadcast([DK, NCH, CHUNK]), ALU.mult)
                    last.then_inc(kst_ready, 1)
                    split(ahead[n + AHEAD])
                    gp = ps[n]
                    n += 1
                    split(ahead[n + AHEAD])
                    dve.wait_ge(bank_free[gp.slot], gp.turn + 1)
                    merge(ps[n], 0, 2 * h, first, False)
                    n += 1
                    dve.wait_ge(ga_done, at("ga_done", l, h + 1))
                    for way, mask in ((0, K_MF), (1, K_MB)):
                        src = bank[7 if way else 4][:, 0:C].rearrange("p (n i) -> p n i", i=CHUNK)
                        last = dve.tensor_tensor(
                            TA[:, way, 0:C].rearrange("p (n i) -> p n i", i=CHUNK)[:, chunk_pairs, :],
                            src[:, chunk_pairs, :],
                            K[:, mask:mask + CHUNK].unsqueeze(1).to_broadcast([P, pairs, CHUNK]), ALU.mult)
                    steps.link(last)
                    for half in range(2):
                        r = slice(half * CHUNK, (half + 1) * CHUNK)
                        t0, t1 = (TA[r, way, 0:C].rearrange("p (n i) -> p n i", i=CHUNK)[:, chunk_pairs, :]
                                  for way in range(2))
                        last = dve.tensor_tensor(gA[r, chunk_pairs, r], t0, t1, ALU.add)
                    last.then_inc(ga_masked, 1)
                    split(ahead[n + AHEAD])
                    gp = ps[n]
                    n += 1
                    split(ahead[n + AHEAD])
                    dve.wait_ge(gu_done, at("gu_done", l, 2 * h + 2))
                    orders = [scan_order(way) for way in range(2)]
                    for m in range(NCH - 1):
                        for way in range(2):
                            r = slice(way * DK, (way + 1) * DK)
                            a, b = orders[way][m], orders[way][m + 1]
                            col = a * CHUNK + (0 if way else CHUNK - 1)
                            last = dve.scalar_tensor_tensor(
                                out=gS[r, b, :], in0=gS[r, a, :], scalar=gE[r, col:col + 1],
                                in1=bank[4 + a % 2][r, (a // 2) * DV:(a // 2 + 1) * DV],
                                op0=ALU.mult, op1=ALU.add)
                        if m < NCH - 2:
                            steps.link(last)
                    last.then_inc(gs_ready, 1)
                    dve.wait_ge(bank_free[gp.slot], gp.turn + 1)
                    merge(ps[n], 1, 2 * h + 1, first, False)
                    n += 1
                    dve.wait_ge(g_std, at("g_std", l, h + 1))
                    steps.link(dve.reciprocal(R[:, first:T], R[:, first:T]))
                    steps.link(dve.scalar_tensor_tensor(
                        out=gE[:, first:T], in0=bank[6][:, first:T], scalar=va[:, l, V_GN + h:V_GN + h + 1],
                        in1=R[:, first:T], op0=ALU.mult, op1=ALU.mult))
                    dve.tensor_tensor(gE[:, first:T], gE[:, first:T], gr[:, first:T], ALU.mult) \
                        .then_inc(go_norm, 1)
                    dve.wait_ge(cat_hi, at("cat_hi", l, 8 + h + 1))
                    dve.scalar_tensor_tensor(out=alo[:, h, first:T], in0=gE[:, first:T], scalar=0.5,
                                             in1=ahi[:, h, first:T].bitcast(F32), op0=ALU.mult,
                                             op1=ALU.subtract).then_inc(cat_lo, 1)

                def gates(i, ps, after):
                    for e in range(2):
                        split((ps + after)[2 * e + 2])
                        split((ps + after)[2 * e + 3])
                        dve.wait_ge(bank_free[2 * e], ps[2 * e].turn + 1)
                        p = ps[2 * e + 1]
                        dst = flat(M[:, bass.ds(i * 2 + e, 1), first:T])
                        dve.scalar_tensor_tensor(out=TA[:, e, first:T], in0=TB[:, e, first:T], scalar=1.0,
                                                 in1=full(p)[:, first:T], op0=ALU.add, op1=ALU.mult) \
                            .then_inc(bank_free[p.slot], 1)
                        dve.wait_ge(bank_free[p.slot], p.turn + 1)
                        dve.tensor_tensor(dst, dst, TA[:, e, first:T], ALU.add).then_inc(m_ready, 1)

                turns = KD // 2
                with dve.Fori(0, turns - 1) as i:
                    gates(i, st.body(i, GATE_BODY), st.body(i + 1, GATE_BODY)[0:AHEAD])
                last_body = st.body(turns - 1, GATE_BODY)
                st.skip(turns, GATE_BODY)
                gates(turns - 1, last_body, st.peek(UP_BODY)[0:AHEAD])
                for k in range(KD):
                    dve.wait_ge(m_hi, 8 * l + k + 1)
                    dve.scalar_tensor_tensor(out=hlo[:, k, first:T], in0=M[:, k, first:T], scalar=0.5,
                                             in1=hhi[:, k, first:T].bitcast(F32), op0=ALU.mult,
                                             op1=ALU.subtract).then_inc(m_lo, 1)

                def residual_stage(kinds, g, after):
                    turns = KD // SLOTS
                    with dve.Fori(0, turns - 1) as i:
                        ahead = st.body(i, kinds)[AHEAD:] + st.body(i + 1, kinds)[0:AHEAD]
                        for n, p in enumerate(st.body(i, kinds)):
                            split(ahead[n])
                            residual(p, l, i * SLOTS + n, g)
                    ps = st.body(turns - 1, kinds)
                    st.skip(turns, kinds)
                    ahead = ps[AHEAD:] + (st.peek(after)[0:AHEAD] if after else [])
                    for n, p in enumerate(ps):
                        if n < len(ahead):
                            split(ahead[n])
                        residual(p, l, (turns - 1) * SLOTS + n, g)

                residual_stage(UP_BODY, G1, UP_BODY)
                norm(2 * l + 1, l, 1, first)
                for n, (off, tiles) in enumerate(parts(l)):
                    def hidden(i, ps, after):
                        for e in range(2):
                            pg, pu = ps[2 * e], ps[2 * e + 1]
                            split((ps + after)[2 * e + 2])
                            t = i * 2 + (off + e)
                            g, y = seg(full(pg)[:, :], l), seg(fy[:, e, :], l)
                            dve.wait_ge(f_mid, t + at("f_mid", l, 1))
                            steps.link(dve.scalar_tensor_tensor(
                                out=y[:, :, 1:C], in0=g[:, :, 0:C - 1], scalar=vb[:, l, bass.ds(t + V_FW, 1)],
                                in1=y[:, :, 1:C], op0=ALU.mult, op1=ALU.add))
                            dve.scalar_tensor_tensor(
                                out=y[:, :, 0:C - 1], in0=g[:, :, 1:C],
                                scalar=vb[:, l, bass.ds(t + (V_FW + 2 * KF), 1)], in1=y[:, :, 0:C - 1],
                                op0=ALU.mult, op1=ALU.add).then_inc(bank_free[pg.slot], 1)
                            split((ps + after)[2 * e + 3])
                            dve.wait_ge(f_silu, t + at("f_silu", l, 1))
                            dve.tensor_tensor(ff[:, e, first:T], fs[:, e, first:T], full(pu)[:, first:T],
                                              ALU.mult).then_inc(bank_free[pu.slot], 1)
                            dve.wait_ge(f_hi, t + at("f_hi", l, 1))
                            dve.tensor_tensor(flat(alo[:, bass.ds(i * 2 + e, 1), first:T]), ff[:, e, first:T],
                                              flat(ahi[:, bass.ds(i * 2 + e, 1), first:T]).bitcast(F32),
                                              ALU.subtract).then_inc(f_lo, 1)
                        if l == 0:
                            ada_in(1, i + off // 2, i + (12 + off // 2))

                    turns = tiles // 2
                    with dve.Fori(0, turns - 1) as i:
                        steps.enter(i, 2)
                        hidden(i, st.body(i, UP_BODY), st.body(i + 1, UP_BODY)[0:AHEAD])
                    steps.leave(turns - 1)
                    last_body = st.body(turns - 1, UP_BODY)
                    st.skip(turns, UP_BODY)
                    hidden(turns - 1, last_body, st.peek(down_body(n))[0:AHEAD])
                    final = l == L - 1 and n + 1 == len(FF_PARTS)
                    residual_stage(down_body(n), G2,
                                   None if final else UP_BODY if n + 1 < len(FF_PARTS) else PROJ)
                if l == 0:
                    ada_in(1, 11, 23)
                    coefficients(1, 0, 24)
                    coefficients(1, 1, 24)
            norm(2 * L, None, None, C)
            for q in range(2):
                dve.wait_ge(fin_t, 2 * q + 1)
                dve.tensor_copy(Z[:, q * 512:(q + 1) * 512], bank[q][:, :]).then_inc(fin_v, 1)


def constants():
    k = np.zeros((P, K_ALL), np.float32)
    k[:, K_ID:K_ID + P] = np.eye(P)
    j, i = np.arange(P)[:, None] % CHUNK, np.arange(CHUNK)[None, :]
    k[:, K_MF:K_MF + CHUNK] = j <= i
    k[:, K_MB:K_MB + CHUNK] = j >= i
    t = np.arange(T)
    k[0:DK, K_SCAN:K_SCAN + T] = t % CHUNK != 0
    k[DK:P, K_SCAN:K_SCAN + T] = t % CHUNK != CHUNK - 1
    freqs = ROPE // 4
    inv = (10000.0 ** (-np.arange(freqs, dtype=np.float32) / freqs)).astype(np.float32)
    pos = [np.arange(C) // GRID_W, np.arange(C) % GRID_W]
    for axis in range(2):
        ang = (pos[axis][None, :].astype(np.float32) * inv[:, None]).astype(np.float32)
        for half in range(2):
            r = axis * 2 * freqs + half * freqs
            k[NOPE + r:NOPE + r + freqs, K_ROPE:K_ROPE + C] = np.cos(ang)
            k[QK + r:QK + r + freqs, K_ROPE:K_ROPE + C] = np.sin(ang) * (1 if half else -1)
    return k


_INS = ["x", "c", "ctx", "c_ctx", "w_ada", "b_ada", "norm1_g", "w_in", "w_gk2", "b_gk2", "gla_norm_g",
        "mla_q_norm_g", "w_uq", "mla_kv_norm_g", "w_ukv", "sc_w", "w_br_a", "w_br_b", "w_br_c", "w_o",
        "norm2_g", "w_ffn_gate", "w_ffn_up", "ffn_conv_w", "ffn_conv_b", "w_ffn_down", "final_norm_g"]


def kernel(**inputs):
    import concourse.bacc as bacc
    from concourse.bass_utils import run_bass_kernel_spmd

    nc = bacc.Bacc("TRN2", target_bir_lowering=False, num_devices=1)
    arrays, args = {}, []
    for name in _INS + ["consts"]:
        a = constants() if name == "consts" else np.ascontiguousarray(inputs[name])
        arrays[f"in_{name}"] = a
        args.append(nc.dram_tensor(f"in_{name}", a.shape, F32, kind="ExternalInput").ap())
    args.append(nc.dram_tensor("out_0", (1, C, D), F32, kind="ExternalOutput").ap())
    build(nc, *args)
    r = run_bass_kernel_spmd(nc, [arrays], core_ids=[0])
    return r.results[0]["out_0"]
```

```python
from contextlib import ExitStack

import numpy as np

import concourse.bass as bass
from concourse import mybir

F32 = mybir.dt.float32
F32R = mybir.dt.float32r
ALU = mybir.AluOpType
ACT = mybir.ActivationFunctionType
AX_X = mybir.AxisListType.X

P = 128
D = 1024
KD = D // P
C = 256
T = 2 * C
L = 2
GRID_W = 64
EPS = 1e-6
GH, DK, DV, RANK, CHUNK = 4, 64, 128, 16, 64
NCH = T // CHUNK
GATE_NORM = 16.0
MH, NOPE, ROPE, MDV = 8, 64, 32, 64
QK = NOPE + ROPE
QLORA, KVLORA = 256, 128
SCW = 512
FF = 2816
KF = FF // P
FF_PARTS = [8, 8, 6]
SLOTS = 4
AHEAD = 2
ADA_SLOTS = 4
ADA_CHUNK = 512
ADA_TURNS = 6 * D // ADA_CHUNK
ADA_FIRST = 4
O_Q, O_K, O_V, O_R, O_LR = 0, 256, 512, 1024, 1536
O_CQ = O_LR + 2 * RANK
O_CKV = O_CQ + QLORA
O_KR = O_CKV + KVLORA
O_SB = O_KR + ROPE
O_SC, O_SX = O_SB + SCW, O_SB + 2 * SCW
O_G = O_SX + SCW
BR_A, BR_B, BR_C = 0, 1, 2
V_ADA, V_N1, V_N2, V_GN, V_QN, V_KN, V_SC, V_GK = 0, 48, 56, 64, 68, 70, 71, 83
VA = 87
V_FW, V_FB = 0, 3 * KF
VB = 4 * KF
VC_FIN, VC_CTX, VC_LAT = 0, 8, 16
VC = 24
SH1, SC1, G1, SH2, SC2, G2 = (8 * m for m in range(6))
K_ID, K_MF, K_MB, K_SCAN, K_ROPE = 0, 128, 192, 256, 768
K_ALL = 1024

PROJ = [(8, 1)] * 3 + [(8, 7)] + [(8, 1)] * 12
MLA_BODY = [(7, 7), (8, 1), (7, 7), (8, 1)]
HEAD_PANELS = [(8, 1), (8, 1), (8, 1), (4, 1), (8, 1), (4, 1)]
GLA = ([(8, 1)] * 2 + HEAD_PANELS * 2) * 2
GATE_BODY = [(8, 1), (4, 1)] * 2
WO = [(8, 1)] * 8
UP_BODY = [(8, 1)] * 4
VEC_DMAS = L * 11 + 3


def down_body(part):
    return [(FF_PARTS[part], 1)] * 4


class Panel:

    def __init__(self, slot, turn, loaded, nk, dmas):
        self.slot, self.turn, self.loaded, self.nk, self.dmas = slot, turn, loaded, nk, dmas


class Stream:

    def __init__(self):
        self.turns, self.loaded, self.at = [0] * SLOTS, [0] * SLOTS, 0

    def take(self, kinds):
        out = []
        for nk, dmas in kinds:
            s = self.at % SLOTS
            self.loaded[s] += 16 * dmas
            out.append(Panel(s, self.turns[s], self.loaded[s], nk, dmas))
            self.turns[s] += 1
            self.at += 1
        return out

    def peek(self, kinds):
        keep = list(self.turns), list(self.loaded), self.at
        out = self.take(kinds)
        self.turns, self.loaded, self.at = keep
        return out

    def body(self, i, kinds):
        assert self.at % SLOTS == 0 and len(kinds) == SLOTS
        return [Panel(s, i + self.turns[s], i * (16 * d) + (self.loaded[s] + 16 * d), nk, d)
                for s, (nk, d) in enumerate(kinds)]

    def skip(self, n, kinds):
        for _ in range(n):
            self.take(kinds)


class Steps:

    def __init__(self, eng, sem):
        self.eng, self.sem, self.base, self.n = eng, sem, 0, 0

    def link(self, ins):
        self.mark(ins)
        self.wait()

    def mark(self, ins):
        ins.then_inc(self.sem, 1)
        self.n += 1

    def wait(self, back=0):
        self.eng.wait_ge(self.sem, self.base + (self.n - back))

    def enter(self, i, per):
        self.kept, self.per, self.base = self.n, per, i * per

    def leave(self, turns):
        assert self.n - self.kept == self.per, self.n - self.kept
        self.base, self.n = 0, self.kept + self.per * turns


def build(nc, x, c, ctx, c_ctx, w_ada, b_ada, norm1_g, w_in, w_gk2, b_gk2, gla_norm_g, mla_q_norm_g,
          w_uq, mla_kv_norm_g, w_ukv, sc_w, w_br_a, w_br_b, w_br_c, w_o, norm2_g, w_ffn_gate,
          w_ffn_up, ffn_conv_w, ffn_conv_b, w_ffn_down, final_norm_g, consts, out):
    w_br = [w_br_a, w_br_b, w_br_c]

    with ExitStack() as stack:
        def sb(name, shape, dt=F32):
            return stack.enter_context(nc.sbuf_tensor(name, shape, dt))

        def sem(name):
            return stack.enter_context(nc.semaphore(name))

        def sems(name, n):
            return [sem(f"{name}{i}") for i in range(n)]

        bank = [stack.enter_context(nc.psum_tensor(f"bank{i}", [P, 512], F32)) for i in range(8)]

        raw = sb("raw", [P, SLOTS, 8, P])
        whi = sb("whi", [P, SLOTS, 8, P], F32R)
        wlo = sb("wlo", [P, SLOTS, 8, P], F32R)
        X = sb("X", [P, KD, T])
        hhi = sb("hhi", [P, KD, T], F32R)
        hlo = sb("hlo", [P, KD, T], F32R)
        M = sb("M", [P, KD, T])
        ahi = sb("ahi", [P, 8, T], F32R)
        alo = sb("alo", [P, 8, T], F32R)
        chi = sb("chi", [P, 3, T], F32R)
        clo = sb("clo", [P, 3, T], F32R)
        TA = sb("TA", [P, 2, T])
        TB = sb("TB", [P, 2, T])
        R = sb("R", [P, T])
        K = sb("K", [P, K_ALL])
        ones = sb("ones", [P, P])
        eps = sb("eps", [P, 1])
        va = sb("va", [P, L, VA])
        vb = sb("vb", [P, L, VB])
        vc = sb("vc", [P, VC])
        cs = sb("cs", [P, KD, 2])
        csr = sb("csr", [P, KD, 4], F32R)
        mod = sb("mod", [P, L, 48, 2])
        am = sb("am", [P, L, 2, KD, 2])
        Z = sb("Z", [P, 7680])
        W2 = sb("W2", [2 * RANK, GH, P])

        vec_in = [TB[:, :, :].rearrange("p a n -> p (a n)")[:, n * P:(n + 1) * P] for n in range(5)]
        vec_rows = [VA, VA, VB, VB, VC]


        def zv(at, *shape):
            n = int(np.prod(shape))
            v = Z[:, at:at + n]
            if len(shape) == 2:
                v = v.rearrange("p (a b) -> p a b", a=shape[0])
            if len(shape) == 3:
                v = v.rearrange("p (a b c) -> p a b c", a=shape[0], b=shape[1])
            return v

        LR = Z[0:2 * RANK, 0:T]
        z0 = T
        adaw = zv(z0, ADA_SLOTS, ADA_CHUNK)
        adarow = Z[0:4, z0 + 2048:z0 + 2560]
        ada_half = [zv(z0 + at, ADA_SLOTS, ADA_CHUNK) for at in (0, 2560, 4608)]
        cf = zv(z0 + 2560, 3, T)
        R2 = zv(z0 + 4096, T)
        cu = zv(z0 + 4608, 2, T)
        cy = zv(z0 + 5632, 2, T)
        kr = zv(z0 + 6656, T)
        assert z0 + 7168 <= 7680
        hf = zv(z0 + 2560, KD, T)
        fy, fs = cu, cy
        ff = zv(z0 + 2560, 2, T)
        Kb = zv(z0, 2, T)
        Qb = zv(z0 + 1024, 2, T)
        vT = zv(z0 + 2048, T)
        Vm = zv(z0 + 2560, 2, 4, MDV)
        Pc = zv(z0 + 3072, 2, C)
        Pl = zv(z0 + 3584, 2, T)
        Tc = zv(z0 + 4608, 2, C)
        Tl = zv(z0 + 5120, 4, C)
        OF = zv(z0 + 6144, T)
        mx = zv(z0 + 6656, 4, 4)
        gq = zv(z0, 2, T)
        gk = zv(z0 + 1024, 2, T)
        gV = zv(z0 + 2048, 4, DV)
        gvT = zv(z0 + 2560, T)
        gr = zv(z0 + 3072, T)
        gx = zv(z0 + 3584, T)
        gE = zv(z0 + 4096, T)
        gst = zv(z0 + 4608, T)
        gKT = zv(z0 + 5120, 4, P)
        gA = zv(z0 + 5632, 4, P)
        gS = zv(z0 + 6144, NCH, DV)
        assert z0 + 6144 + NCH * DV <= 7680

        scale = float(QK) ** -0.5

        raw_loaded = sems("raw_loaded", SLOTS)
        hi_ready = sems("hi_ready", SLOTS)
        lo_ready = sems("lo_ready", SLOTS)
        panel_done = sems("panel_done", SLOTS)
        bank_free = sems("bank_free", SLOTS)
        ada_first = sems("ada_first", 3)
        ada_loaded = sems("ada_loaded", ADA_SLOTS)
        c_hi_ready = sem("c_hi_ready")
        c_lo_ready = sem("c_lo_ready")
        ada_hi = sem("ada_hi")
        ada_lo = sem("ada_lo")
        ada_sum = sem("ada_sum")
        ada_used = sem("ada_used")
        ada_row = sem("ada_row")
        ada_cols = sem("ada_cols")
        ada_mod = sem("ada_mod")
        consts_in = sem("consts_in")
        vecs_in = sem("vecs_in")
        tokens_in = sem("tokens_in")
        w2_zero = sem("w2_zero")
        w2_in = sem("w2_in")
        start_t = sem("start_t")
        start_c = sem("start_c")
        fin_t = sem("fin_t")
        fin_a = sem("fin_a")
        fin_v = sem("fin_v")
        stored = sem("stored")
        act_step = sem("act_step")
        dve_step = sem("dve_step")
        x_ready = sem("x_ready")
        sq_ready = sem("sq_ready")
        sum_ready = sem("sum_ready")
        stat_ready = sem("stat_ready")
        rms_ready = sem("rms_ready")
        t_ready = sem("t_ready")
        hf_hi = sem("hf_hi")
        hf_full = sem("hf_full")
        h_ready = sem("h_ready")
        coef = sem("coef")
        m_ready = sem("m_ready")
        m_hi = sem("m_hi")
        m_lo = sem("m_lo")

        per_layer = {}

        def event(name, context_layer, last_layer=None):
            per_layer[name] = context_layer
            return sem(name)

        cf_ready = event("cf_ready", 3)
        cf_sq = event("cf_sq", 3)
        c_stat = event("c_stat", 2)
        c_rms = event("c_rms", 2)
        c_norm = event("c_norm", 3)
        c_hi = event("c_hi", 3)
        c_lo = event("c_lo", 3)
        kr_act = event("kr_act", 1)
        kr_dve = event("kr_dve", 1)
        conv_mid = event("conv_mid", 4)
        cat_hi = event("cat_hi", 12)
        cat_lo = event("cat_lo", 12)
        a_q = event("a_q", MH)
        a_kv = event("a_kv", MH)
        q_act = event("q_act", MH)
        q_dve = event("q_dve", MH)
        k_act = event("k_act", MH)
        v_turned = event("v_turned", MH)
        v_act = event("v_act", MH)
        scored = event("scored", 4 * MH)
        max_ready = event("max_ready", MH)
        exped = event("exped", 4 * MH)
        p_ready = event("p_ready", 4 * MH)
        p_turned = event("p_turned", 3 * MH)
        pt_act = event("pt_act", 2 * MH)
        pt_dve = event("pt_dve", MH)
        o_done = event("o_done", MH)
        o_act = event("o_act", MH)
        z_done = event("z_done", GH)
        z_ln = event("z_ln", GH)
        z_read = event("z_read", GH)
        b_ready = event("b_ready", GH)
        e_ready = event("e_ready", GH)
        qk_decayed = event("qk_decayed", GH)
        kst_ready = event("kst_ready", GH)
        g_turned = event("g_turned", 2 * GH)
        g_turned_act = event("g_turned_act", 2 * GH)
        ga_done = event("ga_done", GH)
        ga_masked = event("ga_masked", GH)
        gu_done = event("gu_done", 2 * GH)
        gs_ready = event("gs_ready", GH)
        go_done = event("go_done", GH)
        go_sq = event("go_sq", GH)
        g_stat = event("g_stat", GH)
        g_rms = event("g_rms", GH)
        r_tanh = event("r_tanh", GH)
        go_norm = event("go_norm", GH)
        f_mid = event("f_mid", KF)
        f_silu = event("f_silu", KF)
        f_hi = event("f_hi", KF)
        f_lo = event("f_lo", KF)

        def at(name, l, value):
            return value + per_layer[name] * l

        def ada_units(l, n):
            if l == 0 and n >= 0:
                return [(ADA_FIRST + n // 2, k) for k in range(4 * (n % 2), 4 * (n % 2) + 4)]
            return [(2 * ADA_TURNS - 1, k) for k in range(4 * (n - 8), 4 * (n - 8) + 4)] if n in (8, 9) else []

        def chunk_of(turn):
            return turn // ADA_TURNS, turn % ADA_TURNS

        def ada_tiles(k, stage):
            if stage == "first":
                return ahi[:, k, :], alo[:, k, :]
            if stage == "projection":
                return ahi[:, 4 + k % 4, :], alo[:, 4 + k % 4, :]
            return chi[:, k % 3, :], clo[:, k % 3, :]

        def ada_before(k, stage):
            if stage == "first":
                return KD
            if stage == "projection":
                return 4
            return 3 if k >= 3 else 2 if k < 2 else 5

        block = stack.enter_context(nc.Block())

        def q0(l):
            return 0 if l < L - 1 else C

        def streams(l):
            return [0, 1] if l < L - 1 else [1]

        def cols(st):
            return slice(C * st, C * st + C)

        def seg(ap, l):
            return ap.rearrange("p (s n) -> p s n", n=C)[:, q0(l) // C:, :]

        def flat(ap):
            return ap.rearrange("p a n -> p (a n)")

        def scan_order(back):
            if not back:
                return list(range(NCH))
            h = NCH // 2
            return list(range(h - 1, -1, -1)) + list(range(NCH - 1, h - 1, -1))

        def parts(l):
            return [(sum(FF_PARTS[:n]), FF_PARTS[n]) for n in range(len(FF_PARTS))]

        @block.sync
        def _(sp):
            st = Stream()

            def slot_of(p):
                if not (isinstance(p.turn, int) and p.turn == 0):
                    sp.wait_ge(lo_ready[p.slot], p.turn)
                return raw[:, p.slot]

            def load(p, src):
                sp.dma_start(slot_of(p)[:, 0:p.nk, :], src.rearrange("(k p) n -> p k n", p=P)) \
                    .then_inc(raw_loaded[p.slot], 16)

            def load_ada(l, chunk, k, turn):
                slot = k % ADA_SLOTS
                sp.wait_ge(ada_lo, turn * KD + (k - ADA_SLOTS + 1))
                sp.dma_start(adaw[:, slot, :],
                             w_ada[l, k * P:(k + 1) * P, bass.ds(chunk * ADA_CHUNK, ADA_CHUNK)]) \
                    .then_inc(ada_loaded[slot], 16)

            def swapped(dst, src, sem_):
                for half in range(2):
                    for axis in range(2):
                        to, fro = axis * 16 + half * 8, axis * 16 + (1 - half) * 8
                        sp.dma_start(dst[:, :, to:to + 8], src[:, :, fro:fro + 8]).then_inc(sem_, 16)

            sp.dma_start(K[:, :], consts).then_inc(consts_in, 16)
            tok = flat(M[:, :, :]).rearrange("p (t d) -> p t d", t=4)
            sp.dma_start(tok[:, 0:2, :], ctx[0].rearrange("(t p) d -> p t d", p=P)).then_inc(tokens_in, 16)
            sp.dma_start(tok[:, 2:4, :], x[0].rearrange("(t p) d -> p t d", p=P)).then_inc(tokens_in, 16)
            n = 0
            for l in range(L):
                va_rows, vb_rows = vec_in[l], vec_in[2 + l]
                for rows, src in ((V_ADA, b_ada[l]), (V_N1, norm1_g[l]), (V_N2, norm2_g[l]),
                                  (V_GN, gla_norm_g[l]), (V_QN, mla_q_norm_g[l]),
                                  (V_KN, mla_kv_norm_g[l]), (V_SC, sc_w[l].rearrange("a b -> (a b)"))):
                    src = src.rearrange("(a b) -> a b", b=P)
                    sp.dma_start(va_rows[rows:rows + src.shape[0], :], src).then_inc(vecs_in, 16)
                    n += 1
                for way in range(2):
                    sp.dma_start(va_rows[V_GK:V_GK + GH, way * DK:(way + 1) * DK],
                                 b_gk2[l, way].rearrange("(h k) -> h k", h=GH)).then_inc(vecs_in, 16)
                    n += 1
                for rows, src in ((V_FW, ffn_conv_w[l].rearrange("a b -> (a b)")), (V_FB, ffn_conv_b[l])):
                    src = src.rearrange("(a b) -> a b", b=P)
                    sp.dma_start(vb_rows[rows:rows + src.shape[0], :], src).then_inc(vecs_in, 16)
                    n += 1
            for rows, src in ((VC_FIN, final_norm_g), (VC_CTX, c_ctx), (VC_LAT, c[0])):
                sp.dma_start(vec_in[4][rows:rows + KD, :], src.rearrange("(a b) -> a b", b=P)) \
                    .then_inc(vecs_in, 16)
                n += 1
            assert n == VEC_DMAS

            def load_w2(l):
                if l == 0:
                    sp.wait_ge(w2_zero, 1)
                else:
                    sp.wait_ge(z_done, at("z_done", l, 0))
                for way in range(2):
                    sp.dma_start(W2[way * RANK:(way + 1) * RANK, :, way * DK:(way + 1) * DK],
                                 w_gk2[l, way].rearrange("r (h k) -> r h k", h=GH)).then_inc(w2_in, 16)

            for n in range(2 * ADA_FIRST):
                if n >= 3:
                    sp.wait_ge(ada_lo, 4 * (n - 3) + 4)
                k = 4 * (n % 2)
                sp.dma_start(ada_half[n % 3],
                             w_ada[0, k * P:(k + 4) * P, n // 2 * ADA_CHUNK:(n // 2 + 1) * ADA_CHUNK]
                             .rearrange("(k p) n -> p k n", p=P)).then_inc(ada_first[n % 3], 16)
            load_w2(0)

            for l in range(L):
                starts = [O_CQ, O_CQ + P, O_CKV, None]
                for j in range(4):
                    starts += [O_SC + j * P, O_SX + j * P, O_SB + j * P]
                ps = st.take(PROJ)
                for n, p in enumerate(ps):
                    if n >= SLOTS:
                        for turn, k in ada_units(l, n - SLOTS):
                            load_ada(*chunk_of(turn), k, turn)
                    if starts[n] is not None:
                        load(p, w_in[l][:, starts[n]:starts[n] + P])
                    else:
                        dst = slot_of(p)
                        w = w_in[l].rearrange("(k p) n -> p k n", p=P)
                        sp.dma_start(dst[:, :, 0:ROPE], w[:, :, O_LR:O_LR + 2 * RANK]) \
                            .then_inc(raw_loaded[p.slot], 16)
                        sp.dma_start(dst[:, :, ROPE:2 * ROPE], w[:, :, O_KR:O_KR + ROPE]) \
                            .then_inc(raw_loaded[p.slot], 16)
                        sp.dma_start(dst[:, :, 2 * ROPE:3 * ROPE], w[:, :, O_KR:O_KR + ROPE]) \
                            .then_inc(raw_loaded[p.slot], 16)
                        swapped(dst[:, :, 3 * ROPE:], w[:, :, O_KR:O_KR + ROPE], raw_loaded[p.slot])
                for n in range(len(ps) - SLOTS, len(ps)):
                    for turn, k in ada_units(l, n):
                        load_ada(*chunk_of(turn), k, turn)
                with sp.Fori(0, MH // 2) as i:
                    for p in st.body(i, MLA_BODY):
                        h = i * 2 + p.slot // 2
                        if p.slot % 2 == 0:
                            wc = w_br_c[l][:, bass.ds(h * P, P)].rearrange("(k p) n -> p k n", p=P)
                            wq = w_uq[l].rearrange("(k p) n -> p k n", p=P)
                            wr = wq[:, :, bass.ds(h * QK + NOPE, ROPE)]
                            wq = wq[:, :, bass.ds(h * QK, QK)]
                            wkv = w_ukv[l][:, bass.ds(h * P, P)]
                            dst = slot_of(p)
                            for part, src in ((dst[:, 0:4, :], wc), (dst[:, 4:6, 0:QK], wq), (dst[:, 6, :], wkv)):
                                sp.dma_start(part, src).then_inc(raw_loaded[p.slot], 16)
                            swapped(dst[:, 4:6, QK:P], wr, raw_loaded[p.slot])
                        else:
                            load(p, w_in[l][:, bass.ds(h * P + (O_G + BR_C * D), P)])
                st.skip(MH // 2, MLA_BODY)
                if l > 0:
                    load_w2(l)
                ps = iter(st.take(GLA))
                for h in range(GH):
                    if h % 2 == 0:
                        load(next(ps), w_in[l][:, O_Q + h * DK:O_Q + h * DK + P])
                        load(next(ps), w_in[l][:, O_K + h * DK:O_K + h * DK + P])
                    load(next(ps), w_in[l][:, O_V + h * DV:O_V + h * DV + P])
                    load(next(ps), w_in[l][:, O_R + h * DV:O_R + h * DV + P])
                    for j in (2 * h, 2 * h + 1):
                        load(next(ps), w_in[l][:, O_G + BR_B * D + j * P:O_G + BR_B * D + (j + 1) * P])
                        load(next(ps), w_br_b[l][:, j * P:(j + 1) * P])
                with sp.Fori(0, KD // 2) as i:
                    for p in st.body(i, GATE_BODY):
                        j = i * 2 + p.slot // 2
                        if p.slot % 2 == 0:
                            load(p, w_in[l][:, bass.ds(i * (2 * P) + (p.slot // 2 * P + O_G + BR_A * D), P)])
                        else:
                            load(p, w_br_a[l][:, bass.ds(j * P, P)])
                st.skip(KD // 2, GATE_BODY)
                with sp.Fori(0, KD // SLOTS) as i:
                    for p in st.body(i, UP_BODY):
                        load(p, w_o[l][:, bass.ds(i * (SLOTS * P) + p.slot * P, P)])
                st.skip(KD // SLOTS, UP_BODY)
                for n, (off, tiles) in enumerate(parts(l)):
                    with sp.Fori(0, tiles // 2) as i:
                        for p in st.body(i, UP_BODY):
                            w = w_ffn_gate if p.slot % 2 == 0 else w_ffn_up
                            load(p, w[l][:, bass.ds(i * (2 * P) + (off + p.slot // 2) * P, P)])
                        if l == 0:
                            for k in range(KD):
                                load_ada(1, i + off // 2, k, i + (12 + off // 2))
                    st.skip(tiles // 2, UP_BODY)
                    with sp.Fori(0, KD // SLOTS) as i:
                        for p in st.body(i, down_body(n)):
                            load(p, w_ffn_down[l][off * P:(off + tiles) * P,
                                                  bass.ds(i * (SLOTS * P) + p.slot * P, P)])
                    st.skip(KD // SLOTS, down_body(n))
            for t in range(2):
                sp.wait_ge(fin_a if t else fin_v, 2)
                sp.dma_start(out[0, t * P:(t + 1) * P, :], Z[:, t * D:(t + 1) * D]).then_inc(stored, 16)
            sp.wait_ge(stored, 32)

        @block.tensor
        def _(pe):
            st = Stream()
            ident = K[:, K_ID:K_ID + P]

            def weights(p):
                pe.wait_ge(lo_ready[p.slot], p.turn + 1)

            def bank_of(p):
                if not (isinstance(p.turn, int) and p.turn == 0):
                    pe.wait_ge(bank_free[p.slot], p.turn)
                return bank[p.slot]

            def mm3(dst, p, ks, rhi, rlo, before=None):
                for n, k in enumerate(ks):
                    if before is not None:
                        before(n)
                    hi, lo = whi[:, p.slot, k, :], wlo[:, p.slot, k, :]
                    pe.matmul(dst, hi, rlo(n), start=(n == 0), stop=False)
                    pe.matmul(dst, hi, rhi(n), start=False, stop=False)
                    last = pe.matmul(dst, lo, rhi(n), start=False, stop=(n == len(ks) - 1))
                return last

            def project(p, first, before=None):
                weights(p)
                mm3(bank_of(p)[:, first:T], p, range(KD), lambda k: hhi[:, k, first:T],
                    lambda k: hlo[:, k, first:T], before).then_inc(panel_done[p.slot], 1)

            def project_pair(pair, first, before):
                for p in pair:
                    weights(p)
                dst = [bank_of(p)[:, first:T] for p in pair]
                for k in range(KD):
                    before(k)
                    for p, d in zip(pair, dst):
                        hi, lo = whi[:, p.slot, k, :], wlo[:, p.slot, k, :]
                        pe.matmul(d, hi, hhi[:, k, first:T], start=(k == 0), stop=False)
                        pe.matmul(d, lo, hhi[:, k, first:T], start=False, stop=False)
                        last = pe.matmul(d, hi, hlo[:, k, first:T], start=False, stop=(k == KD - 1))
                        if k == KD - 1:
                            last.then_inc(panel_done[p.slot], 1)

            def branch(p, tile0, first):
                weights(p)
                mm3(bank_of(p)[:, first:T], p, range(4), lambda k: ahi[:, tile0 + k, first:T],
                    lambda k: alo[:, tile0 + k, first:T]).then_inc(panel_done[p.slot], 1)

            def ada_unit(k, turn, stage):
                if k == 0:
                    if not (isinstance(turn, int) and turn == 0):
                        pe.wait_ge(ada_row, turn)
                pe.wait_ge(ada_lo, turn * KD + (k + 1))
                hi, lo = ada_tiles(k, stage)
                pe.matmul(bank[7][0:4, :], csr[:, k, :], hi, start=(k == 0), stop=False)
                pe.matmul(bank[7][0:4, :], csr[:, k, :], lo, start=False, stop=(k == KD - 1)) \
                    .then_inc(ada_used, 1)

            def ada_wait(turn):
                pe.wait_ge(ada_row, turn + 1)
                if not (isinstance(turn, int) and turn == 0):
                    pe.wait_ge(ada_mod, turn)

            def ada_turn(turn):
                for m in range(4):
                    last = pe.transpose(bank[6][:, 4 * m:4 * m + 4], adarow[:, m * P:(m + 1) * P],
                                        ident[0:4, 0:4])
                last.then_inc(ada_cols, 1)

            def norm_stat(m, first):
                pe.wait_ge(sum_ready, m + 1)
                pe.matmul(bank[4][:, first:T], ones[:, :], M[:, 0, first:T], start=True, stop=True) \
                    .then_inc(stat_ready, 1)

            pe.wait_ge(consts_in, 16)
            pe.wait_ge(vecs_in, 16 * VEC_DMAS)
            for n, rows in enumerate(vec_rows):
                last = pe.transpose(bank[5][:, n * 96:n * 96 + rows], vec_in[n][0:rows, :],
                                    ident[0:rows, 0:rows])
            last.then_inc(start_t, 1)
            pe.wait_ge(tokens_in, 32)
            tok = flat(M[:, :, :]).rearrange("p (t d) -> p t d", t=4)
            for k in range(KD):
                if k >= 4:
                    pe.wait_ge(x_ready, k - 3)
                for t in range(4):
                    last = pe.transpose(bank[k % 4][:, t * P:(t + 1) * P], tok[:, t, k * P:(k + 1) * P],
                                        ident)
                last.then_inc(start_t, 1)
            pe.wait_ge(c_lo_ready, 1)
            for turn in range(ADA_FIRST):
                for k in range(KD):
                    ada_unit(k, turn, "first")
                ada_wait(turn)
                ada_turn(turn)

            for l in range(L):
                first = q0(l)
                norm_stat(2 * l, 0)
                ps = st.take(PROJ)
                for n, p in enumerate(ps):
                    if n == 0:
                        project_pair(ps[0:2], first, lambda k: pe.wait_ge(h_ready, 8 * 2 * l + k + 1))
                    elif n > 1:
                        project(p, 0 if n in (2, 3) else first)
                    if n == 4:
                        pe.wait_ge(cf_sq, at("cf_sq", l, 3))
                        pe.matmul(bank[4][:, first:T], ones[:, :], cy[:, 0, first:T], start=True, stop=False)
                        pe.matmul(bank[4][:, first:T], ones[:, :], cy[:, 1, first:T], start=False, stop=True) \
                            .then_inc(c_stat, 1)
                        pe.matmul(bank[5][:, :], ones[:, :], cu[:, 0, :], start=True, stop=True) \
                            .then_inc(c_stat, 1)
                    if ada_units(l, n - 1) and n % 2 == 0:
                        turn = ada_units(l, n - 1)[0][0]
                        ada_wait(turn)
                        ada_turn(turn)
                    for turn, k in ada_units(l, n):
                        ada_unit(k, turn, "projection")
                if l == 0:
                    ada_wait(ADA_TURNS - 1)
                    ada_turn(ADA_TURNS - 1)
                pe.wait_ge(c_lo, at("c_lo", l, 3))
                pe.wait_ge(kr_dve, at("kr_dve", l, 1))
                pe.wait_ge(cat_lo, at("cat_lo", l, 4))
                nt = 4 if l == 0 else 2
                nb = 3 if l == 0 else 2
                with pe.Fori(0, MH // 2) as i:
                    ps = st.body(i, MLA_BODY)

                    def heads(e):
                        return i * 2 + (e + 1)

                    def project_head(e):
                        p = ps[2 * e]
                        weights(p)
                        mm3(bank[4][:, first:T], p, (4, 5), lambda k: chi[:, k, first:T],
                            lambda k: clo[:, k, first:T]).then_inc(a_q, 1)
                        mm3(bank[5][:, :], p, (6,), lambda k: chi[:, 2, :], lambda k: clo[:, 2, :]) \
                            .then_inc(a_kv, 1)

                    def score(e):
                        pe.wait_ge(k_act, heads(e) + at("k_act", l, 0))
                        pe.wait_ge(q_act, heads(e) + at("q_act", l, 0))
                        pe.wait_ge(q_dve, heads(e) + at("q_dve", l, 0))
                        if e == 0:
                            pe.wait_ge(cat_hi, i + at("cat_hi", l, 4))
                        else:
                            pe.wait_ge(o_act, i * 2 + at("o_act", l, 1))
                        for t in range(2):
                            pe.matmul(bank[4 + t][:, :], Qb[0:QK, e, C + t * P:C + (t + 1) * P], Kb[0:QK, e, :],
                                      start=True, stop=True).then_inc(scored, 1)
                        if l == 0:
                            for t in range(2):
                                pe.matmul(bank[7][:, t * C:(t + 1) * C], Qb[0:QK, e, t * P:(t + 1) * P],
                                          Kb[0:QK, e, 0:C], start=True, stop=True).then_inc(scored, 1)
                        for t in range(4):
                            last = pe.transpose(bank[6][:, t * MDV:(t + 1) * MDV], vT[MDV:2 * MDV, t * P:(t + 1) * P],
                                                ident[MDV:2 * MDV, MDV:2 * MDV])
                        last.then_inc(v_turned, 1)

                    def values(e):
                        pe.wait_ge(p_ready, heads(e) * nt + at("p_ready", l, 0))
                        for k in range(4):
                            for t in range(2):
                                at_ = (k % 2) * C + t * P
                                last = pe.transpose(bank[4 + k // 2][:, at_:at_ + P],
                                                    Pl[:, t, k * P:(k + 1) * P], ident)
                            if k % 2:
                                last.then_inc(p_turned, 1)
                        if l == 0:
                            for k in range(2):
                                for t in range(2):
                                    last = pe.transpose(bank[7][:, k * C + t * P:k * C + (t + 1) * P],
                                                        Pc[:, t, k * P:(k + 1) * P], ident)
                            last.then_inc(p_turned, 1)
                        pe.wait_ge(v_act, heads(e) + at("v_act", l, 0))
                        pe.wait_ge(pt_act, i * (2 * (nb - 1)) + (at("pt_act", l, 0) + e * (nb - 1) + 1))
                        for k in range(4):
                            if k == 2:
                                pe.wait_ge(pt_dve, heads(e) + at("pt_dve", l, 0))
                            last = pe.matmul(bank[6][0:MDV, C:T], Vm[:, e, k, :], Tl[:, k, :],
                                             start=(k == 0), stop=(k == 3))
                        if l == 0:
                            pe.wait_ge(pt_act, heads(e) * 2 + at("pt_act", l, 0))
                            for k in range(2):
                                last = pe.matmul(bank[6][0:MDV, 0:C], Vm[:, e, k, :], Tc[:, k, :],
                                                 start=(k == 0), stop=(k == 1))
                        last.then_inc(o_done, 1)

                    for e in range(2):
                        project_head(e)
                        branch(ps[2 * e], 0, first)
                        score(e)
                        project(ps[2 * e + 1], first)
                        values(e)
                st.skip(MH // 2, MLA_BODY)
                pe.wait_ge(w2_in, 32 * (l + 1))
                ps = iter(st.take(GLA))
                chunks = range(first // CHUNK, NCH)
                for h in range(GH):
                    e = h % 2
                    if e == 0:
                        project(next(ps), first)
                        project(next(ps), 0)
                    pv = next(ps)
                    project(pv, 0)
                    if h > 0:
                        pe.wait_ge(gs_ready, at("gs_ready", l, h))
                    else:
                        pe.wait_ge(pt_act, at("pt_act", l, (nb - 1) * MH))
                    pe.matmul(bank[4][:, :], W2[:, h, :], LR, start=True, stop=True).then_inc(z_done, 1)
                    project(next(ps), first)
                    project(next(ps), first)
                    if h == 0:
                        pe.wait_ge(cat_lo, at("cat_lo", l, 8))
                    branch(next(ps), 4, first)
                    pe.wait_ge(bank_free[pv.slot], pv.turn + 1)
                    for t in range(4):
                        last = pe.transpose(bank[5][:, t * P:(t + 1) * P], gvT[:, t * P:(t + 1) * P], ident)
                    last.then_inc(g_turned, 1)
                    pe.wait_ge(kst_ready, at("kst_ready", l, h + 1))
                    if h > 0:
                        pe.wait_ge(go_norm, at("go_norm", l, h))
                    for t in range(4):
                        last = pe.transpose(bank[6][:, t * P:(t + 1) * P], gst[:, t * P:(t + 1) * P], ident)
                    last.then_inc(g_turned, 1)
                    for n in chunks:
                        for way in range(2):
                            r = slice(way * DK, (way + 1) * DK)
                            o = slice((n % 2) * CHUNK, (n % 2 + 1) * CHUNK)
                            at_ = (n // 2) * CHUNK
                            tk = slice(n * CHUNK, (n + 1) * CHUNK)
                            last = pe.matmul(bank[7 if way else 4][o, at_:at_ + CHUNK], gk[r, e, tk], gq[r, e, tk],
                                             start=True, stop=True)
                    last.then_inc(ga_done, 1)
                    project(next(ps), first)
                    pe.wait_ge(g_turned_act, at("g_turned_act", l, 2 * h + 2))
                    pe.wait_ge(ga_masked, at("ga_masked", l, h + 1))
                    for n in range(NCH):
                        o = slice((n % 2) * CHUNK, (n % 2 + 1) * CHUNK)
                        last = pe.matmul(bank[4 + n % 2][:, (n // 2) * DV:(n // 2 + 1) * DV],
                                         gKT[o, n // 2, :], gV[o, n // 2, :], start=True, stop=True)
                        if n >= NCH - 2:
                            last.then_inc(gu_done, 1)
                    branch(next(ps), 4, first)
                    for n in range(first // P, T // P):
                        pe.matmul(bank[6][:, n * P:(n + 1) * P], gV[:, n, :], gA[:, n, :],
                                  start=(n == first // P), stop=False, skip_group_check=True)
                    pe.wait_ge(gs_ready, at("gs_ready", l, h + 1))
                    for n in chunks:
                        tk = slice(n * CHUNK, (n + 1) * CHUNK)
                        last = pe.matmul(bank[6][:, tk], gS[:, n, :], gq[:, e, tk], start=False,
                                         stop=(n == NCH - 1), skip_group_check=True)
                    last.then_inc(go_done, 1)
                    pe.wait_ge(go_sq, at("go_sq", l, h + 1))
                    pe.matmul(bank[7][:, first:T], ones[:, :], gvT[:, first:T], start=True, stop=True) \
                        .then_inc(g_stat, 1)
                pe.wait_ge(cat_lo, at("cat_lo", l, 12))
                with pe.Fori(0, KD // 2) as i:
                    for n, p in enumerate(st.body(i, GATE_BODY)):
                        if n % 2 == 0:
                            project(p, first)
                        else:
                            branch(p, 0, first)
                st.skip(KD // 2, GATE_BODY)
                with pe.Fori(0, KD // SLOTS) as i:
                    for n, p in enumerate(st.body(i, UP_BODY)):
                        project(p, first, (lambda k: pe.wait_ge(m_lo, 8 * l + k + 1)) if n == 0 else None)
                st.skip(KD // SLOTS, UP_BODY)
                norm_stat(2 * l + 1, first)
                for n, (off, tiles) in enumerate(parts(l)):
                    with pe.Fori(0, tiles // 2) as i:
                        turn = i + (ADA_TURNS + off // 2)
                        ps = st.body(i, UP_BODY)

                        def units(ks):
                            if l == 0:
                                for k in ks:
                                    ada_unit(k, turn, "FFN")

                        def before(k):
                            pe.wait_ge(h_ready, 8 * (2 * l + 1) + k + 1)
                            if k == 4:
                                units((0, 1, 2))

                        if n == 0:
                            project_pair(ps[0:2], first, before)
                        else:
                            project(ps[0], first)
                            units((0, 1, 2))
                            project(ps[1], first)
                        units((3, 4, 5))
                        project(ps[2], first)
                        units((6, 7))
                        if l == 0:
                            ada_wait(turn)
                        project(ps[3], first)
                        if l == 0:
                            ada_turn(turn)
                    st.skip(tiles // 2, UP_BODY)
                    pe.wait_ge(f_lo, at("f_lo", l, off + tiles))
                    with pe.Fori(0, KD // SLOTS) as i:
                        for p in st.body(i, down_body(n)):
                            weights(p)
                            mm3(bank_of(p)[:, first:T], p, range(tiles), lambda k: ahi[:, k, first:T],
                                lambda k: alo[:, k, first:T]).then_inc(panel_done[p.slot], 1)
                    st.skip(KD // SLOTS, down_body(n))
            norm_stat(2 * L, C)
            for k in range(KD):
                pe.wait_ge(h_ready, 8 * 2 * L + k + 1)
                for t in range(2):
                    last = pe.transpose(bank[2 * t + k // 4][:, (k % 4) * P:(k % 4 + 1) * P],
                                        M[:, k, C + t * P:C + (t + 1) * P], ident)
                    if k % 4 == 3:
                        last.then_inc(fin_t, 1)

        @block.scalar
        def _(act):
            st = Stream()
            steps = Steps(act, act_step)

            def split(p):
                act.wait_ge(raw_loaded[p.slot], p.loaded)
                if not (isinstance(p.turn, int) and p.turn == 0):
                    act.wait_ge(panel_done[p.slot], p.turn)
                act.activation(whi[:, p.slot, 0:p.nk, :], raw[:, p.slot, 0:p.nk, :], ACT.Copy) \
                    .then_inc(hi_ready[p.slot], 1)

            def full(p):
                act.wait_ge(panel_done[p.slot], p.turn + 1)
                return bank[p.slot]

            def emptied(p):
                act.wait_ge(bank_free[p.slot], p.turn + 1)

            def gate(p, e, first):
                act.activation(TB[:, e, first:T], full(p)[:, first:T], ACT.Tanh, scale=0.5) \
                    .then_inc(bank_free[p.slot], 1)

            def ada_out(turn):
                act.wait_ge(ada_used, (turn + 1) * KD)
                if not (isinstance(turn, int) and turn == 0):
                    act.wait_ge(ada_cols, turn)
                act.activation(adarow, bank[7][0:4, :], ACT.Copy).then_inc(ada_row, 1)

            def ada_split(k, turn, stage):
                if stage == "first":
                    n = 2 * turn + k // 4
                    if k % 4 == 0:
                        act.wait_ge(ada_first[n % 3], 16 * (n // 3 + 1))
                    src = ada_half[n % 3][:, k % 4, :]
                else:
                    act.wait_ge(ada_loaded[k % ADA_SLOTS], (turn - ADA_FIRST) * 32 + 16 * (k // 4 + 1))
                    src = adaw[:, k % ADA_SLOTS, :]
                if stage != "first" or turn > 0:
                    act.wait_ge(ada_used, turn * KD + (k + 1 - ada_before(k, stage)))
                act.activation(ada_tiles(k, stage)[0], src, ACT.Copy).then_inc(ada_hi, 1)

            def inverse_root(dst, src, n):
                steps.link(act.activation(dst, src, ACT.Ln, scale=1.0 / n, bias=eps[:, :]))
                return act.activation(dst, dst, ACT.Exp, scale=-0.5)

            def square(k, first):
                act.activation(M[:, k, first:T], X[:, k, first:T], ACT.Square).then_inc(sq_ready, 1)

            def norm(m, l, w, first):
                act.wait_ge(stat_ready, m + 1)
                inverse_root(R[:, first:T], bank[4][:, first:T], D).then_inc(rms_ready, 1)
                if w is None:
                    return
                act.wait_ge(coef, 2 * l + w + 1)
                for k in range(KD):
                    act.wait_ge(t_ready, 8 * m + k + 1)
                    for s_ in range(first // C, 2):
                        last = act.activation(hhi[:, k, cols(s_)], M[:, k, cols(s_)], ACT.Identity,
                                              scale=am[:, l, w, k, s_:s_ + 1],
                                              bias=mod[:, l, (SH2 if w else SH1) + k, s_:s_ + 1])
                    last.then_inc(hf_hi, 1)

            act.wait_ge(start_t, 1)
            for s_, row in ((0, VC_CTX), (1, VC_LAT)):
                last = act.activation(cs[:, :, s_], bank[5][:, 4 * 96 + row:4 * 96 + row + KD], ACT.Silu)
            last.then_inc(start_c, 1)
            act.wait_ge(start_c, 1)
            act.activation(csr[:, :, 0:2], cs[:, :, :], ACT.Copy).then_inc(c_hi_ready, 1)
            for turn in range(ADA_FIRST):
                for k in range(KD):
                    ada_split(k, turn, "first")
                    if k == 1 and turn > 0:
                        ada_out(turn - 1)
                if turn < 2:
                    act.wait_ge(start_t, KD + 1)
                    for k in range(4 * turn, 4 * turn + 4):
                        act.wait_ge(x_ready, k + 1)
                        square(k, 0)
            ada_out(ADA_FIRST - 1)
            for p in st.peek(PROJ)[0:AHEAD]:
                split(p)

            for l in range(L):
                first = q0(l)
                norm(2 * l, l, 0, 0)
                ps = st.take(PROJ)
                ahead = ps + st.peek(MLA_BODY)[0:AHEAD]
                split(ahead[AHEAD])
                for n, p in enumerate(ps):
                    for turn, k in ada_units(l, n):
                        ada_split(k, turn, "projection")
                    if n != 1:
                        split(ahead[max(n + AHEAD, AHEAD + 1)])
                    if n < 3:
                        f = 0 if n == 2 else first
                        src = full(p)[:, f:T]
                        act.activation(cf[:, n, f:T], src, ACT.Copy).then_inc(cf_ready, 1)
                        act.activation(cy[:, n, f:T] if n < 2 else cu[:, 0, :], src, ACT.Square) \
                            .then_inc(cf_sq, 1)
                        act.wait_ge(cf_sq, at("cf_sq", l, n + 1))
                        act.sem_inc(bank_free[p.slot], 1)
                    elif n == 3:
                        full(p)
                        act.activation(LR, bank[p.slot][0:2 * RANK, :], ACT.Copy)
                        act.activation(kr[NOPE:QK, 0:C], bank[p.slot][NOPE:QK, 0:C], ACT.Copy).then_inc(kr_act, 1)
                    else:
                        j, what = (n - 4) // 3, (n - 4) % 3
                        if what == 0:
                            if j >= 2:
                                emptied(ps[n - 5])
                            act.activation(TB[:, j % 2, first:T], full(p)[:, first:T], ACT.Copy) \
                                .then_inc(bank_free[p.slot], 1)
                        elif what == 1:
                            emptied(p)
                            if j >= 2:
                                act.wait_ge(cat_lo, at("cat_lo", l, j - 1))
                            act.activation(cy[:, j % 2, first:T], cu[:, j % 2, first:T], ACT.Copy,
                                           scale=va[:, l, V_SC + 4 + j:V_SC + 5 + j]).then_inc(conv_mid, 1)
                        else:
                            emptied(p)
                            act.activation(ahi[:, j, first:T], cy[:, j % 2, first:T], ACT.Copy) \
                                .then_inc(cat_hi, 1)
                    if n == 4:
                        act.wait_ge(c_stat, at("c_stat", l, 2))
                        inverse_root(R[:, first:T], bank[4][:, first:T], QLORA).then_inc(c_rms, 1)
                        inverse_root(R2, bank[5][:, :], KVLORA).then_inc(c_rms, 1)
                    if 5 <= n <= 7:
                        f = 0 if n == 7 else first
                        act.wait_ge(c_norm, at("c_norm", l, n - 4))
                        act.activation(chi[:, n - 5, f:T], cf[:, n - 5, f:T], ACT.Copy).then_inc(c_hi, 1)
                    if ada_units(l, n) and n % 2:
                        ada_out(ada_units(l, n)[0][0])
                nt = 4 if l == 0 else 2

                def body(i, ps, after):
                    def heads(e):
                        return i * 2 + (e + 1)

                    def project_out(e):
                        act.wait_ge(a_q, heads(e) + at("a_q", l, 0))
                        if l == 0:
                            act.activation(Qb[0:QK, e, 0:C], bank[4][0:QK, 0:C], ACT.Copy)
                        act.activation(Qb[0:NOPE, e, C:T], bank[4][0:NOPE, C:T], ACT.Copy).then_inc(q_act, 1)
                        act.wait_ge(a_kv, heads(e) + at("a_kv", l, 0))
                        act.activation(Kb[0:NOPE, e, :], bank[5][0:NOPE, :], ACT.Copy)
                        act.activation(vT[NOPE:P, :], bank[5][NOPE:P, :], ACT.Copy).then_inc(k_act, 1)

                    def softmax(e):
                        act.wait_ge(v_turned, heads(e) + at("v_turned", l, 0))
                        act.activation(Vm[:, e, :, :], bank[6][:, 0:4 * MDV].rearrange("p (t n) -> p t n", t=4),
                                       ACT.Copy).then_inc(v_act, 1)
                        act.wait_ge(max_ready, heads(e) + at("max_ready", l, 0))
                        for t in range(nt):
                            src = bank[4 + t][:, :] if t < 2 else bank[7][:, (t - 2) * C:(t - 1) * C]
                            dst = Pl[:, t, :] if t < 2 else Pc[:, t - 2, :]
                            act.activation(dst, src, ACT.Exp, bias=mx[:, 1, t:t + 1], scale=scale,
                                           accum_out=mx[:, 2, t:t + 1]).then_inc(exped, 1)

                    def values_out(e):
                        nb = 3 if l == 0 else 2
                        act.wait_ge(p_turned, i * (2 * nb) + (at("p_turned", l, 0) + e * nb + 1))
                        act.activation(Tl[:, 0:2, :], bank[4][:, :].rearrange("p (k n) -> p k n", k=2), ACT.Copy) \
                            .then_inc(pt_act, 1)
                        if l == 0:
                            act.wait_ge(p_turned, i * (2 * nb) + (at("p_turned", l, 0) + e * nb + 3))
                            act.activation(Tc[:, :, :], bank[7][:, :].rearrange("p (k n) -> p k n", k=2), ACT.Copy) \
                                .then_inc(pt_act, 1)
                        act.wait_ge(bank_free[2 * e], ps[2 * e].turn)
                        gate(ps[2 * e + 1], e, first)
                        act.wait_ge(o_done, heads(e) + at("o_done", l, 0))
                        act.activation(OF[e * MDV:(e + 1) * MDV, first:T], bank[6][0:MDV, first:T], ACT.Copy) \
                            .then_inc(o_act, 1)

                    for e in range(2):
                        project_out(e)
                        split((ps + after)[2 * e + 2])
                        softmax(e)
                        split((ps + after)[2 * e + 3])
                        values_out(e)
                    act.wait_ge(o_act, i * 2 + (at("o_act", l, 2)))
                    act.activation(flat(ahi[:, bass.ds(i + 4, 1), first:T]), OF[:, first:T], ACT.Copy) \
                        .then_inc(cat_hi, 1)

                turns = MH // 2
                with act.Fori(0, turns - 1) as i:
                    body(i, st.body(i, MLA_BODY), st.body(i + 1, MLA_BODY))
                last_body = st.body(turns - 1, MLA_BODY)
                st.skip(turns, MLA_BODY)
                body(turns - 1, last_body, st.peek(GLA))

                ps = st.take(GLA)
                ahead = ps + st.peek(GATE_BODY)[0:AHEAD]
                of_branch = [p for p in ps if p.nk == 4]
                n = 0
                for h in range(GH):
                    e = h % 2
                    if e == 0:
                        for dst, f, mul in ((gq, first, DK ** -0.5), (gk, 0, 1.0)):
                            split(ahead[n + AHEAD])
                            src = full(ps[n])
                            for eh in range(2):
                                for way in range(2):
                                    last = act.activation(dst[way * DK:(way + 1) * DK, eh, f:T],
                                                          src[eh * DK:(eh + 1) * DK, f:T], ACT.Copy, scale=mul)
                            last.then_inc(bank_free[ps[n].slot], 1)
                            n += 1
                    split(ahead[n + AHEAD])
                    act.activation(gvT[:, :], full(ps[n])[:, :], ACT.Copy).then_inc(bank_free[ps[n].slot], 1)
                    n += 1
                    act.wait_ge(z_done, at("z_done", l, h + 1))
                    if h > 0:
                        act.wait_ge(cat_lo, at("cat_lo", l, 8 + h))
                    bias = va[:, l, V_GK + h:V_GK + h + 1]
                    steps.link(act.activation(gE[:, :], bank[4][:, :], ACT.Abs, bias=bias))
                    steps.link(act.activation(gE[:, :], gE[:, :], ACT.Exp, scale=-1.0))
                    act.activation(gE[:, :], gE[:, :], ACT.Ln, bias=1.0).then_inc(z_ln, 1)
                    split(ahead[n + AHEAD])
                    act.activation(gr[:, first:T], full(ps[n])[:, first:T], ACT.Tanh, scale=0.5) \
                        .then_inc(r_tanh, 1)
                    n += 1
                    act.wait_ge(b_ready, at("b_ready", l, h + 1))
                    act.activation(gE[:, :], gst[:, :], ACT.Exp, scale=1.0 / GATE_NORM)
                    act.activation(gx[:, :], gst[:, :], ACT.Exp, scale=-1.0 / GATE_NORM).then_inc(e_ready, 1)
                    split(ahead[n + AHEAD])
                    if h > 0:
                        emptied(of_branch[2 * h - 2])
                    gate(ps[n], 0, first)
                    n += 1
                    split(ahead[n + AHEAD])
                    n += 1
                    act.wait_ge(g_turned, at("g_turned", l, 2 * h + 1))
                    act.activation(gV[:, :, :], bank[5][:, :].rearrange("p (t n) -> p t n", t=4), ACT.Copy) \
                        .then_inc(g_turned_act, 1)
                    act.wait_ge(g_turned, at("g_turned", l, 2 * h + 2))
                    act.activation(gKT[:, :, :], bank[6][:, :].rearrange("p (t n) -> p t n", t=4), ACT.Copy) \
                        .then_inc(g_turned_act, 1)
                    split(ahead[n + AHEAD])
                    if h > 0:
                        emptied(of_branch[2 * h - 1])
                    gate(ps[n], 1, first)
                    n += 1
                    split(ahead[n + AHEAD])
                    n += 1
                    act.wait_ge(go_done, at("go_done", l, h + 1))
                    act.activation(gvT[:, first:T], bank[6][:, first:T], ACT.Square).then_inc(go_sq, 1)
                    act.wait_ge(g_stat, at("g_stat", l, h + 1))
                    inverse_root(R[:, first:T], bank[7][:, first:T], DV).then_inc(g_rms, 1)
                    act.wait_ge(go_norm, at("go_norm", l, h + 1))
                    act.activation(ahi[:, h, first:T], gE[:, first:T], ACT.Copy, scale=0.5).then_inc(cat_hi, 1)

                def gates(i, ps, after):
                    for e in range(2):
                        split((ps + after)[2 * e + 2])
                        if e == 0:
                            act.wait_ge(bank_free[1], ps[1].turn)
                        else:
                            act.wait_ge(bank_free[3], ps[3].turn)
                        gate(ps[2 * e], e, first)
                        split((ps + after)[2 * e + 3])

                turns = KD // 2
                with act.Fori(0, turns - 1) as i:
                    gates(i, st.body(i, GATE_BODY), st.body(i + 1, GATE_BODY)[0:AHEAD])
                last_body = st.body(turns - 1, GATE_BODY)
                st.skip(turns, GATE_BODY)
                gates(turns - 1, last_body, st.peek(UP_BODY)[0:AHEAD])
                act.wait_ge(panel_done[2], last_body[2].turn + 1)
                for k in range(KD):
                    act.wait_ge(m_ready, 8 * l + k + 1)
                    act.activation(hhi[:, k, first:T], M[:, k, first:T], ACT.Copy, scale=0.5).then_inc(m_hi, 1)

                def residual_stage(kinds, after, squares_from):
                    with act.Fori(0, KD // SLOTS - 1) as i:
                        for p in st.body(i, kinds)[AHEAD:] + st.body(i + 1, kinds)[0:AHEAD]:
                            split(p)
                    done = st.body(0, kinds) + st.body(1, kinds)
                    st.skip(KD // SLOTS, kinds)
                    ahead = done[SLOTS + AHEAD:] + (st.peek(after)[0:AHEAD] if after else [])
                    squared = 0
                    for n, p in enumerate(done[SLOTS:]):
                        if n < len(ahead):
                            split(ahead[n])
                        if squares_from is not None and n > 0:
                            for k in range(squared, SLOTS + n if n < SLOTS - 1 else KD):
                                emptied(done[k])
                                square(k, squares_from)
                                squared = k + 1

                residual_stage(UP_BODY, UP_BODY, first)
                norm(2 * l + 1, l, 1, first)
                for n, (off, tiles) in enumerate(parts(l)):
                    def hidden(i, ps, after):
                        def units(ks):
                            if l == 0:
                                for k in ks:
                                    ada_split(k, i + (ADA_TURNS + off // 2), "FFN")

                        for e in range(2):
                            pg, pu = ps[2 * e], ps[2 * e + 1]
                            if e == 0:
                                units((0, 1, 2))
                            else:
                                units((6, 7))
                            split((ps + after)[2 * e + 2])
                            split((ps + after)[2 * e + 3])
                            if e == 0:
                                units((3, 4, 5))
                            t = i * 2 + (off + e)
                            act.activation(fy[:, e, first:T], full(pg)[:, first:T], ACT.Identity,
                                           scale=vb[:, l, bass.ds(t + (V_FW + KF), 1)],
                                           bias=vb[:, l, bass.ds(t + V_FB, 1)]).then_inc(f_mid, 1)
                            if l == 0 and e == 1:
                                ada_out(i + (ADA_TURNS + off // 2))
                            emptied(pg)
                            act.activation(fs[:, e, first:T], fy[:, e, first:T], ACT.Silu).then_inc(f_silu, 1)
                            emptied(pu)
                            act.activation(flat(ahi[:, bass.ds(i * 2 + e, 1), first:T]), ff[:, e, first:T],
                                           ACT.Copy).then_inc(f_hi, 1)

                    turns = tiles // 2
                    with act.Fori(0, turns - 1) as i:
                        hidden(i, st.body(i, UP_BODY), st.body(i + 1, UP_BODY)[0:AHEAD])
                    last_body = st.body(turns - 1, UP_BODY)
                    st.skip(turns, UP_BODY)
                    hidden(turns - 1, last_body, st.peek(down_body(n))[0:AHEAD])
                    if n + 1 < len(FF_PARTS):
                        residual_stage(down_body(n), UP_BODY, None)
                    elif l < L - 1:
                        residual_stage(down_body(n), PROJ, 0)
                    else:
                        residual_stage(down_body(n), None, C)
            norm(2 * L, None, None, C)
            for q in range(2):
                act.wait_ge(fin_t, 2 * q + 2)
                act.activation(Z[:, D + q * 512:D + (q + 1) * 512], bank[2 + q][:, :], ACT.Copy) \
                    .then_inc(fin_a, 1)

        @block.gpsimd
        def _(pool):
            def ada_split(k, turn, stage):
                pool.wait_ge(ada_hi, turn * KD + (k + 1))
                hi, lo = ada_tiles(k, stage)
                pool.tensor_tensor(lo, adaw[:, k % ADA_SLOTS, :], hi.bitcast(F32), ALU.subtract) \
                    .then_inc(ada_lo, 1)

            def norm(l, w):
                m, first = 2 * l + w, q0(l) if w else 0
                pool.wait_ge(coef, m + 1)
                for k in range(KD):
                    pool.wait_ge(t_ready, 8 * m + k + 1)
                    for s_ in range(first // C, 2):
                        sh = (SH2 if w else SH1) + k
                        last = pool.tensor_scalar(hf[:, k, cols(s_)], M[:, k, cols(s_)],
                                                  am[:, l, w, k, s_:s_ + 1], mod[:, l, sh, s_:s_ + 1],
                                                  ALU.mult, ALU.add)
                    last.then_inc(hf_full, 1)

            for l in range(L):
                norm(l, 0)
                for n in range(len(PROJ)):
                    for turn, k in ada_units(l, n):
                        ada_split(k, turn, "projection")
                norm(l, 1)
                if l == 0:
                    with pool.Fori(0, KF // 2) as i:
                        for k in range(KD):
                            ada_split(k, i + ADA_TURNS, "FFN")

        @block.vector
        def _(dve):
            st = Stream()
            steps = Steps(dve, dve_step)

            def split(p):
                dve.wait_ge(hi_ready[p.slot], p.turn + 1)
                dve.tensor_tensor(wlo[:, p.slot, 0:p.nk, :], raw[:, p.slot, 0:p.nk, :],
                                  whi[:, p.slot, 0:p.nk, :].bitcast(F32), ALU.subtract) \
                    .then_inc(lo_ready[p.slot], 1)

            def full(p):
                dve.wait_ge(panel_done[p.slot], p.turn + 1)
                return bank[p.slot]

            def add_square(m, k, first):
                dve.wait_ge(sq_ready, 8 * m + k + 1)
                add = dve.tensor_tensor(M[:, 0, first:T], M[:, 0, first:T], M[:, k, first:T], ALU.add)
                if k < KD - 1:
                    steps.link(add)
                else:
                    add.then_inc(sum_ready, 1)

            def norm(m, l, w, first):
                dve.wait_ge(rms_ready, m + 1)
                if w is None:
                    for k in range(KD):
                        dve.scalar_tensor_tensor(out=M[:, k, first:T], in0=X[:, k, first:T],
                                                 scalar=vc[:, VC_FIN + k:VC_FIN + k + 1], in1=R[:, first:T],
                                                 op0=ALU.mult, op1=ALU.mult).then_inc(h_ready, 1)
                    return
                for k in range(KD + 1):
                    if k < KD:
                        dve.tensor_tensor(M[:, k, first:T], X[:, k, first:T], R[:, first:T], ALU.mult) \
                            .then_inc(t_ready, 1)
                    if k > 0:
                        dve.wait_ge(hf_hi, 8 * m + k)
                        dve.wait_ge(hf_full, 8 * m + k)
                        dve.tensor_tensor(hlo[:, k - 1, first:T], hf[:, k - 1, first:T],
                                          hhi[:, k - 1, first:T].bitcast(F32), ALU.subtract) \
                            .then_inc(h_ready, 1)

            def ada_in(l, chunk, turn):
                dve.wait_ge(ada_cols, turn + 1)
                b = va[:, l, bass.ds(chunk * 4 + V_ADA, 4)] if not isinstance(chunk, int) else \
                    va[:, l, V_ADA + 4 * chunk:V_ADA + 4 * chunk + 4]
                dst = mod[:, l, bass.ds(chunk * 4, 4), :] if not isinstance(chunk, int) else \
                    mod[:, l, 4 * chunk:4 * chunk + 4, :]
                src = bank[6][:, 0:16].rearrange("p (m s) -> p m s", s=4)
                dve.tensor_tensor(dst, src[:, :, 0:2], b.unsqueeze(2).to_broadcast([P, 4, 2]), ALU.add) \
                    .then_inc(ada_sum, 1)
                dve.wait_ge(ada_sum, turn + 1)
                dve.tensor_tensor(dst, dst, src[:, :, 2:4], ALU.add).then_inc(ada_mod, 1)

            def coefficients(l, w, turns):
                dve.wait_ge(ada_mod, turns)
                sc, g = (SC2, V_N2) if w else (SC1, V_N1)
                dve.scalar_tensor_tensor(out=am[:, l, w, :, :], in0=mod[:, l, sc:sc + KD, :], scalar=1.0,
                                         in1=va[:, l, g:g + KD].unsqueeze(2).to_broadcast([P, KD, 2]),
                                         op0=ALU.add, op1=ALU.mult).then_inc(coef, 1)

            def merge(p, e, j, first, begin):
                src = full(p)[:, first:T]
                dst = flat(M[:, bass.ds(j, 1), first:T]) if not isinstance(j, int) else M[:, j, first:T]
                if begin:
                    dve.scalar_tensor_tensor(out=dst, in0=TB[:, e, first:T], scalar=1.0, in1=src,
                                             op0=ALU.add, op1=ALU.mult).then_inc(bank_free[p.slot], 1)
                    return
                dve.scalar_tensor_tensor(out=TA[:, e, first:T], in0=TB[:, e, first:T], scalar=1.0, in1=src,
                                         op0=ALU.add, op1=ALU.mult).then_inc(bank_free[p.slot], 1)
                dve.wait_ge(bank_free[p.slot], p.turn + 1)
                steps.link(dve.tensor_tensor(dst, dst, TA[:, e, first:T], ALU.add))

            def residual(p, l, j, g):
                first_s = 0 if l < L - 1 else 1
                for s_ in range(first_s, 2):
                    dst = flat(X[:, bass.ds(j, 1), cols(s_)])
                    last = dve.scalar_tensor_tensor(
                        out=dst, in0=full(p)[:, cols(s_)], scalar=mod[:, l, bass.ds(j + g, 1), s_:s_ + 1]
                        .rearrange("p a b -> p (a b)"), in1=dst, op0=ALU.mult, op1=ALU.add)
                last.then_inc(bank_free[p.slot], 1)

            dve.memset(ones[:, :], 1.0)
            dve.memset(eps[:, :], EPS)
            dve.memset(W2[:, :, :], 0.0).then_inc(w2_zero, 1)
            dve.wait_ge(start_t, 1)
            dve.wait_ge(start_c, 1)
            dve.wait_ge(c_hi_ready, 1)
            dve.tensor_tensor(csr[:, :, 2:4], cs[:, :, :], csr[:, :, 0:2].bitcast(F32), ALU.subtract) \
                .then_inc(c_lo_ready, 1)
            for l in range(L):
                dve.tensor_copy(va[:, l, :], bank[5][:, l * 96:l * 96 + VA])
                dve.tensor_copy(vb[:, l, :], bank[5][:, (2 + l) * 96:(2 + l) * 96 + VB])
            dve.tensor_copy(vc[:, :], bank[5][:, 4 * 96:4 * 96 + VC])
            for k in range(KD):
                dve.wait_ge(start_t, k + 2)
                dve.tensor_copy(X[:, k, :], bank[k % 4][:, :]).then_inc(x_ready, 1)
            for turn in range(ADA_FIRST):
                for k in range(KD):
                    dve.wait_ge(ada_hi, turn * KD + k + 1)
                    n = 2 * turn + k // 4
                    hi, lo = ada_tiles(k, "first")
                    dve.tensor_tensor(lo, ada_half[n % 3][:, k % 4, :], hi.bitcast(F32), ALU.subtract) \
                        .then_inc(ada_lo, 1)
                    if k == 3 and turn > 0:
                        ada_in(0, turn - 1, turn - 1)
                if turn in (1, 2):
                    for k in range(1, 4) if turn == 1 else range(4, KD):
                        add_square(0, k, 0)
            ada_in(0, ADA_FIRST - 1, ADA_FIRST - 1)
            coefficients(0, 0, ADA_FIRST)
            for p in st.peek(PROJ)[0:AHEAD]:
                split(p)

            for l in range(L):
                first = q0(l)
                norm(2 * l, l, 0, 0)
                ps = st.take(PROJ)
                ahead = ps + st.peek(MLA_BODY)[0:AHEAD]
                split(ahead[AHEAD])
                for n, p in enumerate(ps):
                    if n != 1:
                        split(ahead[max(n + AHEAD, AHEAD + 1)])
                    if n == 3:
                        src = full(p)
                        dve.wait_ge(kr_act, at("kr_act", l, 1))
                        dve.tensor_tensor(TA[NOPE:QK, 0, C:T], src[QK:P, C:T], K[QK:P, K_ROPE:K_ROPE + C],
                                          ALU.mult)
                        steps.link(dve.tensor_tensor(kr[NOPE:QK, C:T], src[NOPE:QK, C:T],
                                                     K[NOPE:QK, K_ROPE:K_ROPE + C], ALU.mult))
                        dve.tensor_tensor(kr[NOPE:QK, C:T], kr[NOPE:QK, C:T], TA[NOPE:QK, 0, C:T], ALU.add) \
                            .then_inc(bank_free[p.slot], 1)
                    elif n > 3:
                        j, what = (n - 4) // 3, (n - 4) % 3
                        if what == 0:
                            pass
                        elif what == 1:
                            dve.wait_ge(bank_free[ps[n - 1].slot], ps[n - 1].turn + 1)
                            dve.tensor_tensor(cu[:, j % 2, first:T], TB[:, j % 2, first:T], full(p)[:, first:T],
                                              ALU.mult).then_inc(bank_free[p.slot], 1)
                            dve.wait_ge(conv_mid, at("conv_mid", l, j + 1))
                            u, y = seg(cu[:, j % 2, :], l), seg(cy[:, j % 2, :], l)
                            steps.link(dve.scalar_tensor_tensor(
                                out=y[:, :, 1:C], in0=u[:, :, 0:C - 1], scalar=va[:, l, V_SC + j:V_SC + j + 1],
                                in1=y[:, :, 1:C], op0=ALU.mult, op1=ALU.add))
                            steps.link(dve.scalar_tensor_tensor(
                                out=y[:, :, 0:C - 1], in0=u[:, :, 1:C],
                                scalar=va[:, l, V_SC + 8 + j:V_SC + 9 + j], in1=y[:, :, 0:C - 1],
                                op0=ALU.mult, op1=ALU.add))
                        else:
                            dve.tensor_tensor(cy[:, j % 2, first:T], cy[:, j % 2, first:T], full(p)[:, first:T],
                                              ALU.mult).then_inc(bank_free[p.slot], 1)
                            dve.wait_ge(cat_hi, at("cat_hi", l, j + 1))
                            dve.tensor_tensor(alo[:, j, first:T], cy[:, j % 2, first:T],
                                              ahi[:, j, first:T].bitcast(F32), ALU.subtract).then_inc(cat_lo, 1)
                    if n == 4:
                        dve.wait_ge(c_rms, at("c_rms", l, 2))
                        for m in range(3):
                            f, r = (0, R2) if m == 2 else (first, R)
                            g = va[:, l, (V_KN if m == 2 else V_QN + m):(V_KN if m == 2 else V_QN + m) + 1]
                            dve.scalar_tensor_tensor(out=cf[:, m, f:T], in0=cf[:, m, f:T], scalar=g,
                                                     in1=r[:, f:T], op0=ALU.mult, op1=ALU.mult) \
                                .then_inc(c_norm, 1)
                    if 6 <= n <= 8:
                        f = 0 if n == 8 else first
                        dve.wait_ge(c_hi, at("c_hi", l, n - 5))
                        dve.tensor_tensor(clo[:, n - 6, f:T], cf[:, n - 6, f:T],
                                          chi[:, n - 6, f:T].bitcast(F32), ALU.subtract).then_inc(c_lo, 1)
                    if ada_units(l, n - 1) and n % 2 == 0:
                        turn = ada_units(l, n - 1)[0][0]
                        ada_in(*chunk_of(turn), turn)
                if l == 0:
                    ada_in(0, ADA_TURNS - 1, ADA_TURNS - 1)
                    coefficients(0, 1, ADA_TURNS)
                dve.wait_ge(bank_free[3], ps[3].turn + 1)
                for e in range(2):
                    last = dve.tensor_copy(Kb[NOPE:QK, e, :], kr[NOPE:QK, :])
                last.then_inc(kr_dve, 1)
                nt = 4 if l == 0 else 2
                nb = 3 if l == 0 else 2

                def body(i, ps, after):
                    def heads(e):
                        return i * 2 + (e + 1)

                    def rotate(e):
                        dve.wait_ge(a_q, heads(e) + at("a_q", l, 0))
                        dve.wait_ge(q_act, heads(e) + at("q_act", l, 0))
                        dve.tensor_tensor(TA[NOPE:QK, 0, C:T], bank[4][QK:P, C:T], K[QK:P, K_ROPE:K_ROPE + C],
                                          ALU.mult)
                        steps.link(dve.tensor_tensor(Qb[NOPE:QK, e, C:T], bank[4][NOPE:QK, C:T],
                                                     K[NOPE:QK, K_ROPE:K_ROPE + C], ALU.mult))
                        dve.tensor_tensor(Qb[NOPE:QK, e, C:T], Qb[NOPE:QK, e, C:T], TA[NOPE:QK, 0, C:T],
                                          ALU.add).then_inc(q_dve, 1)

                    def softmax(e):
                        for t in range(nt):
                            if t < 3:
                                tiles = t + 1 if t < 2 else nt
                                dve.wait_ge(scored, i * (2 * nt) + (at("scored", l, 0) + e * nt + tiles))
                            src = bank[4 + t][:, :] if t < 2 else bank[7][:, (t - 2) * C:(t - 1) * C]
                            last = dve.reduce_max(mx[:, 0, t:t + 1], src, AX_X)
                        steps.link(last)
                        dve.tensor_scalar(mx[:, 1, 0:nt], mx[:, 0, 0:nt], -scale, None, ALU.mult) \
                            .then_inc(max_ready, 1)
                        dve.wait_ge(exped, i * (2 * nt) + (at("exped", l, 0) + (e + 1) * nt))
                        steps.link(dve.reciprocal(mx[:, 3, 0:nt], mx[:, 2, 0:nt]))
                        for t in range(nt):
                            pr = Pl[:, t, :] if t < 2 else Pc[:, t - 2, :]
                            dve.tensor_scalar(pr, pr, mx[:, 3, t:t + 1], None, ALU.mult).then_inc(p_ready, 1)

                    def values_out(e):
                        dve.wait_ge(p_turned, i * (2 * nb) + (at("p_turned", l, 0) + e * nb + 2))
                        if e == 1:
                            dve.wait_ge(o_done, i * 2 + at("o_done", l, 1))
                        dve.tensor_copy(Tl[:, 2:4, :], bank[5][:, :].rearrange("p (k n) -> p k n", k=2)) \
                            .then_inc(pt_dve, 1)

                    for e in range(2):
                        rotate(e)
                        split((ps + after)[2 * e + 2])
                        softmax(e)
                        values_out(e)
                        dve.wait_ge(bank_free[2 * e + 1], ps[2 * e + 1].turn + 1)
                        merge(ps[2 * e], e, i * 2 + e, first, True)
                        split((ps + after)[2 * e + 3])
                    dve.wait_ge(cat_hi, i + (at("cat_hi", l, 4) + 1))
                    dve.tensor_tensor(flat(alo[:, bass.ds(i + 4, 1), first:T]), OF[:, first:T],
                                      flat(ahi[:, bass.ds(i + 4, 1), first:T]).bitcast(F32),
                                      ALU.subtract).then_inc(cat_lo, 1)

                turns, links = MH // 2, 6
                with dve.Fori(0, turns - 1) as i:
                    steps.enter(i, links)
                    body(i, st.body(i, MLA_BODY), st.body(i + 1, MLA_BODY))
                steps.leave(turns - 1)
                last_body = st.body(turns - 1, MLA_BODY)
                st.skip(turns, MLA_BODY)
                body(turns - 1, last_body, st.peek(GLA))

                ps = st.take(GLA)
                ahead = ps + st.peek(GATE_BODY)[0:AHEAD]
                n = 0
                dve.wait_ge(cat_lo, at("cat_lo", l, 8))
                for half in range(2):
                    r, o = slice(half * CHUNK, (half + 1) * CHUNK), slice((1 - half) * CHUNK, (2 - half) * CHUNK)
                    dve.memset(gA[r, :, o], 0.0)
                dve.memset(gS[0:DK, 0, :], 0.0)
                steps.link(dve.memset(gS[DK:P, NCH // 2 - 1, :], 0.0))
                chunk_pairs = slice(first // P, T // P)
                pairs = (T - first) // P
                for h in range(GH):
                    e = h % 2
                    if e == 0:
                        split(ahead[n + AHEAD])
                        split(ahead[n + 1 + AHEAD])
                        n += 2
                    split(ahead[n + AHEAD])
                    n += 1
                    dve.wait_ge(z_done, at("z_done", l, h + 1))
                    dve.wait_ge(z_ln, at("z_ln", l, h + 1))
                    if h > 0:
                        dve.wait_ge(g_turned, at("g_turned", l, 2 * h))
                    steps.link(dve.tensor_scalar(gx[:, :], bank[4][:, :], va[:, l, V_GK + h:V_GK + h + 1], 0.0,
                                                 ALU.add, ALU.min))
                    steps.link(dve.tensor_tensor(gx[:, :], gx[:, :], gE[:, :], ALU.subtract))
                    dve.tensor_tensor_scan(gst[0:DK, :], K[0:DK, K_SCAN:K_SCAN + T], gx[0:DK, :], 0.0,
                                           ALU.mult, ALU.add)
                    dve.tensor_tensor_scan(gst[DK:P, ::-1], K[DK:P, K_SCAN:K_SCAN + T][:, ::-1],
                                           gx[DK:P, ::-1], 0.0, ALU.mult, ALU.add).then_inc(b_ready, 1)
                    split(ahead[n + AHEAD])
                    dve.wait_ge(r_tanh, at("r_tanh", l, h + 1))
                    dve.scalar_tensor_tensor(out=gr[:, first:T], in0=gr[:, first:T], scalar=1.0,
                                             in1=full(ps[n])[:, first:T], op0=ALU.add, op1=ALU.mult) \
                        .then_inc(bank_free[ps[n].slot], 1)
                    n += 1
                    dve.wait_ge(e_ready, at("e_ready", l, h + 1))
                    if e == 0:
                        for m in (n - 4, n - 3):
                            dve.wait_ge(bank_free[ps[m].slot], ps[m].turn + 1)
                    steps.mark(dve.tensor_tensor(gq[:, e, first:T], gq[:, e, first:T], gE[:, first:T], ALU.mult))
                    dve.tensor_tensor(gk[:, e, :], gk[:, e, :], gx[:, :], ALU.mult).then_inc(qk_decayed, 1)
                    dve.wait_ge(qk_decayed, at("qk_decayed", l, h + 1))
                    for way in range(2):
                        r = slice(way * DK, (way + 1) * DK)
                        end = 0 if way else CHUNK - 1
                        ends = gE[r, :].rearrange("p (n i) -> p n i", i=CHUNK)[:, :, end:end + 1]
                        last = dve.tensor_tensor(gst[r, :].rearrange("p (n i) -> p n i", i=CHUNK),
                                                 gk[r, e, :].rearrange("p (n i) -> p n i", i=CHUNK),
                                                 ends.to_broadcast([DK, NCH, CHUNK]), ALU.mult)
                    last.then_inc(kst_ready, 1)
                    split(ahead[n + AHEAD])
                    gp = ps[n]
                    n += 1
                    split(ahead[n + AHEAD])
                    dve.wait_ge(bank_free[gp.slot], gp.turn + 1)
                    merge(ps[n], 0, 2 * h, first, False)
                    n += 1
                    dve.wait_ge(ga_done, at("ga_done", l, h + 1))
                    for way, mask in ((0, K_MF), (1, K_MB)):
                        src = bank[7 if way else 4][:, 0:C].rearrange("p (n i) -> p n i", i=CHUNK)
                        last = dve.tensor_tensor(
                            TA[:, way, 0:C].rearrange("p (n i) -> p n i", i=CHUNK)[:, chunk_pairs, :],
                            src[:, chunk_pairs, :],
                            K[:, mask:mask + CHUNK].unsqueeze(1).to_broadcast([P, pairs, CHUNK]), ALU.mult)
                    steps.link(last)
                    for half in range(2):
                        r = slice(half * CHUNK, (half + 1) * CHUNK)
                        t0, t1 = (TA[r, way, 0:C].rearrange("p (n i) -> p n i", i=CHUNK)[:, chunk_pairs, :]
                                  for way in range(2))
                        last = dve.tensor_tensor(gA[r, chunk_pairs, r], t0, t1, ALU.add)
                    last.then_inc(ga_masked, 1)
                    split(ahead[n + AHEAD])
                    gp = ps[n]
                    n += 1
                    split(ahead[n + AHEAD])
                    dve.wait_ge(gu_done, at("gu_done", l, 2 * h + 2))
                    orders = [scan_order(way) for way in range(2)]
                    for m in range(NCH - 1):
                        for way in range(2):
                            r = slice(way * DK, (way + 1) * DK)
                            a, b = orders[way][m], orders[way][m + 1]
                            col = a * CHUNK + (0 if way else CHUNK - 1)
                            last = dve.scalar_tensor_tensor(
                                out=gS[r, b, :], in0=gS[r, a, :], scalar=gE[r, col:col + 1],
                                in1=bank[4 + a % 2][r, (a // 2) * DV:(a // 2 + 1) * DV],
                                op0=ALU.mult, op1=ALU.add)
                        if m < NCH - 2:
                            steps.link(last)
                    last.then_inc(gs_ready, 1)
                    dve.wait_ge(bank_free[gp.slot], gp.turn + 1)
                    merge(ps[n], 1, 2 * h + 1, first, False)
                    n += 1
                    dve.wait_ge(g_rms, at("g_rms", l, h + 1))
                    steps.link(dve.scalar_tensor_tensor(
                        out=gE[:, first:T], in0=bank[6][:, first:T], scalar=va[:, l, V_GN + h:V_GN + h + 1],
                        in1=R[:, first:T], op0=ALU.mult, op1=ALU.mult))
                    dve.tensor_tensor(gE[:, first:T], gE[:, first:T], gr[:, first:T], ALU.mult) \
                        .then_inc(go_norm, 1)
                    dve.wait_ge(cat_hi, at("cat_hi", l, 8 + h + 1))
                    dve.scalar_tensor_tensor(out=alo[:, h, first:T], in0=gE[:, first:T], scalar=0.5,
                                             in1=ahi[:, h, first:T].bitcast(F32), op0=ALU.mult,
                                             op1=ALU.subtract).then_inc(cat_lo, 1)

                def gates(i, ps, after):
                    for e in range(2):
                        split((ps + after)[2 * e + 2])
                        split((ps + after)[2 * e + 3])
                        dve.wait_ge(bank_free[2 * e], ps[2 * e].turn + 1)
                        p = ps[2 * e + 1]
                        dst = flat(M[:, bass.ds(i * 2 + e, 1), first:T])
                        dve.scalar_tensor_tensor(out=TA[:, e, first:T], in0=TB[:, e, first:T], scalar=1.0,
                                                 in1=full(p)[:, first:T], op0=ALU.add, op1=ALU.mult) \
                            .then_inc(bank_free[p.slot], 1)
                        dve.wait_ge(bank_free[p.slot], p.turn + 1)
                        dve.tensor_tensor(dst, dst, TA[:, e, first:T], ALU.add).then_inc(m_ready, 1)

                turns = KD // 2
                with dve.Fori(0, turns - 1) as i:
                    gates(i, st.body(i, GATE_BODY), st.body(i + 1, GATE_BODY)[0:AHEAD])
                last_body = st.body(turns - 1, GATE_BODY)
                st.skip(turns, GATE_BODY)
                gates(turns - 1, last_body, st.peek(UP_BODY)[0:AHEAD])
                for k in range(KD):
                    dve.wait_ge(m_hi, 8 * l + k + 1)
                    dve.scalar_tensor_tensor(out=hlo[:, k, first:T], in0=M[:, k, first:T], scalar=0.5,
                                             in1=hhi[:, k, first:T].bitcast(F32), op0=ALU.mult,
                                             op1=ALU.subtract).then_inc(m_lo, 1)

                def residual_stage(kinds, g, after, m, norm_first):
                    turns = KD // SLOTS
                    with dve.Fori(0, turns - 1) as i:
                        ahead = st.body(i, kinds)[AHEAD:] + st.body(i + 1, kinds)[0:AHEAD]
                        for n, p in enumerate(st.body(i, kinds)):
                            split(ahead[n])
                            residual(p, l, i * SLOTS + n, g)
                    ps = st.body(turns - 1, kinds)
                    st.skip(turns, kinds)
                    ahead = ps[AHEAD:] + (st.peek(after)[0:AHEAD] if after else [])
                    for n, p in enumerate(ps):
                        if n < len(ahead):
                            split(ahead[n])
                        residual(p, l, (turns - 1) * SLOTS + n, g)
                        if m is not None:
                            for k in ((), (1, 2, 3), (4, 5), (6, 7))[n]:
                                add_square(m, k, norm_first)

                residual_stage(UP_BODY, G1, UP_BODY, 2 * l + 1, first)
                norm(2 * l + 1, l, 1, first)
                for n, (off, tiles) in enumerate(parts(l)):
                    def hidden(i, ps, after):
                        for e in range(2):
                            pg, pu = ps[2 * e], ps[2 * e + 1]
                            split((ps + after)[2 * e + 2])
                            split((ps + after)[2 * e + 3])
                            t = i * 2 + (off + e)
                            g, y = seg(full(pg)[:, :], l), seg(fy[:, e, :], l)
                            dve.wait_ge(f_mid, t + at("f_mid", l, 1))
                            steps.link(dve.scalar_tensor_tensor(
                                out=y[:, :, 1:C], in0=g[:, :, 0:C - 1], scalar=vb[:, l, bass.ds(t + V_FW, 1)],
                                in1=y[:, :, 1:C], op0=ALU.mult, op1=ALU.add))
                            dve.scalar_tensor_tensor(
                                out=y[:, :, 0:C - 1], in0=g[:, :, 1:C],
                                scalar=vb[:, l, bass.ds(t + (V_FW + 2 * KF), 1)], in1=y[:, :, 0:C - 1],
                                op0=ALU.mult, op1=ALU.add).then_inc(bank_free[pg.slot], 1)
                            dve.wait_ge(f_silu, t + at("f_silu", l, 1))
                            dve.tensor_tensor(ff[:, e, first:T], fs[:, e, first:T], full(pu)[:, first:T],
                                              ALU.mult).then_inc(bank_free[pu.slot], 1)
                            dve.wait_ge(f_hi, t + at("f_hi", l, 1))
                            dve.tensor_tensor(flat(alo[:, bass.ds(i * 2 + e, 1), first:T]), ff[:, e, first:T],
                                              flat(ahi[:, bass.ds(i * 2 + e, 1), first:T]).bitcast(F32),
                                              ALU.subtract).then_inc(f_lo, 1)
                        if l == 0:
                            ada_in(1, i + off // 2, i + (ADA_TURNS + off // 2))

                    turns = tiles // 2
                    with dve.Fori(0, turns - 1) as i:
                        steps.enter(i, 2)
                        hidden(i, st.body(i, UP_BODY), st.body(i + 1, UP_BODY)[0:AHEAD])
                    steps.leave(turns - 1)
                    last_body = st.body(turns - 1, UP_BODY)
                    st.skip(turns, UP_BODY)
                    hidden(turns - 1, last_body, st.peek(down_body(n))[0:AHEAD])
                    if n + 1 < len(FF_PARTS):
                        residual_stage(down_body(n), G2, UP_BODY, None, None)
                    elif l < L - 1:
                        residual_stage(down_body(n), G2, PROJ, 2 * l + 2, 0)
                    else:
                        residual_stage(down_body(n), G2, None, 2 * l + 2, C)
                if l == 0:
                    coefficients(1, 0, 2 * ADA_TURNS - 1)
                    coefficients(1, 1, 2 * ADA_TURNS - 1)
            norm(2 * L, None, None, C)
            for q in range(2):
                dve.wait_ge(fin_t, 2 * q + 1)
                dve.tensor_copy(Z[:, q * 512:(q + 1) * 512], bank[q][:, :]).then_inc(fin_v, 1)


def constants():
    k = np.zeros((P, K_ALL), np.float32)
    k[:, K_ID:K_ID + P] = np.eye(P)
    j, i = np.arange(P)[:, None] % CHUNK, np.arange(CHUNK)[None, :]
    k[:, K_MF:K_MF + CHUNK] = j <= i
    k[:, K_MB:K_MB + CHUNK] = j >= i
    t = np.arange(T)
    k[0:DK, K_SCAN:K_SCAN + T] = t % CHUNK != 0
    k[DK:P, K_SCAN:K_SCAN + T] = t % CHUNK != CHUNK - 1
    freqs = ROPE // 4
    inv = (10000.0 ** (-np.arange(freqs, dtype=np.float32) / freqs)).astype(np.float32)
    pos = [np.arange(C) // GRID_W, np.arange(C) % GRID_W]
    for axis in range(2):
        ang = (pos[axis][None, :].astype(np.float32) * inv[:, None]).astype(np.float32)
        for half in range(2):
            r = axis * 2 * freqs + half * freqs
            k[NOPE + r:NOPE + r + freqs, K_ROPE:K_ROPE + C] = np.cos(ang)
            k[QK + r:QK + r + freqs, K_ROPE:K_ROPE + C] = np.sin(ang) * (1 if half else -1)
    return k


_INS = ["x", "c", "ctx", "c_ctx", "w_ada", "b_ada", "norm1_g", "w_in", "w_gk2", "b_gk2", "gla_norm_g",
        "mla_q_norm_g", "w_uq", "mla_kv_norm_g", "w_ukv", "sc_w", "w_br_a", "w_br_b", "w_br_c", "w_o",
        "norm2_g", "w_ffn_gate", "w_ffn_up", "ffn_conv_w", "ffn_conv_b", "w_ffn_down", "final_norm_g"]


def kernel(**inputs):
    import concourse.bacc as bacc
    from concourse.bass_utils import run_bass_kernel_spmd

    nc = bacc.Bacc("TRN2", target_bir_lowering=False, num_devices=1)
    arrays, args = {}, []
    for name in _INS + ["consts"]:
        a = constants() if name == "consts" else np.ascontiguousarray(inputs[name])
        arrays[f"in_{name}"] = a
        args.append(nc.dram_tensor(f"in_{name}", a.shape, F32, kind="ExternalInput").ap())
    args.append(nc.dram_tensor("out_0", (1, C, D), F32, kind="ExternalOutput").ap())
    build(nc, *args)
    r = run_bass_kernel_spmd(nc, [arrays], core_ids=[0])
    return r.results[0]["out_0"]
```

```python
from contextlib import ExitStack

import numpy as np

import concourse.bass as bass
from concourse import mybir

F32 = mybir.dt.float32
F32R = mybir.dt.float32r
ALU = mybir.AluOpType
ACT = mybir.ActivationFunctionType
AX_X = mybir.AxisListType.X

P = 128
D = 1024
KD = D // P
C = 256
T = 2 * C
L = 2
GRID_W = 64
EPS = 1e-6
GH, DK, DV, RANK, CHUNK = 4, 64, 128, 16, 64
NCH = T // CHUNK
GATE_NORM = 16.0
MH, NOPE, ROPE, MDV = 8, 64, 32, 64
QK = NOPE + ROPE
QLORA, KVLORA = 256, 128
SCW = 512
FF = 2816
KF = FF // P
FF_PARTS = [8, 8, 6]
SLOTS = 4
AHEAD = 2
MERGED_EARLY = 4
ADA_SLOTS = 4
ADA_CHUNK = 512
ADA_TURNS = 6 * D // ADA_CHUNK
ADA_FIRST = 4
O_Q, O_K, O_V, O_R, O_LR = 0, 256, 512, 1024, 1536
O_CQ = O_LR + 2 * RANK
O_CKV = O_CQ + QLORA
O_KR = O_CKV + KVLORA
O_SB = O_KR + ROPE
O_SC, O_SX = O_SB + SCW, O_SB + 2 * SCW
O_G = O_SX + SCW
BR_A, BR_B, BR_C = 0, 1, 2
V_ADA, V_N1, V_N2, V_GN, V_QN, V_KN, V_SC, V_GK = 0, 48, 56, 64, 68, 70, 71, 83
VA = 87
V_FW, V_FB = 0, 3 * KF
VB = 4 * KF
VC_FIN, VC_CTX, VC_LAT = 0, 8, 16
VC = 24
SH1, SC1, G1, SH2, SC2, G2 = (8 * m for m in range(6))
K_ID, K_MF, K_MB, K_SCAN, K_ROPE = 0, 128, 192, 256, 768
K_ALL = 1024

PROJ = [(8, 1)] * 3 + [(8, 7)] + [(8, 1)] * 12
PROJ_COLUMNS = [O_CQ, O_CQ + P, O_CKV, None] + [o + j * P for j in range(SCW // P) for o in (O_SC, O_SX, O_SB)]
EARLY = 3
MLA_BODY = [(7, 7), (8, 1), (7, 7), (8, 1)]
HEAD_PANELS = [(8, 1), (8, 1), (8, 1), (4, 1), (8, 1), (4, 1)]
GLA = ([(8, 1)] * 2 + HEAD_PANELS * 2) * 2
GATE_BODY = [(8, 1), (4, 1)] * 2
UP_BODY = [(8, 1)] * 4
VEC_DMAS = 9 + 2 + 3


def down_body(part):
    return [(FF_PARTS[part], 1)] * 4


class Panel:

    def __init__(self, slot, turn, loaded, nk, dmas):
        self.slot, self.turn, self.loaded, self.nk, self.dmas = slot, turn, loaded, nk, dmas


class Stream:

    def __init__(self):
        self.turns, self.loaded, self.at = [0] * SLOTS, [0] * SLOTS, 0

    def take(self, kinds):
        out = []
        for nk, dmas in kinds:
            s = self.at % SLOTS
            self.loaded[s] += 16 * dmas
            out.append(Panel(s, self.turns[s], self.loaded[s], nk, dmas))
            self.turns[s] += 1
            self.at += 1
        return out

    def peek(self, kinds):
        keep = list(self.turns), list(self.loaded), self.at
        out = self.take(kinds)
        self.turns, self.loaded, self.at = keep
        return out

    def body(self, i, kinds):
        assert self.at % SLOTS == 0 and len(kinds) == SLOTS
        return [Panel(s, i + self.turns[s], i * (16 * d) + (self.loaded[s] + 16 * d), nk, d)
                for s, (nk, d) in enumerate(kinds)]

    def skip(self, n, kinds):
        for _ in range(n):
            self.take(kinds)


class Steps:

    def __init__(self, eng, sem):
        self.eng, self.sem, self.base, self.n = eng, sem, 0, 0

    def link(self, ins):
        self.mark(ins)
        self.wait()

    def mark(self, ins):
        ins.then_inc(self.sem, 1)
        self.n += 1

    def wait(self, back=0):
        self.eng.wait_ge(self.sem, self.base + (self.n - back))

    def enter(self, i, per):
        self.kept, self.per, self.base = self.n, per, i * per

    def leave(self, turns):
        assert self.n - self.kept == self.per, self.n - self.kept
        self.base, self.n = 0, self.kept + self.per * turns


def build(nc, x, c, ctx, c_ctx, w_ada, b_ada, norm1_g, w_in, w_gk2, b_gk2, gla_norm_g, mla_q_norm_g,
          w_uq, mla_kv_norm_g, w_ukv, sc_w, w_br_a, w_br_b, w_br_c, w_o, norm2_g, w_ffn_gate,
          w_ffn_up, ffn_conv_w, ffn_conv_b, w_ffn_down, final_norm_g, consts, out):
    w_br = [w_br_a, w_br_b, w_br_c]

    with ExitStack() as stack:
        def sb(name, shape, dt=F32):
            return stack.enter_context(nc.sbuf_tensor(name, shape, dt))

        def sem(name):
            return stack.enter_context(nc.semaphore(name))

        def sems(name, n):
            return [sem(f"{name}{i}") for i in range(n)]

        bank = [stack.enter_context(nc.psum_tensor(f"bank{i}", [P, 512], F32)) for i in range(8)]

        raw = sb("raw", [P, SLOTS, 8, P])
        whi = sb("whi", [P, SLOTS, 8, P], F32R)
        wlo = sb("wlo", [P, SLOTS, 8, P], F32R)
        X = sb("X", [P, KD, T])
        hhi = sb("hhi", [P, KD, T], F32R)
        hlo = sb("hlo", [P, KD, T], F32R)
        M = sb("M", [P, KD, T])
        ahi = sb("ahi", [P, 8, T], F32R)
        alo = sb("alo", [P, 8, T], F32R)
        chi = sb("chi", [P, 3, T], F32R)
        clo = sb("clo", [P, 3, T], F32R)
        TA = sb("TA", [P, 2, T])
        TB = sb("TB", [P, 2, T])
        gL = sb("gL", [P, T])
        R = sb("R", [P, T])
        K = sb("K", [P, K_ALL])
        ones = sb("ones", [P, P])
        eps = sb("eps", [P, 1])
        ln_out = sb("ln_out", [P, 1])
        va = sb("va", [P, L, VA])
        vb = sb("vb", [P, L, VB])
        vc = sb("vc", [P, VC])
        cs = sb("cs", [P, KD, 2])
        csr = sb("csr", [P, KD, 4], F32R)
        mod = sb("mod", [P, L, 48, 2])
        am = sb("am", [P, L, 2, KD, 2])
        Z = sb("Z", [P, 7680])
        W2 = sb("W2", [2 * RANK, GH, P])

        vec_in = [TB[:, :, :].rearrange("p a n -> p (a n)")[:, n * P:(n + 1) * P] for n in range(5)]
        vec_rows = [VA, VA, VB, VB, VC]


        def zv(at, *shape):
            n = int(np.prod(shape))
            v = Z[:, at:at + n]
            if len(shape) == 2:
                v = v.rearrange("p (a b) -> p a b", a=shape[0])
            if len(shape) == 3:
                v = v.rearrange("p (a b c) -> p a b c", a=shape[0], b=shape[1])
            return v

        LR = Z[0:2 * RANK, 0:T]
        z0 = T
        adaw = zv(z0, ADA_SLOTS, ADA_CHUNK)
        adarow = Z[0:4, z0 + 2048:z0 + 2560]
        ada_half = [zv(z0 + at, ADA_SLOTS, ADA_CHUNK) for at in (0, 2560, 4608)]
        cf = zv(z0 + 2560, 3, T)
        R2 = zv(z0 + 4096, T)
        cu = zv(z0 + 4608, 2, T)
        cy = zv(z0 + 5632, 2, T)
        kr = zv(z0 + 6656, T)
        assert z0 + 7168 <= 7680
        hf = zv(z0 + 2560, KD, T)
        fy, fs = cu, cy
        ff = zv(z0 + 2560, 2, T)
        Kb = zv(z0, 2, T)
        Qb = zv(z0 + 1024, 2, T)
        vT = zv(z0 + 2048, T)
        Vm = zv(z0 + 2560, 2, 4, MDV)
        Pc = zv(z0 + 3072, 2, C)
        Pl = zv(z0 + 3584, 2, T)
        Tc = zv(z0 + 4608, 2, C)
        Tl = zv(z0 + 5120, 4, C)
        OF = zv(z0 + 6144, T)
        mx = zv(z0 + 6656, 4, 4)
        gq = zv(z0, 2, T)
        gk = zv(z0 + 1024, 2, T)
        gV = zv(z0 + 2048, 4, DV)
        gvT = zv(z0 + 2560, T)
        gr = zv(z0 + 3072, T)
        gx = zv(z0 + 3584, T)
        gE = zv(z0 + 4096, T)
        gst = zv(z0 + 4608, T)
        gKT = zv(z0 + 5120, 4, P)
        gA = zv(z0 + 5632, 4, P)
        gS = zv(z0 + 6144, NCH, DV)
        assert z0 + 6144 + NCH * DV <= 7680

        scale = float(QK) ** -0.5

        raw_loaded = sems("raw_loaded", SLOTS)
        hi_ready = sems("hi_ready", SLOTS)
        lo_ready = sems("lo_ready", SLOTS)
        panel_done = sems("panel_done", SLOTS)
        bank_free = sems("bank_free", SLOTS)
        ada_first = sems("ada_first", 3)
        ada_loaded = sems("ada_loaded", ADA_SLOTS)
        ln_ahead = sem("ln_ahead")
        c_hi_ready = sem("c_hi_ready")
        c_lo_ready = sem("c_lo_ready")
        ada_hi = sem("ada_hi")
        ada_lo = sem("ada_lo")
        ada_sum = sem("ada_sum")
        ada_used = sem("ada_used")
        ada_row = sem("ada_row")
        ada_cols = sem("ada_cols")
        ada_mod = sem("ada_mod")
        consts_in = sem("consts_in")
        vecs_in = sem("vecs_in")
        tokens_in = sem("tokens_in")
        w2_zero = sem("w2_zero")
        w2_in = sem("w2_in")
        start_t = sem("start_t")
        start_c = sem("start_c")
        fin_t = sem("fin_t")
        fin_a = sem("fin_a")
        fin_v = sem("fin_v")
        stored = sem("stored")
        act_step = sem("act_step")
        dve_step = sem("dve_step")
        x_ready = sems("x_ready", 2)
        sq_ready = sem("sq_ready")
        sum_ready = sem("sum_ready")
        stat_ready = sem("stat_ready")
        rms_ready = sem("rms_ready")
        t_ready = sem("t_ready")
        hf_hi = sem("hf_hi")
        hf_full = sem("hf_full")
        h_ready = sem("h_ready")
        coef = sem("coef")
        m_ready = sem("m_ready")
        m_hi = sem("m_hi")
        m_lo = sem("m_lo")

        per_layer = {}

        def event(name, context_layer, last_layer=None):
            per_layer[name] = context_layer
            return sem(name)

        cf_sq = event("cf_sq", 3)
        c_stat = event("c_stat", 2)
        c_rms = event("c_rms", 2)
        c_norm = event("c_norm", 3)
        c_hi = event("c_hi", 3)
        c_lo = event("c_lo", 3)
        kr_act = event("kr_act", 1)
        kr_dve = event("kr_dve", 1)
        conv_mid = event("conv_mid", 4)
        cat_hi = event("cat_hi", 12)
        cat_lo = event("cat_lo", 12)
        a_q = event("a_q", MH)
        a_kv = event("a_kv", MH)
        q_act = event("q_act", MH)
        q_dve = event("q_dve", MH)
        k_act = event("k_act", MH)
        v_turned = event("v_turned", MH)
        v_act = event("v_act", MH)
        scored = event("scored", 4 * MH)
        max_ready = event("max_ready", MH)
        exped = event("exped", 4 * MH)
        p_ready = event("p_ready", 4 * MH)
        p_turned = event("p_turned", 3 * MH)
        pt_act = event("pt_act", 2 * MH)
        pt_dve = event("pt_dve", MH)
        o_done = event("o_done", MH)
        o_act = event("o_act", MH)
        z_done = event("z_done", GH)
        z_exp = event("z_exp", GH)
        z_ln = event("z_ln", GH)
        b_ready = event("b_ready", GH)
        e_ready = event("e_ready", GH)
        k_decayed = event("k_decayed", GH)
        q_decayed = event("q_decayed", GH)
        kst_ready = event("kst_ready", GH)
        g_turned = event("g_turned", 2 * GH)
        g_turned_act = event("g_turned_act", 2 * GH)
        ga_done = event("ga_done", GH)
        ga_masked = event("ga_masked", GH)
        gu_done = event("gu_done", 2 * GH)
        gs_ready = event("gs_ready", GH)
        go_done = event("go_done", GH)
        go_sq = event("go_sq", GH)
        g_stat = event("g_stat", GH)
        g_rms = event("g_rms", GH)
        r_tanh = event("r_tanh", GH)
        go_norm = event("go_norm", GH)
        f_mid = event("f_mid", KF)
        f_tanh = event("f_tanh", KF)
        f_hi = event("f_hi", KF)
        f_lo = event("f_lo", KF)

        def at(name, l, value):
            return value + per_layer[name] * l

        def ada_units(l, n):
            if l == 0 and n >= 0:
                return [(ADA_FIRST + n // 2, k) for k in range(4 * (n % 2), 4 * (n % 2) + 4)]
            return [(2 * ADA_TURNS - 1, n - 8)] if l > 0 and n >= 8 else []

        def ada_ends(l, n):
            return next((turn for turn, k in ada_units(l, n) if k == KD - 1), None)

        def chunk_of(turn):
            return turn // ADA_TURNS, turn % ADA_TURNS

        def ada_tiles(k, stage):
            if stage == "first":
                return ahi[:, k, :], alo[:, k, :]
            if stage == "projection":
                return ahi[:, 4 + k % 4, :], alo[:, 4 + k % 4, :]
            return chi[:, k % 3, :], clo[:, k % 3, :]

        def ada_before(k, stage):
            if stage == "first":
                return KD
            if stage == "projection":
                return 4
            return 3 if k >= 3 else 2 if k < 2 else 5

        block = stack.enter_context(nc.Block())

        def q0(l):
            return 0 if l < L - 1 else C

        def streams(l):
            return [0, 1] if l < L - 1 else [1]

        def cols(st):
            return slice(C * st, C * st + C)

        def seg(ap, l):
            return ap.rearrange("p (s n) -> p s n", n=C)[:, q0(l) // C:, :]

        def flat(ap):
            return ap.rearrange("p a n -> p (a n)")

        def scan_order(back):
            if not back:
                return list(range(NCH))
            h = NCH // 2
            return list(range(h - 1, -1, -1)) + list(range(NCH - 1, h - 1, -1))

        def parts(l):
            return [(sum(FF_PARTS[:n]), FF_PARTS[n]) for n in range(len(FF_PARTS))]

        @block.sync
        def _(sp):
            st = Stream()

            def slot_of(p):
                if not (isinstance(p.turn, int) and p.turn == 0):
                    sp.wait_ge(lo_ready[p.slot], p.turn)
                return raw[:, p.slot]

            def load(p, src):
                sp.dma_start(slot_of(p)[:, 0:p.nk, :], src.rearrange("(k p) n -> p k n", p=P)) \
                    .then_inc(raw_loaded[p.slot], 16)

            def load_ada(l, chunk, k, turn):
                slot = k % ADA_SLOTS
                sp.wait_ge(ada_lo, turn * KD + (k - ADA_SLOTS + 1))
                sp.dma_start(adaw[:, slot, :],
                             w_ada[l, k * P:(k + 1) * P, bass.ds(chunk * ADA_CHUNK, ADA_CHUNK)]) \
                    .then_inc(ada_loaded[slot], 16)

            def swapped(dst, src, sem_):
                for half in range(2):
                    for axis in range(2):
                        to, fro = axis * 16 + half * 8, axis * 16 + (1 - half) * 8
                        sp.dma_start(dst[:, :, to:to + 8], src[:, :, fro:fro + 8]).then_inc(sem_, 16)

            tok = flat(M[:, :, :]).rearrange("p (t d) -> p t d", t=4)
            sp.dma_start(tok[:, 0:2, :], ctx[0].rearrange("(t p) d -> p t d", p=P)).then_inc(tokens_in, 16)
            sp.dma_start(tok[:, 2:4, :], x[0].rearrange("(t p) d -> p t d", p=P)).then_inc(tokens_in, 16)

            def load_w2(l):
                if l == 0:
                    sp.wait_ge(w2_zero, 1)
                else:
                    sp.wait_ge(z_done, at("z_done", l, 0))
                for way in range(2):
                    sp.dma_start(W2[way * RANK:(way + 1) * RANK, :, way * DK:(way + 1) * DK],
                                 w_gk2[l, way].rearrange("r (h k) -> r h k", h=GH)).then_inc(w2_in, 16)

            for n in range(2 * ADA_FIRST):
                if n == 1:
                    sp.wait_ge(vecs_in, 16 * VEC_DMAS)
                if n == 6:
                    for col, p in zip(PROJ_COLUMNS, st.peek(PROJ[0:EARLY])):
                        load(p, w_in[0][:, col:col + P])
                if n >= 3:
                    sp.wait_ge(ada_lo, 4 * (n - 3) + 4)
                k = 4 * (n % 2)
                sp.dma_start(ada_half[n % 3],
                             w_ada[0, k * P:(k + 4) * P, n // 2 * ADA_CHUNK:(n // 2 + 1) * ADA_CHUNK]
                             .rearrange("(k p) n -> p k n", p=P)).then_inc(ada_first[n % 3], 16)
            load_w2(0)

            for l in range(L):
                ps = st.take(PROJ)
                for n, p in enumerate(ps):
                    for turn, k in ada_units(l, n - (SLOTS if l == 0 else 0)):
                        load_ada(*chunk_of(turn), k, turn)
                    if l == 0 and n < EARLY:
                        continue
                    if PROJ_COLUMNS[n] is not None:
                        load(p, w_in[l][:, PROJ_COLUMNS[n]:PROJ_COLUMNS[n] + P])
                    else:
                        dst = slot_of(p)
                        w = w_in[l].rearrange("(k p) n -> p k n", p=P)
                        sp.dma_start(dst[:, :, 0:ROPE], w[:, :, O_LR:O_LR + 2 * RANK]) \
                            .then_inc(raw_loaded[p.slot], 16)
                        sp.dma_start(dst[:, :, ROPE:2 * ROPE], w[:, :, O_KR:O_KR + ROPE]) \
                            .then_inc(raw_loaded[p.slot], 16)
                        sp.dma_start(dst[:, :, 2 * ROPE:3 * ROPE], w[:, :, O_KR:O_KR + ROPE]) \
                            .then_inc(raw_loaded[p.slot], 16)
                        swapped(dst[:, :, 3 * ROPE:], w[:, :, O_KR:O_KR + ROPE], raw_loaded[p.slot])
                for n in range(len(ps) - SLOTS, len(ps)) if l == 0 else ():
                    for turn, k in ada_units(l, n):
                        load_ada(*chunk_of(turn), k, turn)
                with sp.Fori(0, MH // 2) as i:
                    for p in st.body(i, MLA_BODY):
                        h = i * 2 + p.slot // 2
                        if p.slot % 2 == 0:
                            wc = w_br_c[l][:, bass.ds(h * P, P)].rearrange("(k p) n -> p k n", p=P)
                            wq = w_uq[l].rearrange("(k p) n -> p k n", p=P)
                            wr = wq[:, :, bass.ds(h * QK + NOPE, ROPE)]
                            wq = wq[:, :, bass.ds(h * QK, QK)]
                            wkv = w_ukv[l][:, bass.ds(h * P, P)]
                            dst = slot_of(p)
                            for part, src in ((dst[:, 0:4, :], wc), (dst[:, 4:6, 0:QK], wq), (dst[:, 6, :], wkv)):
                                sp.dma_start(part, src).then_inc(raw_loaded[p.slot], 16)
                            swapped(dst[:, 4:6, QK:P], wr, raw_loaded[p.slot])
                        else:
                            load(p, w_in[l][:, bass.ds(h * P + (O_G + BR_C * D), P)])
                st.skip(MH // 2, MLA_BODY)
                if l > 0:
                    load_w2(l)
                ps = iter(st.take(GLA))
                for h in range(GH):
                    if h % 2 == 0:
                        load(next(ps), w_in[l][:, O_Q + h * DK:O_Q + h * DK + P])
                        load(next(ps), w_in[l][:, O_K + h * DK:O_K + h * DK + P])
                    load(next(ps), w_in[l][:, O_V + h * DV:O_V + h * DV + P])
                    load(next(ps), w_in[l][:, O_R + h * DV:O_R + h * DV + P])
                    for j in (2 * h, 2 * h + 1):
                        load(next(ps), w_in[l][:, O_G + BR_B * D + j * P:O_G + BR_B * D + (j + 1) * P])
                        load(next(ps), w_br_b[l][:, j * P:(j + 1) * P])
                with sp.Fori(0, KD // 2) as i:
                    for p in st.body(i, GATE_BODY):
                        j = i * 2 + p.slot // 2
                        if p.slot % 2 == 0:
                            load(p, w_in[l][:, bass.ds(i * (2 * P) + (p.slot // 2 * P + O_G + BR_A * D), P)])
                        else:
                            load(p, w_br_a[l][:, bass.ds(j * P, P)])
                st.skip(KD // 2, GATE_BODY)
                with sp.Fori(0, KD // SLOTS) as i:
                    for p in st.body(i, UP_BODY):
                        load(p, w_o[l][:, bass.ds(i * (SLOTS * P) + p.slot * P, P)])
                st.skip(KD // SLOTS, UP_BODY)
                for n, (off, tiles) in enumerate(parts(l)):
                    with sp.Fori(0, tiles // 2) as i:
                        for p in st.body(i, UP_BODY):
                            w = w_ffn_gate if p.slot % 2 == 0 else w_ffn_up
                            load(p, w[l][:, bass.ds(i * (2 * P) + (off + p.slot // 2) * P, P)])
                        if l == 0:
                            for k in range(KD):
                                load_ada(1, i + off // 2, k, i + (12 + off // 2))
                    st.skip(tiles // 2, UP_BODY)
                    with sp.Fori(0, KD // SLOTS) as i:
                        for p in st.body(i, down_body(n)):
                            load(p, w_ffn_down[l][off * P:(off + tiles) * P,
                                                  bass.ds(i * (SLOTS * P) + p.slot * P, P)])
                    st.skip(KD // SLOTS, down_body(n))
            for t in range(2):
                sp.wait_ge(fin_a if t else fin_v, 2)
                sp.dma_start(out[0, t * P:(t + 1) * P, :], Z[:, t * D:(t + 1) * D]).then_inc(stored, 16)
            sp.wait_ge(stored, 32)

        @block.tensor
        def _(pe):
            st = Stream()
            ident = K[:, K_ID:K_ID + P]

            def weights(p):
                pe.wait_ge(lo_ready[p.slot], p.turn + 1)

            def bank_of(p):
                if not (isinstance(p.turn, int) and p.turn == 0):
                    pe.wait_ge(bank_free[p.slot], p.turn)
                return bank[p.slot]

            def mm3(dst, p, ks, rhi, rlo, before=None):
                for n, k in enumerate(ks):
                    if before is not None:
                        before(n)
                    hi, lo = whi[:, p.slot, k, :], wlo[:, p.slot, k, :]
                    pe.matmul(dst, hi, rlo(n), start=(n == 0), stop=False)
                    pe.matmul(dst, hi, rhi(n), start=False, stop=False)
                    last = pe.matmul(dst, lo, rhi(n), start=False, stop=(n == len(ks) - 1))
                return last

            def project(p, first, before=None):
                weights(p)
                mm3(bank_of(p)[:, first:T], p, range(KD), lambda k: hhi[:, k, first:T],
                    lambda k: hlo[:, k, first:T], before).then_inc(panel_done[p.slot], 1)

            def project_pair(pair, first, m):
                for p in pair:
                    weights(p)
                dst = [bank_of(p)[:, first:T] for p in pair]
                for k in range(KD):
                    pe.wait_ge(hf_hi, 8 * m + k + 1)
                    for p, d in zip(pair, dst):
                        pe.matmul(d, whi[:, p.slot, k, :], hhi[:, k, first:T], start=(k == 0), stop=False)
                        pe.matmul(d, wlo[:, p.slot, k, :], hhi[:, k, first:T], start=False, stop=False)
                    pe.wait_ge(h_ready, 8 * m + k + 1)
                    for p, d in zip(pair, dst):
                        last = pe.matmul(d, whi[:, p.slot, k, :], hlo[:, k, first:T], start=False,
                                         stop=(k == KD - 1))
                        if k == KD - 1:
                            last.then_inc(panel_done[p.slot], 1)

            def branch(p, tile0, first):
                weights(p)
                mm3(bank_of(p)[:, first:T], p, range(4), lambda k: ahi[:, tile0 + k, first:T],
                    lambda k: alo[:, tile0 + k, first:T]).then_inc(panel_done[p.slot], 1)

            def ada_unit(k, turn, stage):
                if k == 0:
                    if not (isinstance(turn, int) and turn == 0):
                        pe.wait_ge(ada_row, turn)
                pe.wait_ge(ada_lo, turn * KD + (k + 1))
                hi, lo = ada_tiles(k, stage)
                pe.matmul(bank[7][0:4, :], csr[:, k, :], hi, start=(k == 0), stop=False)
                pe.matmul(bank[7][0:4, :], csr[:, k, :], lo, start=False, stop=(k == KD - 1)) \
                    .then_inc(ada_used, 1)

            def ada_wait(turn):
                pe.wait_ge(ada_row, turn + 1)
                if not (isinstance(turn, int) and turn == 0):
                    pe.wait_ge(ada_mod, turn)

            def ada_turn(turn):
                for m in range(4):
                    last = pe.transpose(bank[6][:, 4 * m:4 * m + 4], adarow[:, m * P:(m + 1) * P],
                                        ident[0:4, 0:4])
                last.then_inc(ada_cols, 1)

            def norm_stat(m, first):
                pe.wait_ge(sum_ready, m)
                pe.matmul(bank[4][:, first:T], ones[:, :], M[:, 0, first:T], start=True, stop=True) \
                    .then_inc(stat_ready, 1)

            pe.wait_ge(consts_in, 16)
            pe.wait_ge(vecs_in, 16 * VEC_DMAS)
            for n, rows in enumerate(vec_rows):
                last = pe.transpose(bank[5][:, n * 96:n * 96 + rows], vec_in[n][0:rows, :],
                                    ident[0:rows, 0:rows])
            last.then_inc(start_t, 1)
            pe.wait_ge(tokens_in, 32)
            tok = flat(M[:, :, :]).rearrange("p (t d) -> p t d", t=4)
            for k in range(KD):
                if k >= 4:
                    pe.wait_ge(x_ready[k % 2], k // 2 - 1)
                for t in range(4):
                    last = pe.transpose(bank[k % 4][:, t * P:(t + 1) * P], tok[:, t, k * P:(k + 1) * P],
                                        ident)
                last.then_inc(start_t, 1)
            pe.wait_ge(c_lo_ready, 1)
            for turn in range(ADA_FIRST):
                if turn == 2:
                    for k in range(KD):
                        pe.wait_ge(sq_ready, k + 1)
                        last = pe.matmul(bank[4][:, :], ones[:, :], M[:, k, :], start=(k == 0), stop=(k == KD - 1))
                    last.then_inc(stat_ready, 1)
                for k in range(KD):
                    ada_unit(k, turn, "first")
                ada_wait(turn)
                ada_turn(turn)

            for l in range(L):
                first = q0(l)
                if l > 0:
                    norm_stat(2 * l, 0)
                ps = st.take(PROJ)
                for n, p in enumerate(ps):
                    if n == 0:
                        project_pair(ps[0:2], first, 2 * l)
                    elif n > 1:
                        for turn, k in ada_units(l, n):
                            ada_unit(k, turn, "projection")
                        project(p, 0 if n in (2, 3) else first)
                    if n == 4:
                        pe.wait_ge(cf_sq, at("cf_sq", l, 3))
                        pe.matmul(bank[4][:, first:T], ones[:, :], cy[:, 0, first:T], start=True, stop=False)
                        pe.matmul(bank[4][:, first:T], ones[:, :], cy[:, 1, first:T], start=False, stop=True) \
                            .then_inc(c_stat, 1)
                        pe.matmul(bank[5][:, :], ones[:, :], cu[:, 0, :], start=True, stop=True) \
                            .then_inc(c_stat, 1)
                    turn = ada_ends(l, 1 if n == 2 else n)
                    if turn is not None and n > 1:
                        ada_wait(turn)
                        ada_turn(turn)
                    if n == 1:
                        for m in (0, 1):
                            for turn, k in ada_units(l, m):
                                ada_unit(k, turn, "projection")
                pe.wait_ge(c_lo, at("c_lo", l, 3))
                nt = 4 if l == 0 else 2
                nb = 3 if l == 0 else 2
                with pe.Fori(0, MH // 2) as i:
                    ps = st.body(i, MLA_BODY)

                    def heads(e):
                        return i * 2 + (e + 1)

                    def project_head(e):
                        p = ps[2 * e]
                        weights(p)
                        mm3(bank[4][:, first:T], p, (4, 5), lambda k: chi[:, k, first:T],
                            lambda k: clo[:, k, first:T]).then_inc(a_q, 1)
                        mm3(bank[5][:, :], p, (6,), lambda k: chi[:, 2, :], lambda k: clo[:, 2, :]) \
                            .then_inc(a_kv, 1)

                    def score(e):
                        pe.wait_ge(kr_dve, at("kr_dve", l, 1))
                        pe.wait_ge(k_act, heads(e) + at("k_act", l, 0))
                        pe.wait_ge(q_act, heads(e) + at("q_act", l, 0))
                        pe.wait_ge(q_dve, heads(e) + at("q_dve", l, 0))
                        if e == 0:
                            pe.wait_ge(cat_hi, i + at("cat_hi", l, 4))
                        else:
                            pe.wait_ge(o_act, i * 2 + at("o_act", l, 1))
                        for t in range(2):
                            pe.matmul(bank[4 + t][:, :], Qb[0:QK, e, C + t * P:C + (t + 1) * P], Kb[0:QK, e, :],
                                      start=True, stop=True).then_inc(scored, 1)
                        if l == 0:
                            for t in range(2):
                                pe.matmul(bank[7][:, t * C:(t + 1) * C], Qb[0:QK, e, t * P:(t + 1) * P],
                                          Kb[0:QK, e, 0:C], start=True, stop=True).then_inc(scored, 1)
                        for t in range(4):
                            last = pe.transpose(bank[6][:, t * MDV:(t + 1) * MDV], vT[MDV:2 * MDV, t * P:(t + 1) * P],
                                                ident[MDV:2 * MDV, MDV:2 * MDV])
                        last.then_inc(v_turned, 1)

                    def values(e):
                        for n, (k, t) in enumerate(((0, 0), (1, 0), (0, 1), (1, 1), (2, 0), (2, 1), (3, 0), (3, 1))):
                            if n in (0, 2):
                                pe.wait_ge(p_ready, i * (2 * nt) + (at("p_ready", l, 0) + e * nt + t + 1))
                            at_ = (k % 2) * C + t * P
                            last = pe.transpose(bank[4 + k // 2][:, at_:at_ + P],
                                                Pl[:, t, k * P:(k + 1) * P], ident)
                            if k % 2 and t:
                                last.then_inc(p_turned, 1)
                        if l == 0:
                            pe.wait_ge(p_ready, heads(e) * nt + at("p_ready", l, 0))
                            for k in range(2):
                                for t in range(2):
                                    last = pe.transpose(bank[7][:, k * C + t * P:k * C + (t + 1) * P],
                                                        Pc[:, t, k * P:(k + 1) * P], ident)
                            last.then_inc(p_turned, 1)
                        pe.wait_ge(v_act, heads(e) + at("v_act", l, 0))
                        pe.wait_ge(pt_act, i * (2 * (nb - 1)) + (at("pt_act", l, 0) + e * (nb - 1) + 1))
                        for k in range(4):
                            if k == 2:
                                pe.wait_ge(pt_dve, heads(e) + at("pt_dve", l, 0))
                            last = pe.matmul(bank[6][0:MDV, C:T], Vm[:, e, k, :], Tl[:, k, :],
                                             start=(k == 0), stop=(k == 3))
                        if l == 0:
                            pe.wait_ge(pt_act, heads(e) * 2 + at("pt_act", l, 0))
                            for k in range(2):
                                last = pe.matmul(bank[6][0:MDV, 0:C], Vm[:, e, k, :], Tc[:, k, :],
                                                 start=(k == 0), stop=(k == 1))
                        last.then_inc(o_done, 1)

                    for e in range(2):
                        project_head(e)
                        pe.wait_ge(cat_lo, at("cat_lo", l, 4))
                        branch(ps[2 * e], 0, first)
                        score(e)
                        project(ps[2 * e + 1], first)
                        values(e)
                st.skip(MH // 2, MLA_BODY)
                pe.wait_ge(w2_in, 32 * (l + 1))
                ps = iter(st.take(GLA))
                chunks = range(first // CHUNK, NCH)

                def decay_logits(h):
                    pe.matmul(bank[4][:, :], W2[:, h, :], LR, start=True, stop=True).then_inc(z_done, 1)

                def output_stat(h):
                    pe.wait_ge(go_sq, at("go_sq", l, h + 1))
                    pe.matmul(bank[7][:, first:T], ones[:, :], gvT[:, first:T], start=True, stop=True) \
                        .then_inc(g_stat, 1)

                pe.wait_ge(pt_act, at("pt_act", l, (nb - 1) * MH))
                decay_logits(0)
                for h in range(GH):
                    e = h % 2
                    if e == 0:
                        project(next(ps), first)
                        if h > 0:
                            output_stat(h - 1)
                        project(next(ps), 0)
                    pv = next(ps)
                    project(pv, 0)
                    if e == 1:
                        output_stat(h - 1)
                    project(next(ps), first)
                    project(next(ps), first)
                    pe.wait_ge(bank_free[pv.slot], pv.turn + 1)
                    for t in range(4):
                        last = pe.transpose(bank[5][:, t * P:(t + 1) * P], gvT[:, t * P:(t + 1) * P], ident)
                    last.then_inc(g_turned, 1)
                    pe.wait_ge(kst_ready, at("kst_ready", l, h + 1))
                    if h > 0:
                        pe.wait_ge(go_norm, at("go_norm", l, h))
                    for t in range(4):
                        last = pe.transpose(bank[6][:, t * P:(t + 1) * P], gst[:, t * P:(t + 1) * P], ident)
                    last.then_inc(g_turned, 1)
                    pe.wait_ge(q_decayed, at("q_decayed", l, h + 1))
                    for n in chunks:
                        for way in range(2):
                            r = slice(way * DK, (way + 1) * DK)
                            o = slice((n % 2) * CHUNK, (n % 2 + 1) * CHUNK)
                            at_ = (n // 2) * CHUNK
                            tk = slice(n * CHUNK, (n + 1) * CHUNK)
                            last = pe.matmul(bank[7 if way else 4][o, at_:at_ + CHUNK], gk[r, e, tk], gq[r, e, tk],
                                             start=True, stop=True)
                    last.then_inc(ga_done, 1)
                    if h == 0:
                        pe.wait_ge(cat_lo, at("cat_lo", l, 8))
                    branch(next(ps), 4, first)
                    pe.wait_ge(g_turned_act, at("g_turned_act", l, 2 * h + 2))
                    pe.wait_ge(ga_masked, at("ga_masked", l, h + 1))
                    for n in range(NCH):
                        o = slice((n % 2) * CHUNK, (n % 2 + 1) * CHUNK)
                        last = pe.matmul(bank[4 + n % 2][:, (n // 2) * DV:(n // 2 + 1) * DV],
                                         gKT[o, n // 2, :], gV[o, n // 2, :], start=True, stop=True)
                        if n >= NCH - 2:
                            last.then_inc(gu_done, 1)
                    project(next(ps), first)
                    branch(next(ps), 4, first)
                    for n in range(first // P, T // P):
                        pe.matmul(bank[6][:, n * P:(n + 1) * P], gV[:, n, :], gA[:, n, :],
                                  start=(n == first // P), stop=False, skip_group_check=True)
                    pe.wait_ge(gs_ready, at("gs_ready", l, h + 1))
                    if h + 1 < GH:
                        decay_logits(h + 1)
                    for n in chunks:
                        tk = slice(n * CHUNK, (n + 1) * CHUNK)
                        last = pe.matmul(bank[6][:, tk], gS[:, n, :], gq[:, e, tk], start=False,
                                         stop=(n == NCH - 1), skip_group_check=True)
                    last.then_inc(go_done, 1)
                output_stat(GH - 1)
                with pe.Fori(0, KD // 2) as i:
                    for n, p in enumerate(st.body(i, GATE_BODY)):
                        if n % 2 == 0:
                            project(p, first)
                        else:
                            pe.wait_ge(cat_lo, at("cat_lo", l, 12))
                            branch(p, 0, first)
                st.skip(KD // 2, GATE_BODY)
                with pe.Fori(0, KD // SLOTS) as i:
                    for n, p in enumerate(st.body(i, UP_BODY)):
                        project(p, first, (lambda k: pe.wait_ge(m_lo, 8 * l + k + 1)) if n == 0 else None)
                st.skip(KD // SLOTS, UP_BODY)
                norm_stat(2 * l + 1, first)
                for n, (off, tiles) in enumerate(parts(l)):
                    def hidden(i, stream_arrives):
                        turn = i + (ADA_TURNS + off // 2)
                        ps = st.body(i, UP_BODY)

                        def units(ks):
                            if l == 0:
                                for k in ks:
                                    ada_unit(k, turn, "FFN")

                        if stream_arrives:
                            project_pair(ps[0:2], first, 2 * l + 1)
                            units((0, 1, 2))
                            project(ps[2], first)
                            units((3, 4, 5))
                            project(ps[3], first)
                            units((6, 7))
                        else:
                            project(ps[0], first)
                            units((0, 1, 2))
                            project(ps[1], first)
                            units((3, 4, 5))
                            project(ps[2], first)
                            units((6, 7))
                        if stream_arrives:
                            if l == 0:
                                ada_wait(turn)
                        else:
                            project(ps[3], first, lambda k: ada_wait(turn) if l == 0 and k == 4 else None)
                        if l == 0:
                            ada_turn(turn)

                    if n == 0:
                        hidden(0, True)
                    with pe.Fori(1 if n == 0 else 0, tiles // 2) as i:
                        hidden(i, False)
                    st.skip(tiles // 2, UP_BODY)
                    with pe.Fori(0, KD // SLOTS) as i:
                        for m, p in enumerate(st.body(i, down_body(n))):
                            weights(p)
                            before = (lambda k: pe.wait_ge(f_lo, at("f_lo", l, off + k + 1))) if m == 0 else None
                            mm3(bank_of(p)[:, first:T], p, range(tiles), lambda k: ahi[:, k, first:T],
                                lambda k: alo[:, k, first:T], before).then_inc(panel_done[p.slot], 1)
                    st.skip(KD // SLOTS, down_body(n))
            norm_stat(2 * L, C)
            for k in range(KD):
                pe.wait_ge(h_ready, 8 * 2 * L + k + 1)
                for t in range(2):
                    last = pe.transpose(bank[2 * t + k // 4][:, (k % 4) * P:(k % 4 + 1) * P],
                                        M[:, k, C + t * P:C + (t + 1) * P], ident)
                    if k % 4 == 3:
                        last.then_inc(fin_t, 1)

        @block.scalar
        def _(act):
            st = Stream()
            steps = Steps(act, act_step)

            def split(p):
                act.wait_ge(raw_loaded[p.slot], p.loaded)
                if not (isinstance(p.turn, int) and p.turn == 0):
                    act.wait_ge(panel_done[p.slot], p.turn)
                act.activation(whi[:, p.slot, 0:p.nk, :], raw[:, p.slot, 0:p.nk, :], ACT.Copy) \
                    .then_inc(hi_ready[p.slot], 1)

            def full(p):
                act.wait_ge(panel_done[p.slot], p.turn + 1)
                return bank[p.slot]

            def emptied(p):
                act.wait_ge(bank_free[p.slot], p.turn + 1)

            def gate(p, e, first):
                act.activation(TB[:, e, first:T], full(p)[:, first:T], ACT.Tanh, scale=0.5) \
                    .then_inc(bank_free[p.slot], 1)

            def ada_out(turn):
                act.wait_ge(ada_used, (turn + 1) * KD)
                if not (isinstance(turn, int) and turn == 0):
                    act.wait_ge(ada_cols, turn)
                act.activation(adarow, bank[7][0:4, :], ACT.Copy).then_inc(ada_row, 1)

            def ada_split(k, turn, stage):
                if stage == "first":
                    n = 2 * turn + k // 4
                    if k % 4 == 0:
                        act.wait_ge(ada_first[n % 3], 16 * (n // 3 + 1))
                    src = ada_half[n % 3][:, k % 4, :]
                else:
                    act.wait_ge(ada_loaded[k % ADA_SLOTS], (turn - ADA_FIRST) * 32 + 16 * (k // 4 + 1))
                    src = adaw[:, k % ADA_SLOTS, :]
                if stage != "first" or turn > 0:
                    act.wait_ge(ada_used, turn * KD + (k + 1 - ada_before(k, stage)))
                act.activation(ada_tiles(k, stage)[0], src, ACT.Copy).then_inc(ada_hi, 1)

            def inverse_root(dst, src, n):
                steps.link(act.activation(dst, src, ACT.Ln, scale=1.0 / n, bias=eps[:, :]))
                return act.activation(dst, dst, ACT.Exp, scale=-0.5)

            def square(k, first):
                act.activation(M[:, k, first:T], X[:, k, first:T], ACT.Square).then_inc(sq_ready, 1)

            def root(m, first):
                if m > 0:
                    act.wait_ge(ln_ahead, m)
                act.activation(ln_out[:, :], ones[:, 0:1], ACT.Ln).then_inc(ln_ahead, 1)
                act.wait_ge(stat_ready, m + 1)
                inverse_root(R[:, first:T], bank[4][:, first:T], D).then_inc(rms_ready, 1)

            def norm(m, l, w, first):
                act.wait_ge(coef, 2 * l + w + 1)
                for k in range(KD):
                    act.wait_ge(t_ready, 8 * m + k + 1)
                    for s_ in range(first // C, 2):
                        last = act.activation(hhi[:, k, cols(s_)], M[:, k, cols(s_)], ACT.Identity,
                                              scale=am[:, l, w, k, s_:s_ + 1],
                                              bias=mod[:, l, (SH2 if w else SH1) + k, s_:s_ + 1])
                    last.then_inc(hf_hi, 1)

            act.dma_start(K[:, :], consts).then_inc(consts_in, 16)
            n = 0
            for rows, src in ((VC_CTX, c_ctx), (VC_LAT, c[0]), (VC_FIN, final_norm_g)):
                act.dma_start(vec_in[4][rows:rows + KD, :], src.rearrange("(a b) -> a b", b=P)) \
                    .then_inc(vecs_in, 16)
                n += 1

            def both(at_, rows, count):
                return flat(TB[:, :, :])[rows:rows + count, at_ * P:(at_ + L) * P] \
                    .rearrange("p (l n) -> p l n", l=L)

            for at_, rows, src in ((0, V_ADA, b_ada), (0, V_N1, norm1_g), (0, V_N2, norm2_g), (0, V_GN, gla_norm_g),
                                   (0, V_QN, mla_q_norm_g), (0, V_KN, mla_kv_norm_g),
                                   (0, V_SC, sc_w.rearrange("l a b -> l (a b)")),
                                   (L, V_FW, ffn_conv_w.rearrange("l a b -> l (a b)")), (L, V_FB, ffn_conv_b)):
                count = src.shape[1] // P
                act.dma_start(both(at_, rows, count), src.rearrange("l (a b) -> a l b", b=P)).then_inc(vecs_in, 16)
                n += 1
            for way in range(2):
                act.dma_start(both(0, V_GK, GH)[:, :, way * DK:(way + 1) * DK],
                              b_gk2[:, way].rearrange("l (h k) -> h l k", h=GH)).then_inc(vecs_in, 16)
                n += 1
            assert n == VEC_DMAS
            for turn in range(ADA_FIRST):
                for k in range(KD):
                    ada_split(k, turn, "first")
                    if k == 1 and turn > 0:
                        ada_out(turn - 1)
                    if k == 3 and turn == 0:
                        act.wait_ge(start_t, 1)
                        for s_, row in ((0, VC_CTX), (1, VC_LAT)):
                            last = act.activation(cs[:, :, s_], bank[5][:, 4 * 96 + row:4 * 96 + row + KD], ACT.Silu)
                        last.then_inc(start_c, 1)
                        act.wait_ge(start_c, 1)
                        act.activation(csr[:, :, 0:2], cs[:, :, :], ACT.Copy).then_inc(c_hi_ready, 1)
                        for m in range(0, KD, 2):
                            act.wait_ge(start_t, m + 2)
                            act.activation(X[:, m, :], bank[m % 4][:, :], ACT.Copy).then_inc(x_ready[0], 1)
                if turn == 2:
                    root(0, 0)
                    for p in st.peek(PROJ)[0:AHEAD]:
                        split(p)
            ada_out(ADA_FIRST - 1)

            for l in range(L):
                first = q0(l)
                if l > 0:
                    root(2 * l, 0)
                norm(2 * l, l, 0, 0)
                ps = st.take(PROJ)
                ahead = ps + st.peek(MLA_BODY)[0:AHEAD]
                split(ahead[AHEAD])
                for n, p in enumerate(ps):
                    if n == 0:
                        split(ahead[AHEAD + 1])
                    for m in ((0, 1) if n == 0 else (n + 1,)) if l == 0 else (n + 3,):
                        if m < len(ps):
                            for turn, k in ada_units(l, m):
                                ada_split(k, turn, "projection")
                    if n > 1:
                        split(ahead[n + AHEAD])
                    if ada_ends(l, n) is not None:
                        ada_out(ada_ends(l, n))
                    if n < 3:
                        f = 0 if n == 2 else first
                        src = full(p)[:, f:T]
                        act.activation(cf[:, n, f:T], src, ACT.Copy)
                        act.activation(cy[:, n, f:T] if n < 2 else cu[:, 0, :], src, ACT.Square) \
                            .then_inc(cf_sq, 1)
                        act.wait_ge(cf_sq, at("cf_sq", l, n + 1))
                        act.sem_inc(bank_free[p.slot], 1)
                    elif n == 3:
                        full(p)
                        act.activation(LR, bank[p.slot][0:2 * RANK, :], ACT.Copy)
                        act.activation(kr[NOPE:QK, 0:C], bank[p.slot][NOPE:QK, 0:C], ACT.Copy).then_inc(kr_act, 1)
                    else:
                        j, what = (n - 4) // 3, (n - 4) % 3
                        if what == 0:
                            if j >= 2:
                                emptied(ps[n - 5])
                            act.activation(TB[:, j % 2, first:T], full(p)[:, first:T], ACT.Copy) \
                                .then_inc(bank_free[p.slot], 1)
                        elif what == 1:
                            emptied(p)
                            if j >= 2:
                                act.wait_ge(cat_lo, at("cat_lo", l, j - 1))
                            act.activation(cy[:, j % 2, first:T], cu[:, j % 2, first:T], ACT.Copy,
                                           scale=va[:, l, V_SC + 4 + j:V_SC + 5 + j]).then_inc(conv_mid, 1)
                        else:
                            emptied(p)
                            act.activation(ahi[:, j, first:T], cy[:, j % 2, first:T], ACT.Copy) \
                                .then_inc(cat_hi, 1)
                    if n == 4:
                        act.wait_ge(c_stat, at("c_stat", l, 2))
                        roots = (R[:, first:T], bank[4][:, first:T], QLORA), (R2, bank[5][:, :], KVLORA)
                        for dst, src, size in roots:
                            steps.link(act.activation(dst, src, ACT.Ln, scale=1.0 / size, bias=eps[:, :]))
                        for dst, _, _ in roots:
                            act.activation(dst, dst, ACT.Exp, scale=-0.5).then_inc(c_rms, 1)
                    if 7 <= n <= 9:
                        f = 0 if n == 9 else first
                        act.wait_ge(c_norm, at("c_norm", l, n - 6))
                        act.activation(chi[:, n - 7, f:T], cf[:, n - 7, f:T], ACT.Copy).then_inc(c_hi, 1)
                nt = 4 if l == 0 else 2

                def body(i, ps, after):
                    def heads(e):
                        return i * 2 + (e + 1)

                    def project_out(e):
                        act.wait_ge(a_q, heads(e) + at("a_q", l, 0))
                        if l == 0:
                            act.activation(Qb[0:QK, e, 0:C], bank[4][0:QK, 0:C], ACT.Copy)
                        act.activation(Qb[0:NOPE, e, C:T], bank[4][0:NOPE, C:T], ACT.Copy).then_inc(q_act, 1)
                        act.wait_ge(a_kv, heads(e) + at("a_kv", l, 0))
                        act.activation(Kb[0:NOPE, e, :], bank[5][0:NOPE, :], ACT.Copy)
                        act.activation(vT[NOPE:P, :], bank[5][NOPE:P, :], ACT.Copy).then_inc(k_act, 1)

                    def softmax(e):
                        act.wait_ge(v_turned, heads(e) + at("v_turned", l, 0))
                        act.activation(Vm[:, e, :, :], bank[6][:, 0:4 * MDV].rearrange("p (t n) -> p t n", t=4),
                                       ACT.Copy).then_inc(v_act, 1)
                        act.wait_ge(max_ready, heads(e) + at("max_ready", l, 0))
                        for t in range(nt):
                            src = bank[4 + t][:, :] if t < 2 else bank[7][:, (t - 2) * C:(t - 1) * C]
                            dst = Pl[:, t, :] if t < 2 else Pc[:, t - 2, :]
                            act.activation(dst, src, ACT.Exp, bias=mx[:, 1, t:t + 1], scale=scale,
                                           accum_out=mx[:, 2, t:t + 1]).then_inc(exped, 1)

                    def values_out(e):
                        nb = 3 if l == 0 else 2
                        act.wait_ge(p_turned, i * (2 * nb) + (at("p_turned", l, 0) + e * nb + 1))
                        act.activation(Tl[:, 0:2, :], bank[4][:, :].rearrange("p (k n) -> p k n", k=2), ACT.Copy) \
                            .then_inc(pt_act, 1)
                        if l == 0:
                            act.wait_ge(p_turned, i * (2 * nb) + (at("p_turned", l, 0) + e * nb + 3))
                            act.activation(Tc[:, :, :], bank[7][:, :].rearrange("p (k n) -> p k n", k=2), ACT.Copy) \
                                .then_inc(pt_act, 1)
                        act.wait_ge(bank_free[2 * e], ps[2 * e].turn)
                        gate(ps[2 * e + 1], e, first)
                        act.wait_ge(o_done, heads(e) + at("o_done", l, 0))
                        act.activation(OF[e * MDV:(e + 1) * MDV, first:T], bank[6][0:MDV, first:T], ACT.Copy) \
                            .then_inc(o_act, 1)

                    for e in range(2):
                        project_out(e)
                        split((ps + after)[2 * e + 2])
                        softmax(e)
                        split((ps + after)[2 * e + 3])
                        values_out(e)
                    act.wait_ge(o_act, i * 2 + (at("o_act", l, 2)))
                    act.activation(flat(ahi[:, bass.ds(i + 4, 1), first:T]), OF[:, first:T], ACT.Copy) \
                        .then_inc(cat_hi, 1)

                turns = MH // 2
                with act.Fori(0, turns - 1) as i:
                    body(i, st.body(i, MLA_BODY), st.body(i + 1, MLA_BODY))
                last_body = st.body(turns - 1, MLA_BODY)
                st.skip(turns, MLA_BODY)
                body(turns - 1, last_body, st.peek(GLA))

                ps = st.take(GLA)
                ahead = ps + st.peek(GATE_BODY)[0:AHEAD]
                of_branch = [p for p in ps if p.nk == 4]
                n = 0

                def exp_z(h):
                    act.wait_ge(z_done, at("z_done", l, h + 1))
                    bias = va[:, l, V_GK + h:V_GK + h + 1]
                    steps.link(act.activation(gL[:, :], bank[4][:, :], ACT.Abs, bias=bias))
                    act.activation(gL[:, :], gL[:, :], ACT.Exp, scale=-1.0).then_inc(z_exp, 1)

                def ln_z(h):
                    act.wait_ge(z_exp, at("z_exp", l, h + 1))
                    act.activation(gL[:, :], gL[:, :], ACT.Ln, bias=1.0).then_inc(z_ln, 1)

                def output_rms(h):
                    act.wait_ge(g_stat, at("g_stat", l, h + 1))
                    inverse_root(R[:, first:T], bank[7][:, first:T], DV).then_inc(g_rms, 1)

                def output_hi(h):
                    act.wait_ge(go_norm, at("go_norm", l, h + 1))
                    act.activation(ahi[:, h, first:T], gE[:, first:T], ACT.Copy, scale=0.5).then_inc(cat_hi, 1)

                exp_z(0)
                ln_z(0)
                for h in range(GH):
                    e = h % 2
                    if e == 0:
                        for dst, f, mul in ((gq, first, DK ** -0.5), (gk, 0, 1.0)):
                            split(ahead[n + AHEAD])
                            src = full(ps[n])
                            for eh in range(2):
                                for way in range(2):
                                    last = act.activation(dst[way * DK:(way + 1) * DK, eh, f:T],
                                                          src[eh * DK:(eh + 1) * DK, f:T], ACT.Copy, scale=mul)
                            last.then_inc(bank_free[ps[n].slot], 1)
                            n += 1
                            if dst is gq and h > 0:
                                output_rms(h - 1)
                    split(ahead[n + AHEAD])
                    if e == 1:
                        output_rms(h - 1)
                    act.activation(gvT[:, :], full(ps[n])[:, :], ACT.Copy).then_inc(bank_free[ps[n].slot], 1)
                    n += 1
                    split(ahead[n + AHEAD])
                    if h > 0:
                        output_hi(h - 1)
                    act.activation(gr[:, first:T], full(ps[n])[:, first:T], ACT.Tanh, scale=0.5) \
                        .then_inc(r_tanh, 1)
                    n += 1
                    act.wait_ge(b_ready, at("b_ready", l, h + 1))
                    if h > 0:
                        act.wait_ge(cat_lo, at("cat_lo", l, 8 + h))
                    act.activation(gE[:, :], gst[:, :], ACT.Exp, scale=1.0 / GATE_NORM)
                    act.activation(gx[:, :], gst[:, :], ACT.Exp, scale=-1.0 / GATE_NORM).then_inc(e_ready, 1)
                    split(ahead[n + AHEAD])
                    if h > 0:
                        emptied(of_branch[2 * h - 2])
                    gate(ps[n], 0, first)
                    n += 1
                    split(ahead[n + AHEAD])
                    n += 1
                    act.wait_ge(g_turned, at("g_turned", l, 2 * h + 1))
                    act.activation(gV[:, :, :], bank[5][:, :].rearrange("p (t n) -> p t n", t=4), ACT.Copy) \
                        .then_inc(g_turned_act, 1)
                    act.wait_ge(g_turned, at("g_turned", l, 2 * h + 2))
                    act.activation(gKT[:, :, :], bank[6][:, :].rearrange("p (t n) -> p t n", t=4), ACT.Copy) \
                        .then_inc(g_turned_act, 1)
                    split(ahead[n + AHEAD])
                    if h > 0:
                        emptied(of_branch[2 * h - 1])
                    gate(ps[n], 1, first)
                    n += 1
                    split(ahead[n + AHEAD])
                    n += 1
                    if h + 1 < GH:
                        exp_z(h + 1)
                    act.wait_ge(go_done, at("go_done", l, h + 1))
                    act.activation(gvT[:, first:T], bank[6][:, first:T], ACT.Square).then_inc(go_sq, 1)
                    if h + 1 < GH:
                        ln_z(h + 1)
                output_rms(GH - 1)
                output_hi(GH - 1)

                def gates(i, ps, after):
                    for e in range(2):
                        split((ps + after)[2 * e + 2])
                        if e == 0:
                            act.wait_ge(bank_free[1], ps[1].turn)
                        else:
                            act.wait_ge(bank_free[3], ps[3].turn)
                        gate(ps[2 * e], e, first)
                        split((ps + after)[2 * e + 3])

                turns = KD // 2
                with act.Fori(0, turns - 1) as i:
                    gates(i, st.body(i, GATE_BODY), st.body(i + 1, GATE_BODY)[0:AHEAD])
                last_body = st.body(turns - 1, GATE_BODY)
                st.skip(turns, GATE_BODY)
                gates(turns - 1, last_body, st.peek(UP_BODY)[0:AHEAD])
                act.wait_ge(panel_done[2], last_body[2].turn + 1)
                for k in range(KD):
                    act.wait_ge(m_ready, 8 * l + k + 1)
                    act.activation(hhi[:, k, first:T], M[:, k, first:T], ACT.Copy, scale=0.5).then_inc(m_hi, 1)

                def residual_stage(kinds, after, squares_from):
                    with act.Fori(0, KD // SLOTS - 1) as i:
                        for p in st.body(i, kinds)[AHEAD:] + st.body(i + 1, kinds)[0:AHEAD]:
                            split(p)
                    done = st.body(0, kinds) + st.body(1, kinds)
                    st.skip(KD // SLOTS, kinds)
                    ahead = done[SLOTS + AHEAD:] + (st.peek(after)[0:AHEAD] if after else [])
                    squared = 0
                    for n, p in enumerate(done[SLOTS:]):
                        if n < len(ahead):
                            split(ahead[n])
                        if squares_from is not None and n > 0:
                            for k in range(squared, SLOTS + n if n < SLOTS - 1 else KD):
                                emptied(done[k])
                                square(k, squares_from)
                                squared = k + 1

                residual_stage(UP_BODY, UP_BODY, first)
                root(2 * l + 1, first)
                norm(2 * l + 1, l, 1, first)
                for n, (off, tiles) in enumerate(parts(l)):
                    def hidden(i, ps, after):
                        def units(ks):
                            if l == 0:
                                for k in ks:
                                    ada_split(k, i + (ADA_TURNS + off // 2), "FFN")

                        for e in range(2):
                            pg, pu = ps[2 * e], ps[2 * e + 1]
                            if e == 0:
                                units((0, 1, 2))
                            t = i * 2 + (off + e)
                            act.activation(fy[:, e, first:T], full(pg)[:, first:T], ACT.Identity,
                                           scale=vb[:, l, bass.ds(t + (V_FW + KF), 1)],
                                           bias=vb[:, l, bass.ds(t + V_FB, 1)]).then_inc(f_mid, 1)
                            if e == 0:
                                units((3, 4, 5))
                            elif l == 0:
                                ada_out(i + (ADA_TURNS + off // 2))
                            for p in after[2 * e:2 * e + 1]:
                                split(p)
                            emptied(pg)
                            act.activation(fs[:, e, first:T], fy[:, e, first:T], ACT.Tanh, scale=0.5) \
                                .then_inc(f_tanh, 1)
                            for p in after[2 * e + 1:2 * e + 2]:
                                split(p)
                            if e == 0:
                                units((6, 7))
                            emptied(pu)
                            act.activation(flat(ahi[:, bass.ds(i * 2 + e, 1), first:T]), ff[:, e, first:T],
                                           ACT.Copy, scale=0.5).then_inc(f_hi, 1)

                    turns = tiles // 2
                    for p in st.peek(UP_BODY)[AHEAD:]:
                        split(p)
                    with act.Fori(0, turns - 1) as i:
                        hidden(i, st.body(i, UP_BODY), st.body(i + 1, UP_BODY))
                    last_body = st.body(turns - 1, UP_BODY)
                    st.skip(turns, UP_BODY)
                    hidden(turns - 1, last_body, st.peek(down_body(n))[0:AHEAD])
                    if n + 1 < len(FF_PARTS):
                        residual_stage(down_body(n), UP_BODY, None)
                    elif l < L - 1:
                        residual_stage(down_body(n), PROJ, 0)
                    else:
                        residual_stage(down_body(n), None, C)
            root(2 * L, C)
            for q in range(2):
                act.wait_ge(fin_t, 2 * q + 2)
                act.activation(Z[:, D + q * 512:D + (q + 1) * 512], bank[2 + q][:, :], ACT.Copy) \
                    .then_inc(fin_a, 1)

        @block.gpsimd
        def _(pool):
            def ada_split(k, turn, stage):
                pool.wait_ge(ada_hi, turn * KD + (k + 1))
                hi, lo = ada_tiles(k, stage)
                pool.tensor_tensor(lo, adaw[:, k % ADA_SLOTS, :], hi.bitcast(F32), ALU.subtract) \
                    .then_inc(ada_lo, 1)

            def norm(l, w):
                m, first = 2 * l + w, q0(l) if w else 0
                pool.wait_ge(coef, m + 1)
                for k in range(KD):
                    pool.wait_ge(t_ready, 8 * m + k + 1)
                    for s_ in range(first // C, 2):
                        sh = (SH2 if w else SH1) + k
                        last = pool.tensor_scalar(hf[:, k, cols(s_)], M[:, k, cols(s_)],
                                                  am[:, l, w, k, s_:s_ + 1], mod[:, l, sh, s_:s_ + 1],
                                                  ALU.mult, ALU.add)
                    last.then_inc(hf_full, 1)

            pool.wait_ge(start_t, KD + 1)
            for k in range(KD):
                pool.wait_ge(x_ready[k % 2], k // 2 + 1)
                pool.tensor_tensor(M[:, k, :], X[:, k, :], X[:, k, :], ALU.mult).then_inc(sq_ready, 1)
            pool.wait_ge(rms_ready, 1)
            for k in range(KD):
                pool.tensor_tensor(M[:, k, :], X[:, k, :], R[:, :], ALU.mult).then_inc(t_ready, 1)
            for l in range(L):
                norm(l, 0)
                for n in range(len(PROJ)):
                    for turn, k in ada_units(l, n):
                        ada_split(k, turn, "projection")
                norm(l, 1)
                if l == 0:
                    with pool.Fori(0, KF // 2) as i:
                        for k in range(KD):
                            ada_split(k, i + ADA_TURNS, "FFN")

        @block.vector
        def _(dve):
            st = Stream()
            steps = Steps(dve, dve_step)

            def split(p):
                dve.wait_ge(hi_ready[p.slot], p.turn + 1)
                dve.tensor_tensor(wlo[:, p.slot, 0:p.nk, :], raw[:, p.slot, 0:p.nk, :],
                                  whi[:, p.slot, 0:p.nk, :].bitcast(F32), ALU.subtract) \
                    .then_inc(lo_ready[p.slot], 1)

            def full(p):
                dve.wait_ge(panel_done[p.slot], p.turn + 1)
                return bank[p.slot]

            def add_square(m, k, first):
                dve.wait_ge(sq_ready, 8 * m + k + 1)
                add = dve.tensor_tensor(M[:, 0, first:T], M[:, 0, first:T], M[:, k, first:T], ALU.add)
                if k < KD - 1:
                    steps.link(add)
                else:
                    add.then_inc(sum_ready, 1)

            def norm(m, l, w, first):
                dve.wait_ge(rms_ready, m + 1)
                if w is None:
                    for k in range(KD):
                        dve.scalar_tensor_tensor(out=M[:, k, first:T], in0=X[:, k, first:T],
                                                 scalar=vc[:, VC_FIN + k:VC_FIN + k + 1], in1=R[:, first:T],
                                                 op0=ALU.mult, op1=ALU.mult).then_inc(h_ready, 1)
                    return
                for k in range(KD + 1):
                    if k < KD and m > 0:
                        dve.tensor_tensor(M[:, k, first:T], X[:, k, first:T], R[:, first:T], ALU.mult) \
                            .then_inc(t_ready, 1)
                    if k > 0:
                        dve.wait_ge(hf_hi, 8 * m + k)
                        dve.wait_ge(hf_full, 8 * m + k)
                        dve.tensor_tensor(hlo[:, k - 1, first:T], hf[:, k - 1, first:T],
                                          hhi[:, k - 1, first:T].bitcast(F32), ALU.subtract) \
                            .then_inc(h_ready, 1)

            def ada_in(l, chunk, turn):
                dve.wait_ge(ada_cols, turn + 1)
                b = va[:, l, bass.ds(chunk * 4 + V_ADA, 4)] if not isinstance(chunk, int) else \
                    va[:, l, V_ADA + 4 * chunk:V_ADA + 4 * chunk + 4]
                dst = mod[:, l, bass.ds(chunk * 4, 4), :] if not isinstance(chunk, int) else \
                    mod[:, l, 4 * chunk:4 * chunk + 4, :]
                src = bank[6][:, 0:16].rearrange("p (m s) -> p m s", s=4)
                dve.tensor_tensor(dst, src[:, :, 0:2], b.unsqueeze(2).to_broadcast([P, 4, 2]), ALU.add) \
                    .then_inc(ada_sum, 1)
                dve.wait_ge(ada_sum, turn + 1)
                dve.tensor_tensor(dst, dst, src[:, :, 2:4], ALU.add).then_inc(ada_mod, 1)

            def coefficients(l, w, turns):
                dve.wait_ge(ada_mod, turns)
                sc, g = (SC2, V_N2) if w else (SC1, V_N1)
                dve.scalar_tensor_tensor(out=am[:, l, w, :, :], in0=mod[:, l, sc:sc + KD, :], scalar=1.0,
                                         in1=va[:, l, g:g + KD].unsqueeze(2).to_broadcast([P, KD, 2]),
                                         op0=ALU.add, op1=ALU.mult).then_inc(coef, 1)

            def merge(p, e, j, first, begin):
                src = full(p)[:, first:T]
                dst = flat(M[:, bass.ds(j, 1), first:T]) if not isinstance(j, int) else M[:, j, first:T]
                if begin:
                    dve.scalar_tensor_tensor(out=dst, in0=TB[:, e, first:T], scalar=1.0, in1=src,
                                             op0=ALU.add, op1=ALU.mult).then_inc(bank_free[p.slot], 1)
                    return
                dve.scalar_tensor_tensor(out=TA[:, e, first:T], in0=TB[:, e, first:T], scalar=1.0, in1=src,
                                         op0=ALU.add, op1=ALU.mult).then_inc(bank_free[p.slot], 1)
                dve.wait_ge(bank_free[p.slot], p.turn + 1)
                steps.link(dve.tensor_tensor(dst, dst, TA[:, e, first:T], ALU.add))

            def residual(p, l, j, g):
                first_s = 0 if l < L - 1 else 1
                for s_ in range(first_s, 2):
                    dst = flat(X[:, bass.ds(j, 1), cols(s_)])
                    last = dve.scalar_tensor_tensor(
                        out=dst, in0=full(p)[:, cols(s_)], scalar=mod[:, l, bass.ds(j + g, 1), s_:s_ + 1]
                        .rearrange("p a b -> p (a b)"), in1=dst, op0=ALU.mult, op1=ALU.add)
                last.then_inc(bank_free[p.slot], 1)

            dve.memset(ones[:, :], 1.0)
            dve.memset(eps[:, :], EPS)
            dve.memset(W2[:, :, :], 0.0).then_inc(w2_zero, 1)
            for turn in range(ADA_FIRST):
                for k in range(KD):
                    dve.wait_ge(ada_hi, turn * KD + k + 1)
                    n = 2 * turn + k // 4
                    hi, lo = ada_tiles(k, "first")
                    dve.tensor_tensor(lo, ada_half[n % 3][:, k % 4, :], hi.bitcast(F32), ALU.subtract) \
                        .then_inc(ada_lo, 1)
                    if k == 3 and turn > 0:
                        ada_in(0, turn - 1, turn - 1)
                    if k == 3 and turn == 0:
                        dve.wait_ge(c_hi_ready, 1)
                        dve.tensor_tensor(csr[:, :, 2:4], cs[:, :, :], csr[:, :, 0:2].bitcast(F32), ALU.subtract) \
                            .then_inc(c_lo_ready, 1)
                        for l in range(L):
                            dve.tensor_copy(va[:, l, :], bank[5][:, l * 96:l * 96 + VA])
                            dve.tensor_copy(vb[:, l, :], bank[5][:, (2 + l) * 96:(2 + l) * 96 + VB])
                        dve.tensor_copy(vc[:, :], bank[5][:, 4 * 96:4 * 96 + VC])
                        for m in range(1, KD, 2):
                            dve.wait_ge(start_t, m + 2)
                            dve.tensor_copy(X[:, m, :], bank[m % 4][:, :]).then_inc(x_ready[1], 1)
                if turn == 2:
                    for p in st.peek(PROJ)[0:AHEAD]:
                        split(p)
            ada_in(0, ADA_FIRST - 1, ADA_FIRST - 1)
            coefficients(0, 0, ADA_FIRST)

            for l in range(L):
                first = q0(l)
                norm(2 * l, l, 0, 0)
                ps = st.take(PROJ)
                ahead = ps + st.peek(MLA_BODY)[0:AHEAD]
                split(ahead[AHEAD])
                for n, p in enumerate(ps):
                    if n == 0:
                        split(ahead[AHEAD + 1])
                    if n > 1:
                        split(ahead[n + AHEAD])
                    if n == 3:
                        src = full(p)
                        dve.wait_ge(kr_act, at("kr_act", l, 1))
                        dve.tensor_tensor(TA[NOPE:QK, 0, C:T], src[QK:P, C:T], K[QK:P, K_ROPE:K_ROPE + C],
                                          ALU.mult)
                        steps.link(dve.tensor_tensor(kr[NOPE:QK, C:T], src[NOPE:QK, C:T],
                                                     K[NOPE:QK, K_ROPE:K_ROPE + C], ALU.mult))
                        dve.tensor_tensor(kr[NOPE:QK, C:T], kr[NOPE:QK, C:T], TA[NOPE:QK, 0, C:T], ALU.add) \
                            .then_inc(bank_free[p.slot], 1)
                    elif n > 3:
                        j, what = (n - 4) // 3, (n - 4) % 3
                        if what == 0:
                            pass
                        elif what == 1:
                            dve.wait_ge(bank_free[ps[n - 1].slot], ps[n - 1].turn + 1)
                            dve.tensor_tensor(cu[:, j % 2, first:T], TB[:, j % 2, first:T], full(p)[:, first:T],
                                              ALU.mult).then_inc(bank_free[p.slot], 1)
                            dve.wait_ge(conv_mid, at("conv_mid", l, j + 1))
                            u, y = seg(cu[:, j % 2, :], l), seg(cy[:, j % 2, :], l)
                            steps.link(dve.scalar_tensor_tensor(
                                out=y[:, :, 1:C], in0=u[:, :, 0:C - 1], scalar=va[:, l, V_SC + j:V_SC + j + 1],
                                in1=y[:, :, 1:C], op0=ALU.mult, op1=ALU.add))
                            steps.link(dve.scalar_tensor_tensor(
                                out=y[:, :, 0:C - 1], in0=u[:, :, 1:C],
                                scalar=va[:, l, V_SC + 8 + j:V_SC + 9 + j], in1=y[:, :, 0:C - 1],
                                op0=ALU.mult, op1=ALU.add))
                        else:
                            dve.tensor_tensor(cy[:, j % 2, first:T], cy[:, j % 2, first:T], full(p)[:, first:T],
                                              ALU.mult).then_inc(bank_free[p.slot], 1)
                            dve.wait_ge(cat_hi, at("cat_hi", l, j + 1))
                            dve.tensor_tensor(alo[:, j, first:T], cy[:, j % 2, first:T],
                                              ahi[:, j, first:T].bitcast(F32), ALU.subtract).then_inc(cat_lo, 1)
                    if n == 4:
                        dve.wait_ge(c_stat, at("c_stat", l, 2))
                    if n == 6:
                        dve.wait_ge(c_rms, at("c_rms", l, 2))
                        for m in range(3):
                            f, r = (0, R2) if m == 2 else (first, R)
                            g = va[:, l, (V_KN if m == 2 else V_QN + m):(V_KN if m == 2 else V_QN + m) + 1]
                            dve.scalar_tensor_tensor(out=cf[:, m, f:T], in0=cf[:, m, f:T], scalar=g,
                                                     in1=r[:, f:T], op0=ALU.mult, op1=ALU.mult) \
                                .then_inc(c_norm, 1)
                    if 8 <= n <= 10:
                        f = 0 if n == 10 else first
                        dve.wait_ge(c_hi, at("c_hi", l, n - 7))
                        dve.tensor_tensor(clo[:, n - 8, f:T], cf[:, n - 8, f:T],
                                          chi[:, n - 8, f:T].bitcast(F32), ALU.subtract).then_inc(c_lo, 1)
                    if ada_ends(l, n - 1) is not None:
                        ada_in(*chunk_of(ada_ends(l, n - 1)), ada_ends(l, n - 1))
                turn = ada_ends(l, len(ps) - 1)
                ada_in(*chunk_of(turn), turn)
                if l == 0:
                    coefficients(0, 1, ADA_TURNS)
                dve.wait_ge(bank_free[3], ps[3].turn + 1)
                for e in range(2):
                    last = dve.tensor_copy(Kb[NOPE:QK, e, :], kr[NOPE:QK, :])
                last.then_inc(kr_dve, 1)
                nt = 4 if l == 0 else 2
                nb = 3 if l == 0 else 2

                def body(i, ps, after):
                    def heads(e):
                        return i * 2 + (e + 1)

                    def rotate(e):
                        dve.wait_ge(a_q, heads(e) + at("a_q", l, 0))
                        dve.wait_ge(q_act, heads(e) + at("q_act", l, 0))
                        dve.tensor_tensor(TA[NOPE:QK, 0, C:T], bank[4][QK:P, C:T], K[QK:P, K_ROPE:K_ROPE + C],
                                          ALU.mult)
                        steps.link(dve.tensor_tensor(Qb[NOPE:QK, e, C:T], bank[4][NOPE:QK, C:T],
                                                     K[NOPE:QK, K_ROPE:K_ROPE + C], ALU.mult))
                        dve.tensor_tensor(Qb[NOPE:QK, e, C:T], Qb[NOPE:QK, e, C:T], TA[NOPE:QK, 0, C:T],
                                          ALU.add).then_inc(q_dve, 1)

                    def softmax(e):
                        for t in range(nt):
                            if t < 3:
                                tiles = t + 1 if t < 2 else nt
                                dve.wait_ge(scored, i * (2 * nt) + (at("scored", l, 0) + e * nt + tiles))
                            src = bank[4 + t][:, :] if t < 2 else bank[7][:, (t - 2) * C:(t - 1) * C]
                            last = dve.reduce_max(mx[:, 0, t:t + 1], src, AX_X)
                        steps.link(last)
                        dve.tensor_scalar(mx[:, 1, 0:nt], mx[:, 0, 0:nt], -scale, None, ALU.mult) \
                            .then_inc(max_ready, 1)
                        for t in range(nt):
                            dve.wait_ge(exped, i * (2 * nt) + (at("exped", l, 0) + e * nt + t + 1))
                            steps.link(dve.reciprocal(mx[:, 3, t:t + 1], mx[:, 2, t:t + 1]))
                            pr = Pl[:, t, :] if t < 2 else Pc[:, t - 2, :]
                            dve.tensor_scalar(pr, pr, mx[:, 3, t:t + 1], None, ALU.mult).then_inc(p_ready, 1)

                    def values_out(e):
                        dve.wait_ge(p_turned, i * (2 * nb) + (at("p_turned", l, 0) + e * nb + 2))
                        if e == 1:
                            dve.wait_ge(o_done, i * 2 + at("o_done", l, 1))
                        dve.tensor_copy(Tl[:, 2:4, :], bank[5][:, :].rearrange("p (k n) -> p k n", k=2)) \
                            .then_inc(pt_dve, 1)

                    for e in range(2):
                        rotate(e)
                        split((ps + after)[2 * e + 2])
                        softmax(e)
                        values_out(e)
                        dve.wait_ge(bank_free[2 * e + 1], ps[2 * e + 1].turn + 1)
                        merge(ps[2 * e], e, i * 2 + e, first, True)
                        split((ps + after)[2 * e + 3])
                    dve.wait_ge(cat_hi, i + (at("cat_hi", l, 4) + 1))
                    dve.tensor_tensor(flat(alo[:, bass.ds(i + 4, 1), first:T]), OF[:, first:T],
                                      flat(ahi[:, bass.ds(i + 4, 1), first:T]).bitcast(F32),
                                      ALU.subtract).then_inc(cat_lo, 1)

                turns, links = MH // 2, 2 * (2 + nt)
                with dve.Fori(0, turns - 1) as i:
                    steps.enter(i, links)
                    body(i, st.body(i, MLA_BODY), st.body(i + 1, MLA_BODY))
                steps.leave(turns - 1)
                last_body = st.body(turns - 1, MLA_BODY)
                st.skip(turns, MLA_BODY)
                body(turns - 1, last_body, st.peek(GLA))

                ps = st.take(GLA)
                ahead = ps + st.peek(GATE_BODY)[0:AHEAD]
                n = 0
                dve.wait_ge(cat_lo, at("cat_lo", l, 8))
                for half in range(2):
                    r, o = slice(half * CHUNK, (half + 1) * CHUNK), slice((1 - half) * CHUNK, (2 - half) * CHUNK)
                    dve.memset(gA[r, :, o], 0.0)
                dve.memset(gS[0:DK, 0, :], 0.0)
                steps.link(dve.memset(gS[DK:P, NCH // 2 - 1, :], 0.0))
                chunk_pairs = slice(first // P, T // P)
                pairs = (T - first) // P

                def log_decay(h):
                    dve.wait_ge(z_done, at("z_done", l, h + 1))
                    dve.wait_ge(z_ln, at("z_ln", l, h + 1))
                    if h > 0:
                        dve.wait_ge(g_turned, at("g_turned", l, 2 * h))
                    steps.link(dve.tensor_scalar(gx[:, :], bank[4][:, :], va[:, l, V_GK + h:V_GK + h + 1], 0.0,
                                                 ALU.add, ALU.min))
                    steps.link(dve.tensor_tensor(gx[:, :], gx[:, :], gL[:, :], ALU.subtract))
                    dve.tensor_tensor_scan(gst[0:DK, :], K[0:DK, K_SCAN:K_SCAN + T], gx[0:DK, :], 0.0,
                                           ALU.mult, ALU.add)
                    dve.tensor_tensor_scan(gst[DK:P, ::-1], K[DK:P, K_SCAN:K_SCAN + T][:, ::-1],
                                           gx[DK:P, ::-1], 0.0, ALU.mult, ALU.add).then_inc(b_ready, 1)

                def output_norm(h):
                    dve.wait_ge(g_rms, at("g_rms", l, h + 1))
                    steps.link(dve.scalar_tensor_tensor(
                        out=gE[:, first:T], in0=bank[6][:, first:T], scalar=va[:, l, V_GN + h:V_GN + h + 1],
                        in1=R[:, first:T], op0=ALU.mult, op1=ALU.mult))
                    dve.tensor_tensor(gE[:, first:T], gE[:, first:T], gr[:, first:T], ALU.mult) \
                        .then_inc(go_norm, 1)

                def output_lo(h):
                    dve.wait_ge(cat_hi, at("cat_hi", l, 8 + h + 1))
                    dve.scalar_tensor_tensor(out=alo[:, h, first:T], in0=gE[:, first:T], scalar=0.5,
                                             in1=ahi[:, h, first:T].bitcast(F32), op0=ALU.mult,
                                             op1=ALU.subtract).then_inc(cat_lo, 1)

                log_decay(0)
                for h in range(GH):
                    e = h % 2
                    if e == 0:
                        split(ahead[n + AHEAD])
                        if h > 0:
                            output_norm(h - 1)
                        split(ahead[n + 1 + AHEAD])
                        n += 2
                    split(ahead[n + AHEAD])
                    if e == 1:
                        output_norm(h - 1)
                    n += 1
                    split(ahead[n + AHEAD])
                    if h > 0:
                        output_lo(h - 1)
                    dve.wait_ge(r_tanh, at("r_tanh", l, h + 1))
                    dve.scalar_tensor_tensor(out=gr[:, first:T], in0=gr[:, first:T], scalar=1.0,
                                             in1=full(ps[n])[:, first:T], op0=ALU.add, op1=ALU.mult) \
                        .then_inc(bank_free[ps[n].slot], 1)
                    n += 1
                    dve.wait_ge(e_ready, at("e_ready", l, h + 1))
                    if e == 0:
                        for m in (n - 4, n - 3):
                            dve.wait_ge(bank_free[ps[m].slot], ps[m].turn + 1)
                    dve.tensor_tensor(gk[:, e, :], gk[:, e, :], gx[:, :], ALU.mult).then_inc(k_decayed, 1)
                    dve.wait_ge(k_decayed, at("k_decayed", l, h + 1))
                    for way in range(2):
                        r = slice(way * DK, (way + 1) * DK)
                        end = 0 if way else CHUNK - 1
                        ends = gE[r, :].rearrange("p (n i) -> p n i", i=CHUNK)[:, :, end:end + 1]
                        last = dve.tensor_tensor(gst[r, :].rearrange("p (n i) -> p n i", i=CHUNK),
                                                 gk[r, e, :].rearrange("p (n i) -> p n i", i=CHUNK),
                                                 ends.to_broadcast([DK, NCH, CHUNK]), ALU.mult)
                    last.then_inc(kst_ready, 1)
                    dve.tensor_tensor(gq[:, e, first:T], gq[:, e, first:T], gE[:, first:T], ALU.mult) \
                        .then_inc(q_decayed, 1)
                    split(ahead[n + AHEAD])
                    gp = ps[n]
                    n += 1
                    dve.wait_ge(ga_done, at("ga_done", l, h + 1))
                    for way, mask in ((0, K_MF), (1, K_MB)):
                        src = bank[7 if way else 4][:, 0:C].rearrange("p (n i) -> p n i", i=CHUNK)
                        last = dve.tensor_tensor(
                            TA[:, way, 0:C].rearrange("p (n i) -> p n i", i=CHUNK)[:, chunk_pairs, :],
                            src[:, chunk_pairs, :],
                            K[:, mask:mask + CHUNK].unsqueeze(1).to_broadcast([P, pairs, CHUNK]), ALU.mult)
                    steps.link(last)
                    for half in range(2):
                        r = slice(half * CHUNK, (half + 1) * CHUNK)
                        t0, t1 = (TA[r, way, 0:C].rearrange("p (n i) -> p n i", i=CHUNK)[:, chunk_pairs, :]
                                  for way in range(2))
                        last = dve.tensor_tensor(gA[r, chunk_pairs, r], t0, t1, ALU.add)
                    last.then_inc(ga_masked, 1)
                    dve.wait_ge(ga_masked, at("ga_masked", l, h + 1))
                    split(ahead[n + AHEAD])
                    dve.wait_ge(bank_free[gp.slot], gp.turn + 1)
                    merge(ps[n], 0, 2 * h, first, False)
                    n += 1
                    split(ahead[n + AHEAD])
                    gp = ps[n]
                    n += 1
                    dve.wait_ge(gu_done, at("gu_done", l, 2 * h + 2))
                    orders = [scan_order(way) for way in range(2)]
                    for m in range(NCH - 1):
                        for way in range(2):
                            r = slice(way * DK, (way + 1) * DK)
                            a, b = orders[way][m], orders[way][m + 1]
                            col = a * CHUNK + (0 if way else CHUNK - 1)
                            last = dve.scalar_tensor_tensor(
                                out=gS[r, b, :], in0=gS[r, a, :], scalar=gE[r, col:col + 1],
                                in1=bank[4 + a % 2][r, (a // 2) * DV:(a // 2 + 1) * DV],
                                op0=ALU.mult, op1=ALU.add)
                        if m < NCH - 2:
                            steps.link(last)
                    last.then_inc(gs_ready, 1)
                    split(ahead[n + AHEAD])
                    dve.wait_ge(bank_free[gp.slot], gp.turn + 1)
                    merge(ps[n], 1, 2 * h + 1, first, False)
                    n += 1
                    if h + 1 < GH:
                        log_decay(h + 1)
                output_norm(GH - 1)
                output_lo(GH - 1)

                def merge_lo(k):
                    dve.wait_ge(m_hi, 8 * l + k + 1)
                    dve.scalar_tensor_tensor(out=hlo[:, k, first:T], in0=M[:, k, first:T], scalar=0.5,
                                             in1=hhi[:, k, first:T].bitcast(F32), op0=ALU.mult,
                                             op1=ALU.subtract).then_inc(m_lo, 1)

                def gates(i, ps, after):
                    for e in range(2):
                        split((ps + after)[2 * e + 2])
                        split((ps + after)[2 * e + 3])
                        dve.wait_ge(bank_free[2 * e], ps[2 * e].turn + 1)
                        if e == 1 and isinstance(i, int):
                            for k in range(MERGED_EARLY):
                                merge_lo(k)
                        p = ps[2 * e + 1]
                        dst = flat(M[:, bass.ds(i * 2 + e, 1), first:T])
                        dve.scalar_tensor_tensor(out=TA[:, e, first:T], in0=TB[:, e, first:T], scalar=1.0,
                                                 in1=full(p)[:, first:T], op0=ALU.add, op1=ALU.mult) \
                            .then_inc(bank_free[p.slot], 1)
                        dve.wait_ge(bank_free[p.slot], p.turn + 1)
                        dve.tensor_tensor(dst, dst, TA[:, e, first:T], ALU.add).then_inc(m_ready, 1)

                turns = KD // 2
                with dve.Fori(0, turns - 1) as i:
                    gates(i, st.body(i, GATE_BODY), st.body(i + 1, GATE_BODY)[0:AHEAD])
                last_body = st.body(turns - 1, GATE_BODY)
                st.skip(turns, GATE_BODY)
                gates(turns - 1, last_body, st.peek(UP_BODY)[0:AHEAD])
                for k in range(MERGED_EARLY, KD):
                    merge_lo(k)

                def residual_stage(kinds, g, after, m, norm_first):
                    turns = KD // SLOTS
                    with dve.Fori(0, turns - 1) as i:
                        ahead = st.body(i, kinds)[AHEAD:] + st.body(i + 1, kinds)[0:AHEAD]
                        for n, p in enumerate(st.body(i, kinds)):
                            split(ahead[n])
                            residual(p, l, i * SLOTS + n, g)
                    ps = st.body(turns - 1, kinds)
                    st.skip(turns, kinds)
                    ahead = ps[AHEAD:] + (st.peek(after)[0:AHEAD] if after else [])
                    for n, p in enumerate(ps):
                        if n < len(ahead):
                            split(ahead[n])
                        residual(p, l, (turns - 1) * SLOTS + n, g)
                        if m is not None:
                            for k in ((), (1, 2, 3), (4, 5), (6, 7))[n]:
                                add_square(m, k, norm_first)

                residual_stage(UP_BODY, G1, UP_BODY, 2 * l + 1, first)
                norm(2 * l + 1, l, 1, first)
                for n, (off, tiles) in enumerate(parts(l)):
                    def hidden(i, ps, after):
                        for e in range(2):
                            pg, pu = ps[2 * e], ps[2 * e + 1]
                            t = i * 2 + (off + e)
                            g, y = seg(full(pg)[:, :], l), seg(fy[:, e, :], l)
                            dve.wait_ge(f_mid, t + at("f_mid", l, 1))
                            steps.link(dve.scalar_tensor_tensor(
                                out=y[:, :, 1:C], in0=g[:, :, 0:C - 1], scalar=vb[:, l, bass.ds(t + V_FW, 1)],
                                in1=y[:, :, 1:C], op0=ALU.mult, op1=ALU.add))
                            dve.scalar_tensor_tensor(
                                out=y[:, :, 0:C - 1], in0=g[:, :, 1:C],
                                scalar=vb[:, l, bass.ds(t + (V_FW + 2 * KF), 1)], in1=y[:, :, 0:C - 1],
                                op0=ALU.mult, op1=ALU.add).then_inc(bank_free[pg.slot], 1)
                            dve.wait_ge(f_tanh, t + at("f_tanh", l, 1))
                            steps.link(dve.scalar_tensor_tensor(
                                out=ff[:, e, first:T], in0=fs[:, e, first:T], scalar=1.0, in1=fy[:, e, first:T],
                                op0=ALU.add, op1=ALU.mult))
                            dve.tensor_tensor(ff[:, e, first:T], ff[:, e, first:T], full(pu)[:, first:T],
                                              ALU.mult).then_inc(bank_free[pu.slot], 1)
                            for p in after[2 * e:2 * e + 2]:
                                split(p)
                            dve.wait_ge(f_hi, t + at("f_hi", l, 1))
                            dve.scalar_tensor_tensor(
                                out=flat(alo[:, bass.ds(i * 2 + e, 1), first:T]), in0=ff[:, e, first:T], scalar=0.5,
                                in1=flat(ahi[:, bass.ds(i * 2 + e, 1), first:T]).bitcast(F32),
                                op0=ALU.mult, op1=ALU.subtract).then_inc(f_lo, 1)
                        if l == 0:
                            ada_in(1, i + off // 2, i + (ADA_TURNS + off // 2))

                    turns = tiles // 2
                    for p in st.peek(UP_BODY)[AHEAD:]:
                        split(p)
                    with dve.Fori(0, turns - 1) as i:
                        steps.enter(i, 4)
                        hidden(i, st.body(i, UP_BODY), st.body(i + 1, UP_BODY))
                    steps.leave(turns - 1)
                    last_body = st.body(turns - 1, UP_BODY)
                    st.skip(turns, UP_BODY)
                    hidden(turns - 1, last_body, st.peek(down_body(n))[0:AHEAD])
                    if n + 1 < len(FF_PARTS):
                        residual_stage(down_body(n), G2, UP_BODY, None, None)
                    elif l < L - 1:
                        residual_stage(down_body(n), G2, PROJ, 2 * l + 2, 0)
                    else:
                        residual_stage(down_body(n), G2, None, 2 * l + 2, C)
                if l == 0:
                    coefficients(1, 0, 2 * ADA_TURNS - 1)
                    coefficients(1, 1, 2 * ADA_TURNS - 1)
            norm(2 * L, None, None, C)
            for q in range(2):
                dve.wait_ge(fin_t, 2 * q + 1)
                dve.tensor_copy(Z[:, q * 512:(q + 1) * 512], bank[q][:, :]).then_inc(fin_v, 1)


def constants():
    k = np.zeros((P, K_ALL), np.float32)
    k[:, K_ID:K_ID + P] = np.eye(P)
    j, i = np.arange(P)[:, None] % CHUNK, np.arange(CHUNK)[None, :]
    k[:, K_MF:K_MF + CHUNK] = j <= i
    k[:, K_MB:K_MB + CHUNK] = j >= i
    t = np.arange(T)
    k[0:DK, K_SCAN:K_SCAN + T] = t % CHUNK != 0
    k[DK:P, K_SCAN:K_SCAN + T] = t % CHUNK != CHUNK - 1
    freqs = ROPE // 4
    inv = (10000.0 ** (-np.arange(freqs, dtype=np.float32) / freqs)).astype(np.float32)
    pos = [np.arange(C) // GRID_W, np.arange(C) % GRID_W]
    for axis in range(2):
        ang = (pos[axis][None, :].astype(np.float32) * inv[:, None]).astype(np.float32)
        for half in range(2):
            r = axis * 2 * freqs + half * freqs
            k[NOPE + r:NOPE + r + freqs, K_ROPE:K_ROPE + C] = np.cos(ang)
            k[QK + r:QK + r + freqs, K_ROPE:K_ROPE + C] = np.sin(ang) * (1 if half else -1)
    return k


_INS = ["x", "c", "ctx", "c_ctx", "w_ada", "b_ada", "norm1_g", "w_in", "w_gk2", "b_gk2", "gla_norm_g",
        "mla_q_norm_g", "w_uq", "mla_kv_norm_g", "w_ukv", "sc_w", "w_br_a", "w_br_b", "w_br_c", "w_o",
        "norm2_g", "w_ffn_gate", "w_ffn_up", "ffn_conv_w", "ffn_conv_b", "w_ffn_down", "final_norm_g"]


def kernel(**inputs):
    import concourse.bacc as bacc
    from concourse.bass_utils import run_bass_kernel_spmd

    nc = bacc.Bacc("TRN2", target_bir_lowering=False, num_devices=1)
    arrays, args = {}, []
    for name in _INS + ["consts"]:
        a = constants() if name == "consts" else np.ascontiguousarray(inputs[name])
        arrays[f"in_{name}"] = a
        args.append(nc.dram_tensor(f"in_{name}", a.shape, F32, kind="ExternalInput").ap())
    args.append(nc.dram_tensor("out_0", (1, C, D), F32, kind="ExternalOutput").ap())
    build(nc, *args)
    r = run_bass_kernel_spmd(nc, [arrays], core_ids=[0])
    return r.results[0]["out_0"]
```
